# Optimizing a Trainium2 kernel written in Bass

```python
import math
import jax
import jax.numpy as jnp
from jax import lax
import numpy as np

D_MODEL = 2048
BATCH = 1
SEQ = 256
DEPTH = 1
DEC_BATCH = 8
DEC_SEQ = 4
PAST_LEN = 256
PAGE_SIZE = 128

HEAD_DIM = 128
N_HEADS = D_MODEL // HEAD_DIM
H_A = N_HEADS // 2
H_M = N_HEADS - H_A
W_A = H_A * HEAD_DIM
W_M = H_M * HEAD_DIM
MIX_WIDTH = W_A + W_M
QK_M = 2 * W_M
N_IN = 3 * W_A + H_A + QK_M + 2 * W_M + 2 * H_M
D_FF = 128 * ((8 * D_MODEL // 3 + 127) // 128)
CONV_W = 4
MLSTM_CHUNK = 64
Q_BLOCK = 128
EPS = 1e-6
ATTN_SCALE = HEAD_DIM ** -0.5

kernel_name = 'fox_mlstm_parallel_heads_macaron_step'

def _rmsnorm(x, g):
    xf = x.astype(jnp.float32)
    y = xf * lax.rsqrt(jnp.mean(xf * xf, axis=-1, keepdims=True) + EPS)
    return (y * g.astype(jnp.float32)).astype(x.dtype)

def _swiglu(x, w_gate, w_up, w_down):
    return (jax.nn.silu(x @ w_gate) * (x @ w_up)) @ w_down

def _fox_attend(q, cq, qpos, k, v, ck, kpos):
    s = jnp.einsum('bqhd,bkhd->bhqk', q, k).astype(jnp.float32) * ATTN_SCALE
    bias = jnp.swapaxes(cq, 1, 2)[:, :, :, None] - jnp.swapaxes(ck, 1, 2)[:, :, None, :]
    causal = (qpos[:, None] >= kpos[None, :])[None, None]
    p = jax.nn.softmax(jnp.where(causal, s + bias, -jnp.inf), axis=-1)
    return jnp.einsum('bhqk,bkhd->bqhd', p.astype(v.dtype), v)

def _fox_prompt(q, k, v, logf):
    B, T, H, D = q.shape
    c = jnp.cumsum(logf.astype(jnp.float32), axis=1)
    pos = jnp.arange(T)
    nb = T // Q_BLOCK
    qb = jnp.swapaxes(q.reshape(B, nb, Q_BLOCK, H, D), 0, 1)
    cb = jnp.swapaxes(c.reshape(B, nb, Q_BLOCK, H), 0, 1)
    pb = pos.reshape(nb, Q_BLOCK)
    out = lax.map(lambda blk: _fox_attend(blk[0], blk[1], blk[2], k, v, c, pos), (qb, cb, pb))
    return jnp.swapaxes(out, 0, 1).reshape(B, T, H, D)

def _fox_sample(q, k, v, logf, k_past, v_past, lf_past):
    T = q.shape[1]
    P = k_past.shape[1]
    c_all = jnp.cumsum(jnp.concatenate([lf_past.astype(jnp.float32), logf.astype(jnp.float32)], axis=1), axis=1)
    c_past = jnp.swapaxes(c_all[:, :P], 1, 2)
    c_new = jnp.swapaxes(c_all[:, P:], 1, 2)
    s_past = jnp.einsum('bqhd,bkhd->bhqk', q, k_past.astype(q.dtype)).astype(jnp.float32) * ATTN_SCALE
    s_past = s_past + c_new[:, :, :, None] - c_past[:, :, None, :]
    s_new = jnp.einsum('bqhd,bkhd->bhqk', q, k).astype(jnp.float32) * ATTN_SCALE
    s_new = s_new + c_new[:, :, :, None] - c_new[:, :, None, :]
    tri = jnp.tril(jnp.ones((T, T), dtype=bool))
    s_new = jnp.where(tri[None, None], s_new, -jnp.inf)
    p = jax.nn.softmax(jnp.concatenate([s_past, s_new], axis=-1), axis=-1).astype(v.dtype)
    return (jnp.einsum('bhqk,bkhd->bqhd', p[..., :P], v_past.astype(v.dtype))
            + jnp.einsum('bhqk,bkhd->bqhd', p[..., P:], v))

def _causal_conv(u, prev, w, b):
    T = u.shape[1]
    ext = jnp.concatenate([prev.astype(u.dtype), u], axis=1)
    out = b
    for j in range(CONV_W):
        out = out + w[j] * ext[:, j:j + T]
    return out, ext[:, T:]

def _mlstm(q, k, v, i_pre, log_f, C0, n0, m0):
    B, T, H, D = q.shape
    L = math.gcd(T, MLSTM_CHUNK)
    nc = T // L

    def vec_chunks(a):
        return a.astype(jnp.float32).reshape(B, nc, L, H, D).transpose(1, 0, 3, 2, 4)

    def gate_chunks(a):
        return a.astype(jnp.float32).reshape(B, nc, L, H).transpose(1, 0, 3, 2)

    tril = jnp.tril(jnp.ones((L, L), dtype=bool))

    def step(carry, xs):
        C, n, m = carry
        qc, kc, vc, ic, fc = xs
        b = jnp.cumsum(fc, axis=-1)
        a = b + m[..., None]
        dmat = jnp.where(tril, b[..., :, None] - b[..., None, :] + ic[..., None, :], -jnp.inf)
        mt = jnp.maximum(a, jnp.max(dmat, axis=-1))
        w_intra = jnp.exp(dmat - mt[..., None]) * jnp.einsum('bhtd,bhsd->bhts', qc, kc)
        w_inter = jnp.exp(a - mt)
        num = (w_inter[..., None] * jnp.einsum('bhtd,bhde->bhte', qc, C)
               + jnp.einsum('bhts,bhse->bhte', w_intra, vc))
        den = w_inter * jnp.einsum('bhtd,bhd->bht', qc, n) + jnp.sum(w_intra, axis=-1)
        h = num / jnp.maximum(jnp.abs(den), jnp.exp(-mt))[..., None]
        m_new = mt[..., -1]
        w_state = jnp.exp(b[..., -1:] - b + ic - m_new[..., None])
        decay = jnp.exp(b[..., -1] + m - m_new)
        C_new = decay[..., None, None] * C + jnp.einsum('bhs,bhsd,bhse->bhde', w_state, kc, vc)
        n_new = decay[..., None] * n + jnp.einsum('bhs,bhsd->bhd', w_state, kc)
        return (C_new, n_new, m_new), h

    carry0 = (C0.astype(jnp.float32), n0.astype(jnp.float32), m0.astype(jnp.float32))
    xs = (vec_chunks(q), vec_chunks(k), vec_chunks(v), gate_chunks(i_pre), gate_chunks(log_f))
    (C, n, m), h = lax.scan(step, carry0, xs)
    h = h.transpose(1, 0, 3, 2, 4).reshape(B, T, H, D)
    return h, C, n, m

def _layer(x, conv_prev, C0, n0, m0, attend, lw):
    B, T, _ = x.shape
    x = x + 0.5 * _swiglu(_rmsnorm(x, lw['g_ffn1']), lw['w1_gate'], lw['w1_up'], lw['w1_down'])
    h = _rmsnorm(x, lw['g_mix'])
    proj = h @ lw['w_in']
    cuts = []
    acc = 0
    for wdt in (W_A, W_A, W_A, H_A, QK_M, W_M, W_M, H_M):
        acc += wdt
        cuts.append(acc)
    q_a, k_a, v_a, f_a, qk_m, v_m, o_m, i_m, f_m = jnp.split(proj, cuts, axis=-1)
    q_a = _rmsnorm(q_a.reshape(B, T, H_A, HEAD_DIM), lw['g_q'])
    k_a = _rmsnorm(k_a.reshape(B, T, H_A, HEAD_DIM), lw['g_k'])
    v_a = v_a.reshape(B, T, H_A, HEAD_DIM)
    logf_a = jax.nn.log_sigmoid((f_a + lw['b_fox_f']).astype(jnp.float32))
    y_a = _rmsnorm(attend(q_a, k_a, v_a, logf_a), lw['g_out_a'])
    qk_c, conv_new = _causal_conv(qk_m, conv_prev, lw['conv_w'], lw['conv_b'])
    qk_c = jax.nn.silu(qk_c)
    q_m = qk_c[..., :W_M].reshape(B, T, H_M, HEAD_DIM)
    k_m = qk_c[..., W_M:].reshape(B, T, H_M, HEAD_DIM) * (HEAD_DIM ** -0.5)
    v_m = v_m.reshape(B, T, H_M, HEAD_DIM)
    i_pre = (i_m + lw['b_m_i']).astype(jnp.float32)
    log_f_m = jax.nn.log_sigmoid((f_m + lw['b_m_f']).astype(jnp.float32))
    h_m, C, n, m = _mlstm(q_m, k_m, v_m, i_pre, log_f_m, C0, n0, m0)
    y_m = jax.nn.sigmoid(o_m).reshape(B, T, H_M, HEAD_DIM) * _rmsnorm(h_m, lw['g_out_m']).astype(x.dtype)
    y = jnp.concatenate([y_a.reshape(B, T, W_A), y_m.reshape(B, T, W_M)], axis=-1) @ lw['w_out']
    x = x + y
    x = x + 0.5 * _swiglu(_rmsnorm(x, lw['g_ffn2']), lw['w2_gate'], lw['w2_up'], lw['w2_down'])
    return x, k_a, v_a, logf_a, conv_new, C, n, m

def setup_inputs(seed: int = 0) -> dict:
    key = jax.random.key(seed)
    ks = jax.random.split(key, 32)
    n_pages = PAST_LEN // PAGE_SIZE
    n_used = DEC_BATCH * n_pages
    n_pool = n_used + n_used // 4

    def nrm(k, shape, scale):
        return scale * jax.random.normal(k, shape, jnp.float32)

    x_prompt = nrm(ks[0], (BATCH, SEQ, D_MODEL), 1.0)
    x_sample = nrm(ks[1], (DEC_BATCH, DEC_SEQ, D_MODEL), 1.0)
    cache_k = nrm(ks[2], (DEPTH, n_pool, PAGE_SIZE, H_A, HEAD_DIM), 1.0)
    cache_v = nrm(ks[3], (DEPTH, n_pool, PAGE_SIZE, H_A, HEAD_DIM), 1.0)
    cache_logf = jax.nn.log_sigmoid(4.0 + nrm(ks[4], (DEPTH, n_pool, PAGE_SIZE, H_A), 1.0))
    state_conv = nrm(ks[5], (DEPTH, DEC_BATCH, CONV_W - 1, QK_M), 1.0)
    state_C = nrm(ks[6], (DEPTH, DEC_BATCH, H_M, HEAD_DIM, HEAD_DIM), 0.1)
    state_n = nrm(ks[7], (DEPTH, DEC_BATCH, H_M, HEAD_DIM), 0.1)
    state_m = 1.0 + nrm(ks[8], (DEPTH, DEC_BATCH, H_M), 1.0)
    page_table = jax.random.permutation(ks[9], n_pool)[:n_used].reshape(DEC_BATCH, n_pages).astype(jnp.int32)
    return {
        'x_prompt': x_prompt,
        'x_sample': x_sample,
        'cache_k': cache_k,
        'cache_v': cache_v,
        'cache_logf': cache_logf,
        'state_conv': state_conv,
        'state_C': state_C,
        'state_n': state_n,
        'state_m': state_m,
        'page_table': page_table,
        'g_ffn1': 1.0 + nrm(ks[10], (DEPTH, D_MODEL), 0.02),
        'w1_gate': nrm(ks[11], (DEPTH, D_MODEL, D_FF), D_MODEL ** -0.5),
        'w1_up': nrm(ks[12], (DEPTH, D_MODEL, D_FF), D_MODEL ** -0.5),
        'w1_down': nrm(ks[13], (DEPTH, D_FF, D_MODEL), D_FF ** -0.5),
        'g_mix': 1.0 + nrm(ks[14], (DEPTH, D_MODEL), 0.02),
        'w_in': nrm(ks[15], (DEPTH, D_MODEL, N_IN), D_MODEL ** -0.5),
        'b_fox_f': 4.0 + nrm(ks[16], (DEPTH, H_A), 0.5),
        'b_m_i': nrm(ks[17], (DEPTH, H_M), 0.1),
        'b_m_f': 4.0 + nrm(ks[18], (DEPTH, H_M), 0.5),
        'conv_w': nrm(ks[19], (DEPTH, CONV_W, QK_M), CONV_W ** -0.5),
        'conv_b': nrm(ks[20], (DEPTH, QK_M), 0.02),
        'g_q': 1.0 + nrm(ks[21], (DEPTH, HEAD_DIM), 0.02),
        'g_k': 1.0 + nrm(ks[22], (DEPTH, HEAD_DIM), 0.02),
        'g_out_a': 1.0 + nrm(ks[23], (DEPTH, H_A, HEAD_DIM), 0.02),
        'g_out_m': 1.0 + nrm(ks[24], (DEPTH, H_M, HEAD_DIM), 0.02),
        'w_out': nrm(ks[25], (DEPTH, MIX_WIDTH, D_MODEL), MIX_WIDTH ** -0.5),
        'g_ffn2': 1.0 + nrm(ks[26], (DEPTH, D_MODEL), 0.02),
        'w2_gate': nrm(ks[27], (DEPTH, D_MODEL, D_FF), D_MODEL ** -0.5),
        'w2_up': nrm(ks[28], (DEPTH, D_MODEL, D_FF), D_MODEL ** -0.5),
        'w2_down': nrm(ks[29], (DEPTH, D_FF, D_MODEL), D_FF ** -0.5),
    }

def reference(x_prompt, x_sample, cache_k, cache_v, cache_logf, state_conv, state_C, state_n, state_m,
              page_table, g_ffn1, w1_gate, w1_up, w1_down, g_mix, w_in, b_fox_f, b_m_i, b_m_f,
              conv_w, conv_b, g_q, g_k, g_out_a, g_out_m, w_out, g_ffn2, w2_gate, w2_up, w2_down):
    n_seq, n_pages = page_table.shape
    past_len = n_pages * cache_k.shape[2]
    bp = x_prompt.shape[0]
    yp = x_prompt
    ys = x_sample
    kp_l, vp_l, lfp_l, convp_l, Cp_l, np_l, mp_l = [], [], [], [], [], [], []
    ks_l, vs_l, lfs_l, convs_l, Cs_l, ns_l, ms_l = [], [], [], [], [], [], []
    for l in range(DEPTH):
        lw = {
            'g_ffn1': g_ffn1[l], 'w1_gate': w1_gate[l], 'w1_up': w1_up[l], 'w1_down': w1_down[l],
            'g_mix': g_mix[l], 'w_in': w_in[l], 'b_fox_f': b_fox_f[l], 'b_m_i': b_m_i[l], 'b_m_f': b_m_f[l],
            'conv_w': conv_w[l], 'conv_b': conv_b[l], 'g_q': g_q[l], 'g_k': g_k[l],
            'g_out_a': g_out_a[l], 'g_out_m': g_out_m[l], 'w_out': w_out[l],
            'g_ffn2': g_ffn2[l], 'w2_gate': w2_gate[l], 'w2_up': w2_up[l], 'w2_down': w2_down[l],
        }
        conv0 = jnp.zeros((bp, CONV_W - 1, QK_M), x_prompt.dtype)
        C0 = jnp.zeros((bp, H_M, HEAD_DIM, HEAD_DIM), jnp.float32)
        n0 = jnp.zeros((bp, H_M, HEAD_DIM), jnp.float32)
        m0 = jnp.zeros((bp, H_M), jnp.float32)
        yp, kp, vp, lfp, convp, Cp, np_, mp = _layer(yp, conv0, C0, n0, m0, _fox_prompt, lw)
        k_past = cache_k[l][page_table].reshape(n_seq, past_len, H_A, HEAD_DIM)
        v_past = cache_v[l][page_table].reshape(n_seq, past_len, H_A, HEAD_DIM)
        lf_past = cache_logf[l][page_table].reshape(n_seq, past_len, H_A)
        attend_s = lambda q, k, v, lf, kp_=k_past, vp_=v_past, lp_=lf_past: _fox_sample(q, k, v, lf, kp_, vp_, lp_)
        ys, k_s, v_s, lfs, convs, Cs, ns, ms = _layer(ys, state_conv[l], state_C[l], state_n[l], state_m[l], attend_s, lw)
        kp_l.append(kp); vp_l.append(vp); lfp_l.append(lfp); convp_l.append(convp)
        Cp_l.append(Cp); np_l.append(np_); mp_l.append(mp)
        ks_l.append(k_s); vs_l.append(v_s); lfs_l.append(lfs); convs_l.append(convs)
        Cs_l.append(Cs); ns_l.append(ns); ms_l.append(ms)
    return (yp, ys,
            jnp.stack(kp_l), jnp.stack(vp_l), jnp.stack(lfp_l), jnp.stack(convp_l),
            jnp.stack(Cp_l), jnp.stack(np_l), jnp.stack(mp_l),
            jnp.stack(ks_l), jnp.stack(vs_l), jnp.stack(lfs_l), jnp.stack(convs_l),
            jnp.stack(Cs_l), jnp.stack(ns_l), jnp.stack(ms_l))


_drawn_inputs = setup_inputs


def setup_inputs(seed=0):
    import zlib

    import numpy as np

    out = dict(_drawn_inputs(seed))
    spreads = {}
    factors = {'g_ffn1': 3.633,
     'g_q': 5.622,
     'g_k': 3.307,
     'g_out_a': 5.198,
     'g_out_m': 8.0,
     'g_ffn2': 8.0}
    for name, (base, spread) in spreads.items():
        noise = np.random.default_rng([zlib.crc32(name.encode()), seed]).standard_normal(out[name].shape)
        drawn = base * np.exp(spread * noise) if base else spread * noise
        out[name] = jnp.asarray(drawn.astype(out[name].dtype))
    for name, factor in factors.items():
        out[name] = (out[name] * factor).astype(out[name].dtype)
    return out
```

```python
from contextlib import ExitStack

import concourse.bass as bass
from concourse import mybir
from concourse.alu_op_type import AluOpType as ALU

F32 = mybir.dt.float32
F32R = mybir.dt.float32r
I32 = mybir.dt.int32
ACT = mybir.ActivationFunctionType
AX = mybir.AxisListType

P = 128
D = 2048
KD = D // P
TP = 256
NB = 8
TS = 4
SM = NB * TS
T = TP + SM
H = 8
HD = 128
PAGE = 128
NPG = 2
F = 5504
CHUNK = 24
CW = 4
QK = 2 * H * HD
EPS = 1e-6
SCALE = float(HD) ** -0.5
BIG = 1.0e30
N_IN = 7192
COL_F_A = 3 * H * HD
COL_M = COL_F_A + H
COL_I_M = N_IN - 2 * H
UW = 1024
SLOTS = 4
NBANK = 8
EXT = CW - 1 + TP
EXTS = CW - 1 + TS
EXTW = EXT + NB * EXTS
TT = [(0, P), (1, P), (2, SM)]


class Group:

    def __init__(self, turn, index, nk, real, tiles):
        self.turn, self.index, self.real, self.tiles = turn, index, real, tiles
        self.turns = nk // SLOTS


def plan():
    turn, index, out = 0, 0, {}
    plain = [j * P for j in range(NBANK)]
    gate_up = [c for j in range(4) for c in (j * P, 512 + j * P)]
    swiglu = [("gu{}a", 6, KD, KD, gate_up), ("down{}a", 2, 24, 24, plain), ("gu{}b", 4, KD, KD, gate_up),
              ("gu{}c", 1, KD, KD, gate_up[:6]), ("down{}b", 2, 20, 19, plain)]
    mixer = [("in_a", 3, KD, KD, plain), ("in_m", 4, KD, KD, plain), ("out", 2, KD, KD, plain)]
    for n, part in ((0, swiglu), (0, mixer), (1, swiglu)):
        for name, count, nk, real, tiles in part:
            out[name.format(n)] = Group(turn, index, nk, real, tiles)
            turn += count * nk // SLOTS
            index += count
    return out, turn, index


def build(nc, A, O):
    groups, n_turns, n_groups = plan()
    ctx = ExitStack()
    sems = {}

    def sem(name):
        if name not in sems:
            sems[name] = ctx.enter_context(nc.semaphore(name))
        return sems[name]

    def area(side):
        scope = ExitStack()
        return scope, lambda name, shape, dt=F32: scope.enter_context(nc.sbuf_tensor(name, shape, dt, side=side))

    ctx.enter_context(nc.allow_non_contiguous_dma(reason="a few small transposed state vectors"))
    keep, t_ = area("left")
    ctx.enter_context(keep)
    ident, ones = t_("ident", [P, P]), t_("ones", [P, P])
    upper = t_("upper", [P, P])
    neg_upper, neg_ones = t_("neg_upper", [P, P]), t_("neg_ones", [P, P])
    lower = t_("lower", [P, P])
    block4 = t_("block4", [SM, SM])
    upper4, neg_upper4, lower4 = t_("upper4", [SM, SM]), t_("neg_upper4", [SM, SM]), t_("lower4", [SM, SM])
    mask_q = t_("mask_q", [P, 3 * P])
    mask_t = t_("mask_t", [P, 3 * P])
    mask4_q = t_("mask4_q", [SM, SM])
    mask4_t = t_("mask4_t", [SM, SM])
    spread = t_("spread", [SM, NB * SM])
    sel = t_("sel", [H, H, P])
    one_hot = t_("one_hot", [P, H, H])
    root = t_("root", [H, 2, T])
    vecs = t_("vecs", [P, 146])
    gq_scaled = t_("gq_scaled", [P, 1])
    w_gates = t_("w_gates", [P, KD, 3 * H])
    b_gates = t_("b_gates", [P, 3 * H])
    G = t_("G", [P, 3, 3 * H])
    LF = t_("LF", [P, 3, 2 * H])
    pages_sb = t_("pages_sb", [1, NB * NPG], I32)
    X = t_("X", [P, KD, T])
    w_raw = t_("w_raw", [P, SLOTS, UW])
    w_hi, w_lo = t_("w_hi", [P, SLOTS, UW], F32R), t_("w_lo", [P, SLOTS, UW], F32R)
    sq, xt, rs = t_("sq", [P, 2, T]), t_("xt", [P, 2, T]), t_("rs", [P, 2, T])
    ps = ctx.enter_context(nc.psum_tensor("ps", [P, NBANK, 512], F32))
    V_FFN, V_MIX, V_CB, V_CW, V_GQ, V_GK, V_GA, V_GM = (0, 32), 16, 48, 64, 128, 129, 130, 138

    scope, l_ = area("left")
    with scope:
        x_rows, vec_rows = l_("x_rows", [P, 3, D]), l_("vec_rows", [P, 2, P])

    def operand_memory(name):
        scope, r_ = area("right")
        with scope:
            return r_(name + "_hi", [P, KD, T], F32R), r_(name + "_lo", [P, KD, T], F32R)

    x_op = [operand_memory("x0"), operand_memory("x1")]
    xm_hi, xm_lo = operand_memory("xm")
    y_hi, y_lo = operand_memory("y")
    right_side, r_ = area("right")
    kmn = r_("kmn", [P, 3, H * HD])
    C = r_("C", [P, 2, NB, HD])
    v_seq = r_("v_seq", [SM, NB, HD])
    Ws, qw, qn = r_("Ws", [SM, H, SM]), r_("qw", [P, H, SM]), r_("qn", [P, H, SM])
    Wt = r_("Wt", [P, 2, 384])
    em_all, dn = r_("em_all", [P, 2, TP]), r_("dn", [P, 2, TP])
    Cp = r_("Cp", [P, 2, HD])
    r_("operand_rest", [P, 2 * KD * T - 8960])

    def swiglu_memory(n):
        scope, l_ = area("left")
        with scope:
            return dict(x=x_op[n], hid=(l_(f"hid_hi{n}", [P, CHUNK, T], F32R), l_(f"hid_lo{n}", [P, CHUNK, T], F32R)),
                        silu=l_(f"silu{n}", [P, 2, T]), prod=l_(f"prod{n}", [P, 2, T]))

    mem = [swiglu_memory(0), swiglu_memory(1)]
    scope_mixer, m_ = area("left")
    with scope_mixer:
        ya = m_("ya", [P, H, T])
        scope, l_ = area("left")
        with scope:
            qa, ka = l_("qa", [P, H, T]), l_("ka", [P, H, T])
            kn, vn = l_("kn", [P, 3, H * HD]), l_("vn", [P, 3, H * HD])
            mx, nmx, den, rden = (l_(n, [P, 2, 2]) for n in ("mx", "nmx", "den", "rden"))
            neg_c = l_("neg_c", [H, TP])
            page = l_("page", [P, 3, H * HD])
            kpT = l_("kpT", [P, 2, H * HD])
            lf_past = l_("lf_past", [P, NB * NPG, H])
            nl_past = l_("nl_past", [P, NPG, NB * SM])
            nl_new = l_("nl_new", [SM, NB * SM])
            scope_p, p_ = area("left")
            with scope_p:
                lt = p_("lt", [P, 3, 3, 2 * H])
            scope_p, p_ = area("left")
            with scope_p:
                Sm, PT = p_("Sm", [P, 2, 384]), p_("PT", [P, 2, 384])
            STs, STn = l_("STs", [P, 512]), l_("STn", [SM, 256])
            PTs, PTn = STs, STn
            Ps = l_("Ps", [P, 2, T])
        scope, l_ = area("left")
        with scope:
            ext = l_("ext", [P, 2 * H, EXTW])
            vm, om = l_("vm", [P, H, T]), l_("om", [P, H, T])
            vmn = l_("vmn", [P, 3, H * HD])
            conv_rows = l_("conv_rows", [27, QK])
            conv_last = l_("conv_last", [P, 2 * H, 27])
            r_row, b_row, R_row, nR_row, m_row, em_row, ws_row = (
                l_(n, [H, T]) for n in ("r_row", "b_row", "R_row", "nR_row", "m_row", "em_row", "ws_row"))
            m0 = l_("m0", [H, NB])
            s_rows = l_("s_rows", [H, 3, SM])
            scope_c, c_ = area("left")
            with scope_c:
                conv_acc = c_("conv_acc", [P, 2, EXTW])
            s_all = l_("s_all", [P, H, 3, SM])
            nat = l_("nat", [P, 6, H])
            n_rows = l_("n_rows", [NB * H, 2, HD])
            n0T, n_new = l_("n0T", [P, NB * H]), l_("n_new", [P, 1 + NB, H])
    right_side.close()
    scope, l_ = area("left")
    with scope:
        y_rows = l_("y_rows", [P, 3, D])

    block = ctx.enter_context(nc.Block())
    w_loaded = [sem(f"w_loaded{s}") for s in range(SLOTS)]
    w_hi_ready, w_lo_ready, w_used = sem("w_hi_ready"), sem("w_lo_ready"), sem("w_used")
    bank_done, banks_free = sem("bank_done"), sem("banks_free")
    small_loaded, pool_const, const_ready = sem("small_loaded"), sem("pool_const"), sem("const_ready")
    out_stored = sem("out_stored")

    G_A, G_M, G_O = groups["in_a"].index, groups["in_m"].index, groups["out"].index

    def wait_bank(eng, g, turn, gi, b):
        n = len(g.tiles)
        if b < n - 1:
            eng.wait_ge(bank_done, gi * (NBANK - 1) + (b + 1 if b < n - 2 else NBANK - 1))
        else:
            eng.wait_ge(w_used, (turn + g.turns) * 2 + 2)

    def x_final(eng, n, t):
        if n == 0:
            eng.wait_ge(sem("xT_copied"), t + 1)
        else:
            g = groups["down0b" if n == 1 else "out"]
            eng.wait_ge(banks_free, NBANK + g.index * NBANK + t + 1)
    def tiles_of(w):
        return w[0].rearrange("(k p) n -> k p n", p=P)

    wg, wu, wd = ([tiles_of(A[f"w{n}_{kind}"]) for n in (1, 2)] for kind in ("gate", "up", "down"))
    wi, wo = tiles_of(A["w_in"]), tiles_of(A["w_out"])

    @block.sync
    def _(sp):
        def load_turn(turn, slots, parts, fresh=False):
            for s in slots:
                if not fresh:
                    sp.wait_ge(w_hi_ready, turn * SLOTS + (s + 1 - SLOTS))
                    sp.wait_ge(w_lo_ready, turn * SLOTS + (s + 1 - SLOTS))
                for c, src in parts(s):
                    sp.dma_start(w_raw[:, s, c:c + src.shape[-1]], src).then_inc(w_loaded[s], 32 // len(parts(s)))

        def load_group(g, turn, unit_src, fresh=False):
            whole = g.real // SLOTS
            if fresh:
                load_turn(turn, range(SLOTS), lambda s: unit_src(s), fresh=True)
            with sp.Fori(1 if fresh else 0, whole) as kt:
                load_turn(turn + kt, range(SLOTS), lambda s: unit_src(kt * SLOTS + s))
            if whole < g.turns:
                load_turn(turn + whole, range(SLOTS), lambda s: unit_src(min(whole * SLOTS + s, g.real - 1)))

        def load_swiglu(n):
            def gate_up(col, w):
                return lambda k: [(0, wg[n][k, :, bass.ds(col, w)]), (512, wu[n][k, :, bass.ds(col, w)])]

            def down(k0, col):
                return lambda k: [(0, wd[n][k + k0, :, bass.ds(col, UW)])]

            g = groups[f"gu{n}a"]
            if n == 0:
                load_group(g, g.turn, gate_up(0, 512), fresh=True)
            with sp.Fori(1 if n == 0 else 0, 6) as i:
                load_group(g, i * g.turns + g.turn, gate_up(i * 512, 512))
            g = groups[f"down{n}a"]
            with sp.Fori(0, 2) as i:
                load_group(g, i * g.turns + g.turn, down(0, i * UW))
            g = groups[f"gu{n}b"]
            with sp.Fori(0, 4) as i:
                load_group(g, i * g.turns + g.turn, gate_up(i * 512 + CHUNK * P, 512))
            g = groups[f"gu{n}c"]
            load_group(g, g.turn, gate_up(40 * P, 384))
            g = groups[f"down{n}b"]
            with sp.Fori(0, 2) as i:
                load_group(g, i * g.turns + g.turn, down(CHUNK, i * UW))

        load_swiglu(0)
        for name, count, w, col in (("in_a", 3, wi, 0), ("in_m", 4, wi, COL_M), ("out", 2, wo, 0)):
            g = groups[name]
            with sp.Fori(0, count) as i:
                load_group(g, i * g.turns + g.turn, lambda k: [(0, w[k, :, bass.ds(i * UW + col, UW)])])
        load_swiglu(1)
        load_turn(n_turns, range(2), lambda s: [(0, wd[1][s, :, 0:UW])])
        for s in range(2):
            sp.wait_ge(w_loaded[s], 32 * (n_turns + 1))

    @block.gpsimd
    def _(pool):
        def small(dst, src):
            pool.dma_start(dst, src).then_inc(small_loaded, 16)

        rows = lambda name: A[name].rearrange("l (r p) -> (l r) p", p=P)
        for name, r0, n in (("g_ffn1", 0, 16), ("g_mix", 16, 16), ("g_ffn2", 32, 16), ("conv_b", 48, 16)):
            small(vec_rows[r0:r0 + n, 0, :], rows(name))
        small(vec_rows[64:128, 0, :], A["conv_w"].rearrange("l c (r p) -> (l c r) p", p=P))
        small(vec_rows[0:1, 1, :], A["g_q"])
        small(vec_rows[1:2, 1, :], A["g_k"])
        small(vec_rows[2:10, 1, :], A["g_out_a"][0])
        small(vec_rows[10:18, 1, :], A["g_out_m"][0])
        wi_p = A["w_in"][0].rearrange("(k p) n -> p k n", p=P)
        small(w_gates[:, :, 0:H], wi_p[:, :, COL_F_A:COL_F_A + H])
        small(w_gates[:, :, H:2 * H], wi_p[:, :, COL_I_M + H:N_IN])
        small(w_gates[:, :, 2 * H:3 * H], wi_p[:, :, COL_I_M:COL_I_M + H])
        for c, name in enumerate(("b_fox_f", "b_m_f", "b_m_i")):
            small(b_gates[:, c * H:(c + 1) * H], A[name].to_broadcast([P, H]))
        small(pages_sb[:, :], A["page_table"].rearrange("b n -> (b n)").unsqueeze(0))

        nc.gpsimd.memset(ones[:, :], 1.0).then_inc(pool_const, 1)
        nc.gpsimd.memset(ident[:, :], 0.0).then_inc(pool_const, 1)
        pool.wait_ge(pool_const, 2)
        nc.gpsimd.affine_select(out=upper[:, :], in_=ones[:, :], compare_op=ALU.is_ge, fill=0.0, base=0,
                                pattern=[[1, P]], channel_multiplier=-1)
        nc.gpsimd.affine_select(out=lower[:, :], in_=ones[:, :], compare_op=ALU.is_ge, fill=0.0, base=0,
                                pattern=[[-1, P]], channel_multiplier=1)
        nc.gpsimd.affine_select(out=block4[:, :].rearrange("p (b t) -> p b t", t=TS),
                                in_=ones[0:SM, 0:SM].rearrange("p (b t) -> p b t", t=TS), compare_op=ALU.is_ge,
                                fill=0.0, base=0, pattern=[[-TS, NB], [0, TS]], channel_multiplier=1)
        nc.gpsimd.affine_select(out=ident[:, :], in_=ident[:, :], compare_op=ALU.not_equal, fill=1.0, base=0,
                                pattern=[[-1, P]], channel_multiplier=1).then_inc(pool_const, 1)
        pool.wait_ge(pool_const, 3)
        nc.gpsimd.affine_select(out=block4[:, :].rearrange("p (b t) -> p b t", t=TS),
                                in_=block4[:, :].rearrange("p (b t) -> p b t", t=TS), compare_op=ALU.is_ge,
                                fill=0.0, base=TS - 1, pattern=[[TS, NB], [0, TS]],
                                channel_multiplier=-1).then_inc(pool_const, 1)

        def store(dst, src):
            pool.dma_start(dst, src).then_inc(out_stored, 16)

        pool.wait_ge(small_loaded, 16 * 16)
        pool.wait_ge(banks_free, NBANK + G_A * NBANK)
        pids = []
        for p in range(NB * NPG):
            pids.append(pool.value_load(pages_sb[0:1, p:p + 1], min_val=0, max_val=A["cache_k"].shape[1] - 1))
            pool.dma_start(lf_past[:, p, :], A["cache_logf"][0][bass.ds(pids[p], 1), :, :]
                           .rearrange("a s h -> (a s) h")).then_inc(sem("lf_past_loaded"), 16)

        def load_page(n):
            cache = A["cache_k"] if n < NB * NPG else A["cache_v"]
            if n >= NB * NPG + 3:
                pool.wait_ge(sem("sample_pv"), n - 2 - NB * NPG)
            elif n >= 3:
                pool.wait_ge(sem("kpT_done"), 2 * (n - 2))
            pid = pool.value_load(pages_sb[0:1, n % 16:n % 16 + 1], min_val=0, max_val=cache.shape[1] - 1)
            pool.dma_start(page[:, n % 3, :], cache[0][bass.ds(pid, 1), :, :, :]
                           .rearrange("a s h d -> (a s) (h d)")).then_inc(sem(f"page_loaded{n % 3}"), 16)

        for n in range(3):
            load_page(n)
        pool.wait_ge(sem("lf_ready"), 1)
        store(O["logf_prompt"][0, 0].rearrange("(t p) h -> p t h", p=P), LF[:, 0:2, 0:H])
        store(O["logf_sample"][0].rearrange("b t h -> (b t) h"), LF[0:SM, 2, 0:H])
        pool.wait_ge(sem("vn_ready"), 6)
        store(O["v_prompt"][0, 0].rearrange("(t p) h d -> p t (h d)", p=P), vn[:, 0:2, :])
        store(O["v_sample"][0].rearrange("b t h d -> (b t) (h d)"), vn[0:SM, 2, :])
        pool.wait_ge(sem("kn_ready"), 6)
        store(O["k_prompt"][0, 0].rearrange("(t p) h d -> p t (h d)", p=P), kn[:, 0:2, :])
        store(O["k_sample"][0].rearrange("b t h d -> (b t) (h d)"), kn[0:SM, 2, :])
        for n in range(3, 2 * NB * NPG):
            load_page(n)

        pool.wait_ge(sem("ya_ready"), H + 1)
        pool.wait_ge(out_stored, 6 * 16)
        pool.dma_start(conv_rows[0:24, :], A["state_conv"][0].rearrange("b r c -> (b r) c")).then_inc(sem("state_loaded"), 16)
        pool.dma_start(n_rows[:, 0, :], A["state_n"][0].rearrange("b h d -> (b h) d")).then_inc(sem("state_loaded"), 16)
        pool.dma_start(m0[:, :], A["state_m"][0].rearrange("b h -> h b")).then_inc(sem("state_loaded"), 16)
        pool.wait_ge(sem("conv_rows_ready"), 4)
        store(O["conv_prompt"][0, 0], conv_rows[0:3, :])
        store(O["conv_sample"][0].rearrange("b r c -> (b r) c"), conv_rows[3:27, :])
        store(O["m_prompt"][0].rearrange("b h -> h b"), m_row[:, TP - 1:TP])
        store(O["m_sample"][0].rearrange("b h -> h b"),
              m_row[:, TP:T].rearrange("h (b t) -> h b t", t=TS)[:, :, TS - 1])
        pool.wait_ge(banks_free, NBANK + G_O * NBANK)

        def load_state(h):
            if h >= 2:
                pool.wait_ge(sem(f"C_stored{h % 2}"), 16 * (h // 2))
            pool.dma_start(C[:, h % 2, :, :], A["state_C"][0, :, h, :, :].rearrange("b d e -> d b e")).then_inc(
                sem(f"C_loaded{h % 2}"), 16)

        load_state(0)
        pool.wait_ge(sem("kmn_ready"), 6)
        pool.wait_ge(sem("nat_ready"), 1)
        for t, n in TT:
            k3 = kmn[0:n, t, :].rearrange("p (h d) -> p h d", h=H)
            nc.gpsimd.tensor_tensor(k3, k3, nat[0:n, 3 + t, :].unsqueeze(2).to_broadcast([n, H, HD]),
                                    ALU.mult).then_inc(sem("kw_ready"), 1)
        for h in range(H):
            if h + 1 < H:
                load_state(h + 1)
            if h >= 1:
                pool.wait_ge(sem("dC_done"), 2 * h)
            nc.gpsimd.tensor_tensor(v_seq[:, :, :],
                                    vmn[0:SM, 2, h * HD:(h + 1) * HD].unsqueeze(1).to_broadcast([SM, NB, HD]),
                                    block4[:, 0:SM:TS].unsqueeze(2).to_broadcast([SM, NB, HD]),
                                    ALU.mult).then_inc(sem("v_seq_ready"), 1)
            pool.wait_ge(sem(f"C_loaded{h % 2}"), 16 * (h // 2 + 1))
            pool.wait_ge(sem("qC_done"), h + 1)
            w_last = s_all[:, h, 0, :].rearrange("p (b t) -> p b t", t=TS)[:, :, TS - 1]
            nc.gpsimd.tensor_tensor(C[:, h % 2, :, :], C[:, h % 2, :, :],
                                    w_last.unsqueeze(2).to_broadcast([P, NB, HD]),
                                    ALU.mult).then_inc(sem("C_decayed"), 1)
            pool.wait_ge(sem("C_new"), 2 * (h + 1))
            pool.dma_start(O["C_sample"][0, :, h, :, :].rearrange("b d e -> d b e"), C[:, h % 2, :, :]).then_inc(
                sem(f"C_stored{h % 2}"), 16)
            pool.wait_ge(sem("Cp_ready"), h + 1)
            pool.dma_start(O["C_prompt"][0, 0, h, :, :], Cp[:, h % 2, :]).then_inc(sem(f"Cp_stored{h % 2}"), 16)
        pool.wait_ge(sem("n_rows_ready"), 2)
        store(O["n_sample"][0].rearrange("b h d -> (b h) d"), n_rows[:, 0, :])
        store(O["n_prompt"][0, 0], n_rows[0:H, 1, :])
        for t, n in TT:
            pool.wait_ge(sem("y_rows_ready"), 2 * (t + 1))
            pool.wait_ge(sem("y_rows_ready_v"), 2 * (t + 1))
            if t < 2:
                store(O["y_prompt"][0, t * P:(t + 1) * P, :], y_rows[:, t, :])
            else:
                store(O["y_sample"].rearrange("b t d -> (b t) d"), y_rows[0:SM, 2, :])
        pool.wait_ge(out_stored, 16 * (6 + 4 + 2 + 3))
        for kind in ("C_stored", "Cp_stored"):
            for b in range(2):
                pool.wait_ge(sem(f"{kind}{b}"), 16 * (H // 2))

    N_FFN = (0, 3)
    SUM_X = {0: 0, 1: 16, 3: 64}
    SUM_QK, SUM_Y = 32, 48
    SILU0 = {"gu0a": 0, "gu0b": 24, "gu0c": 40, "gu1a": 43, "gu1b": 67, "gu1c": 83}
    NGRP = {"a": 6, "b": 4, "c": 1}

    @block.scalar
    def _(act):
        def split_hi(turn, slot):
            act.wait_ge(w_loaded[slot], turn * 32 + 32)
            if not (isinstance(turn, int) and turn == 0):
                act.wait_ge(w_used, turn * 2 + (slot // 2 + 1))
            nc.scalar.copy(w_hi[:, slot, :], w_raw[:, slot, :]).then_inc(w_hi_ready, 1)

        def split_turns(turn, n):
            with act.Fori(0, n) as kt:
                for s in range(SLOTS):
                    split_hi(turn + kt + (s // 2), (s + 2) % SLOTS)

        def square(i, src):
            if i >= 2:
                act.wait_ge(sem("sum_done"), i - 1)
            nc.scalar.activation(sq[:, i % 2, :], src, ACT.Square).then_inc(sem("sq_ready"), 1)

        def operand_hi(m, t, dst):
            act.wait_ge(sem("xn_tmp"), 16 * m + t + 1)
            nc.scalar.copy(dst[:, t, :], xt[:, t % 2, :]).then_inc(sem("xn_hi"), 1)

        def sqrt(i, out, src):
            act.wait_ge(sem("mean_ready"), i + 1)
            nc.scalar.activation(out, src, ACT.Sqrt).then_inc(sem("sqrt_ready"), 1)

        def norm(n, dst_hi):
            for t in range(KD):
                x_final(act, min(n, 2), t)
                square(SUM_X[n] + t, X[:, t, :])
            sqrt((0, 1, None, 4)[n], rs[:, 1, :], rs[:, 0, :])
            for t in range(KD):
                operand_hi(n, t, dst_hi)

        def swiglu(n):
            for part in "abc":
                g = groups[f"gu{n}{part}"]

                def group(i):
                    split_turns(i * g.turns + g.turn, g.turns)
                    for j in range(len(g.tiles) // 2):
                        wait_bank(act, g, i * g.turns + g.turn, i + g.index, 2 * j)
                        act.wait_ge(banks_free, NBANK + (i + g.index) * NBANK + max(0, 2 * j - 2))
                        nc.scalar.activation(mem[n]["silu"][:, j % 2, :], ps[:, 2 * j, 0:T],
                                             ACT.Silu).then_inc(sem("silu_ready"), 1)

                if part != "c":
                    with act.Fori(0, NGRP[part]) as i:
                        group(i)
                    if part == "a":
                        d = groups[f"down{n}a"]
                        split_turns(d.turn, 2 * d.turns)
                else:
                    group(0)
            d = groups[f"down{n}b"]
            split_turns(d.turn, 2 * d.turns)

        for t in range(2):
            act.dma_start(x_rows[:, t, :], A["x_prompt"][0, t * P:(t + 1) * P, :]).then_inc(sem("x_loaded"), 16)
        act.dma_start(x_rows[0:SM, 2, :], A["x_sample"].rearrange("b t d -> (b t) d")).then_inc(sem("x_loaded"), 16)
        split_hi(0, 0)
        split_hi(0, 1)
        norm(0, mem[0]["x"][0])
        swiglu(0)
        norm(1, xm_hi)
        g = groups["in_a"]
        split_turns(g.turn, 3 * g.turns)

        def natural(dst, made, name):
            for i in range(6):
                t, half, n = i // 2, i % 2, TT[i // 2][1]
                act.wait_ge(sem(made), i + 1)
                nc.scalar.copy(dst[0:n, t, half * 512:half * 512 + 512], ps[0:n, 2 + i, :]).then_inc(sem(name), 1)

        act.wait_ge(sem("abs_ready"), 1)
        nc.scalar.activation(lt[:, 1, :, :], lt[:, 0, :, :], ACT.Exp, scale=-1.0).then_inc(sem("abs_exp"), 1)
        natural(vn, "vT_done", "vn_ready")
        for j in range(2 * H):
            act.wait_ge(banks_free, NBANK + G_M * NBANK)
            square(SUM_QK + j, (qa if j < H else ka)[:, j % H, :])
        sqrt(2, root[:, :, :], rs[0:H, :, :])
        natural(kn, "kT_done", "kn_ready")

        def p_exp(h):
            act.wait_ge(sem("s_masked"), h + 1)
            b = h % 2
            for q, c0, c1 in ((0, 0, P), (1, P, 384)):
                nc.scalar.activation(Sm[:, b, c0:c1], Sm[:, b, c0:c1], ACT.Exp, bias=nmx[:, b, q:q + 1],
                                     accum_out=den[:, b, q:q + 1]).then_inc(sem("p_exp"), 1)

        def pt_copy(h):
            act.wait_ge(sem("pt_done"), h + 1)
            if h >= 2:
                act.wait_ge(sem("o_done"), h - 1)
            nc.scalar.copy(PT[:, h % 2, :], ps[:, 2 + h % 2, 0:384]).then_inc(sem("pt_ready"), 1)

        for h in range(H + 1):
            if h < H:
                p_exp(h)
            if h >= 1:
                pt_copy(h - 1)
        for p in range(NB * NPG):
            act.wait_ge(sem("kpT_done"), 2 * p + 1)
            if p >= 2:
                act.wait_ge(sem("sT_done"), p - 1)
            nc.scalar.copy(kpT[:, p % 2, 0:512], ps[:, 2 * (p % 2), :]).then_inc(sem("kpT_lo"), 1)
        for g2 in range(2):
            act.wait_ge(sem("sample_max"), g2 + 1)
            nc.scalar.activation(Ps[:, g2, :], ps[:, 4 + g2, 0:T], ACT.Exp, bias=nmx[:, 0, g2:g2 + 1],
                                 accum_out=den[:, 0, g2:g2 + 1]).then_inc(sem("sample_exp"), 1)
        act.wait_ge(sem("sample_pT"), 1)
        nc.scalar.copy(PTs[:, :], ps[:, 0, :]).then_inc(sem("sample_pT_ready"), 1)
        nc.scalar.copy(PTn[:, :], ps[0:SM, 1, 0:256]).then_inc(sem("sample_pT_ready"), 1)

        act.wait_ge(sem("rows_sum"), 4)
        nc.scalar.activation(em_row[:, :], m_row[:, :], ACT.Exp, scale=-1.0).then_inc(sem("rows_exp"), 1)
        nc.scalar.activation(ws_row[:, 0:TP], r_row[:, 0:TP], ACT.Exp, bias=nR_row[:, TP - 1:TP]).then_inc(sem("rows_exp"), 1)
        nc.scalar.activation(ws_row[:, TP:T], ws_row[:, TP:T], ACT.Exp).then_inc(sem("rows_exp"), 1)
        nc.scalar.activation(s_rows[:, 0, :], s_rows[:, 0, :], ACT.Exp).then_inc(sem("rows_exp"), 1)

        def conv_silu(j):
            act.wait_ge(sem("conv_done"), j + 1)
            act.wait_ge(sem("conv_last"), 2 * (1 + j // H))
            cb = vecs[:, V_CB + j:V_CB + j + 1]
            nc.scalar.activation(ext[:, j, 0:TP], conv_acc[:, j % 2, 0:TP], ACT.Silu, bias=cb).then_inc(sem("conv_used"), 1)
            nc.scalar.activation(ext[:, j, TP:T].rearrange("p (b t) -> p b t", t=TS),
                                 conv_acc[:, j % 2, EXT:EXTW].rearrange("p (b t) -> p b t", t=EXTS)[:, :, 0:TS],
                                 ACT.Silu, bias=cb).then_inc(sem("conv_used"), 1)

        g = groups["in_m"]
        split_turns(g.turn, 2 * g.turns)
        for t in range(2 * g.turns):
            split_turns(g.turn + 2 * g.turns + t, 1)
            conv_silu(2 * t)
            conv_silu(2 * t + 1)
        act.wait_ge(banks_free, NBANK + G_O * NBANK)
        nc.scalar.activation(om[:, :, :], om[:, :, :], ACT.Sigmoid).then_inc(sem("o_sigmoid"), 1)
        for i in range(6):
            t, half, n = i // 2, i % 2, TT[i // 2][1]
            act.wait_ge(sem("vmT_done"), i + 1)
            nc.scalar.copy(vmn[0:n, t, half * 512:half * 512 + 512], ps[0:n, i, :]).then_inc(sem("vmn_ready"), 1)
        for i in range(6):
            t, half, n = i // 2, i % 2, TT[i // 2][1]
            act.wait_ge(sem("kmT_done"), i + 1)
            nc.scalar.copy(kmn[0:n, t, half * 512:half * 512 + 512], ps[0:n, i, :]).then_inc(sem("kmn_ready"), 1)
        for b in range(2):
            act.wait_ge(sem("s_all_done"), b + 1)
            nc.scalar.copy(s_all[:, 4 * b:4 * b + 4, :, :], ps[:, 6 + b, 0:384].rearrange(
                "p (h r s) -> p h r s", h=4, r=3)).then_inc(sem("s_all_ready"), 1)
        act.wait_ge(sem("ws_logits"), 1)
        nc.scalar.activation(Ws[:, :, :], Ws[:, :, :], ACT.Exp).then_inc(sem("ws_exp"), 1)
        for h in range(H):
            act.wait_ge(sem("e_logits"), h + 1)
            for t, c0, c1 in ((0, 0, TP), (1, TP, 384)):
                nc.scalar.activation(Wt[:, h % 2, c0:c1], Wt[:, h % 2, c0:c1], ACT.Exp,
                                     bias=nat[:, t, h:h + 1]).then_inc(sem("e_exp"), 1)
            act.wait_ge(sem("em_done"), h + 1)
            if h >= 2:
                act.wait_ge(sem("h_ready"), h - 1)
            nc.scalar.copy(em_all[:, h % 2, :], ps[:, 6, 0:TP]).then_inc(sem("em_ready"), 1)
            act.wait_ge(sem("Cp_done"), h + 1)
            if h >= 2:
                act.wait_ge(sem(f"Cp_stored{h % 2}"), 16 * (h // 2))
            nc.scalar.copy(Cp[:, h % 2, :], ps[:, 7, 0:HD]).then_inc(sem("Cp_ready"), 1)
        for j in range(KD):
            act.wait_ge(sem("h_ready"), H + 1)
            square(SUM_Y + j, (ya if j < H else vm)[:, j % H, :])
        sqrt(3, root[:, :, :], rs[0:H, :, :])
        for t in range(KD):
            operand_hi(2, t, y_hi)
        g = groups["out"]
        split_turns(g.turn, 2 * g.turns)
        norm(3, mem[1]["x"][0])
        swiglu(1)
        for i in range(12):
            if i % 2 == 0:
                act.wait_ge(sem("y_rows_done"), i + 1)
                t, n = TT[i // 4]
                nc.scalar.copy(y_rows[0:n, t, (i % 4) * 512:(i % 4 + 1) * 512], ps[0:n, i % 4, :]).then_inc(sem("y_rows_ready"), 1)

    @block.vector
    def _(dve):
        chain = [0]

        def link(ins):
            chain[0] += 1
            ins.then_inc(sem("dve_chain"), 1)
            dve.wait_ge(sem("dve_chain"), chain[0])

        def split_lo(turn, slot):
            dve.wait_ge(w_hi_ready, turn * SLOTS + (slot + 1))
            nc.vector.tensor_tensor(w_lo[:, slot, :], w_raw[:, slot, :], w_hi[:, slot, :].bitcast(F32),
                                    ALU.subtract).then_inc(w_lo_ready, 1)

        def split_turns(turn, n):
            with dve.Fori(0, n) as kt:
                for s in range(SLOTS):
                    split_lo(turn + kt + (s // 2), (s + 2) % SLOTS)

        def rsqrt_mean(i, y, v, tmp, src, width):
            nc.vector.tensor_scalar(v, src, 1.0 / width, EPS, ALU.mult, ALU.add).then_inc(sem("mean_ready"), 1)
            dve.wait_ge(sem("sqrt_ready"), i + 1)
            link(nc.vector.reciprocal(y, y))
            link(nc.vector.tensor_tensor(tmp, y, y, ALU.mult))
            link(nc.vector.scalar_tensor_tensor(tmp, v, -0.5, tmp, ALU.mult, ALU.mult))
            return nc.vector.scalar_tensor_tensor(y, tmp, 1.5, y, ALU.add, ALU.mult)

        def head_norm(j, x, gain):
            dve.wait_ge(sem("spread_done"), j + 1)
            bank = j % 2 + (0 if j < 2 * H else 1)
            return lambda out: nc.vector.scalar_tensor_tensor(out, x, gain, ps[:, bank, 0:T], ALU.mult, ALU.mult)

        def operand_lo(m, t, dst_hi, dst_lo):
            dve.wait_ge(sem("xn_hi"), 16 * m + t + 1)
            nc.vector.tensor_tensor(dst_lo[:, t, :], xt[:, t % 2, :], dst_hi[:, t, :].bitcast(F32),
                                    ALU.subtract).then_inc(sem("xn_ready"), 1)

        def norm(n, gain, dst_hi, dst_lo):
            dve.wait_ge(sem("sum_done"), SUM_X[n] + KD)
            link(rsqrt_mean((0, 1, None, 4)[n], rs[:, 1, :], rs[:, 0, :], xt[:, 0, :], ps[:, 0, 0:T], D))
            for t in range(KD + 1):
                if t < KD:
                    if t >= 2:
                        dve.wait_ge(sem("xn_ready"), 16 * n + t - 1)
                    nc.vector.scalar_tensor_tensor(xt[:, t % 2, :], X[:, t, :], vecs[:, gain + t:gain + t + 1],
                                                   rs[:, 1, :], ALU.mult, ALU.mult).then_inc(sem("xn_tmp"), 1)
                if t >= 1:
                    operand_lo(n, t - 1, dst_hi, dst_lo)

        def swiglu(n):
            hid_hi, hid_lo = mem[n]["hid"]
            silu, prod = mem[n]["silu"], mem[n]["prod"]

            def down(name, scale=0.5):
                g = groups[name]
                for half in range(2):
                    split_turns(half * g.turns + g.turn, g.turns)
                    residual(g, half, scale)

            for part in "abc":
                g = groups[f"gu{n}{part}"]
                s0, f0 = SILU0[f"gu{n}{part}"], 16 if part == "c" else 0

                def group(i):
                    split_turns(i * g.turns + g.turn, g.turns)
                    nj = len(g.tiles) // 2
                    for j in range(nj):
                        dve.wait_ge(sem("silu_ready"), i * 4 + (s0 + j + 1))
                        wait_bank(dve, g, i * g.turns + g.turn, i + g.index, 2 * j + 1)
                        freed = 2 if j < nj - 1 else NBANK - 2 * (nj - 1)
                        nc.vector.tensor_tensor(prod[:, j % 2, :], silu[:, j % 2, :], ps[:, 2 * j + 1, 0:T],
                                                ALU.mult).then_inc(banks_free, freed)
                        dve.wait_ge(banks_free, NBANK + (i + g.index) * NBANK + (2 * j + freed))
                        nc.vector.tensor_scalar(hid_hi[:, i * 4 + (f0 + j), :], prod[:, j % 2, :], 1.0, None,
                                                ALU.mult).then_inc(sem("hid_hi_ready"), 1)
                        dve.wait_ge(sem("hid_hi_ready"), i * 4 + (s0 + j + 1))
                        nc.vector.tensor_tensor(hid_lo[:, i * 4 + (f0 + j), :], prod[:, j % 2, :],
                                                hid_hi[:, i * 4 + (f0 + j), :].bitcast(F32),
                                                ALU.subtract).then_inc(sem("hid_ready"), 1)
                        dve.wait_ge(sem("hid_ready"), i * 4 + (s0 + j + 1))

                if part != "c":
                    with dve.Fori(0, NGRP[part]) as i:
                        group(i)
                    if part == "a":
                        down(f"down{n}a")
                else:
                    group(0)
            down(f"down{n}b")

        def residual(g, half, scale):
            for b in range(NBANK):
                wait_bank(dve, g, half * g.turns + g.turn, half + g.index, b)
                x = X[:, half * NBANK + b, :]
                nc.vector.scalar_tensor_tensor(x, ps[:, b, 0:T], scale, x, ALU.mult, ALU.add).then_inc(banks_free, 1)

        nc.vector.memset(neg_ones[:, :], -1.0)
        nc.vector.memset(mask_q[:, P:2 * P], 0.0)
        nc.vector.memset(mask_t[:, P:2 * P], 0.0)
        nc.vector.memset(G[:, :, :], 0.0)
        dve.wait_ge(pool_const, 4)
        nc.vector.tensor_scalar(neg_upper[:, :], upper[:, :], -1.0, None, ALU.mult)
        for c in (0, 2 * P):
            nc.vector.tensor_scalar(mask_q[:, c:c + P], lower[:, :], -1.0, BIG, ALU.add, ALU.mult)
            nc.vector.tensor_scalar(mask_t[:, c:c + P], upper[:, :], -1.0, BIG, ALU.add, ALU.mult)
        nc.vector.tensor_tensor(upper4[:, :], upper[0:SM, 0:SM], block4[:, :], ALU.mult)
        link(nc.vector.tensor_tensor(lower4[:, :], lower[0:SM, 0:SM], block4[:, :], ALU.mult))
        nc.vector.tensor_scalar(neg_upper4[:, :], upper4[:, :], -1.0, None, ALU.mult)
        nc.vector.tensor_scalar(mask4_q[:, :], lower4[:, :], -1.0, BIG, ALU.add, ALU.mult)
        nc.vector.tensor_scalar(mask4_t[:, :], upper4[:, :], -1.0, BIG, ALU.add, ALU.mult)
        nc.vector.tensor_copy(spread[:, :].rearrange("p (b h q) -> p b h q", b=NB, h=H),
                              ident[0:SM, 0:SM].rearrange("p (b q) -> p b q", q=TS).unsqueeze(2)
                              .to_broadcast([SM, NB, H, TS]))
        nc.vector.memset(one_hot[:, :, :], 0.0).then_inc(sem("one_hot_zero"), 1)
        dve.wait_ge(sem("one_hot_zero"), 1)
        for h in range(H):
            nc.vector.memset(one_hot[:, h, h:h + 1], 1.0)
        nc.vector.tensor_copy(sel[:, :, :], ident[0:H, 0:H].unsqueeze(2).to_broadcast([H, H, P])).then_inc(const_ready, 1)
        split_lo(0, 0)
        split_lo(0, 1)
        for t in range(KD):
            dve.wait_ge(sem("xT_done"), t + 1)
            nc.vector.tensor_copy(X[:, t, :], ps[:, t % 4, 0:T]).then_inc(sem("xT_copied"), 1)
        dve.wait_ge(sem("vecT_done"), 1)
        nc.vector.tensor_copy(vecs[:, :], ps[:, 7, 0:146]).then_inc(banks_free, NBANK)
        dve.wait_ge(banks_free, NBANK)
        nc.vector.tensor_scalar(gq_scaled[:, :], vecs[:, V_GQ:V_GQ + 1], SCALE, None, ALU.mult).then_inc(sem("vecs_ready"), 1)

        norm(0, V_FFN[0], *mem[0]["x"])
        swiglu(0)
        norm(1, V_MIX, xm_hi, xm_lo)

        g = groups["in_a"]
        for i, dst in enumerate((qa, ka, ya)):
            split_turns(g.turn + i * g.turns, g.turns)
            for b in range(NBANK):
                wait_bank(dve, g, g.turn + i * g.turns, g.index + i, b)
                nc.vector.tensor_copy(dst[:, b, :], ps[:, b, 0:T]).then_inc(banks_free, 1)
        dve.wait_ge(sem("gates_done"), 1)
        nc.vector.tensor_tensor(G[:, 0:2, :], ps[:, 0, 0:48].rearrange("p (t g) -> p t g", t=2),
                                b_gates[:, :].unsqueeze(1).to_broadcast([P, 2, 3 * H]), ALU.add)
        link(nc.vector.tensor_tensor(G[0:SM, 2, :], ps[0:SM, 0, 48:72], b_gates[0:SM, :], ALU.add))
        gf = G[:, :, 0:2 * H]
        nc.vector.scalar_tensor_tensor(lt[:, 0, :, :], gf, -1.0, gf, ALU.mult, ALU.max).then_inc(sem("abs_ready"), 1)
        dve.wait_ge(sem("abs_exp"), 1)
        e, a, z = lt[:, 1, :, :], lt[:, 0, :, :], lt[:, 2, :, :]
        link(nc.vector.tensor_scalar(a, e, 2.0, None, ALU.add))
        link(nc.vector.reciprocal(a, a))
        link(nc.vector.tensor_tensor(e, e, a, ALU.mult))
        link(nc.vector.tensor_tensor(z, e, e, ALU.mult))
        link(nc.vector.tensor_scalar(a, z, 1.0 / 17, None, ALU.mult))
        for c in range(15, 1, -2):
            link(nc.vector.scalar_tensor_tensor(a, a, 1.0 / c, z, ALU.add, ALU.mult))
        link(nc.vector.scalar_tensor_tensor(e, a, 1.0, e, ALU.add, ALU.mult))
        link(nc.vector.tensor_scalar(z, gf, 0.0, None, ALU.min))
        nc.vector.scalar_tensor_tensor(LF[:, :, :], e, -2.0, z, ALU.mult, ALU.add).then_inc(sem("lf_ready"), 1)
        dve.wait_ge(sem("sum_done"), SUM_QK + 2 * H)
        rsqrt_mean(2, root[:, :, :], rs[0:H, :, :], xt[0:H, :, :], ps[0:H, 0:2, 0:T], HD).then_inc(sem("root_ready"), 1)
        for j in range(2 * H):
            x = (qa if j < H else ka)[:, j % H, :]
            gain = gq_scaled[:, :] if j < H else vecs[:, V_GK:V_GK + 1]
            head_norm(j, x, gain)(x).then_inc(sem("qk_normed"), 1)
        dve.wait_ge(sem("c_done"), 1)
        nc.vector.tensor_copy(neg_c[:, :], ps[0:H, 1, 0:TP]).then_inc(sem("neg_c_ready"), 1)

        def s_mask(h):
            dve.wait_ge(sem("s_done"), h + 1)
            b = h % 2
            if h >= 2:
                dve.wait_ge(sem("pt_done"), h - 1)
            for q, c0, c1 in ((0, 0, P), (1, P, 384)):
                link(nc.vector.tensor_tensor(Sm[:, b, c0:c1], ps[:, b, c0:c1], mask_q[:, c0:c1], ALU.add))
                link(nc.vector.tensor_reduce(mx[:, b, q:q + 1], Sm[:, b, c0:c1], AX.X, ALU.max))
            nc.vector.tensor_scalar(nmx[:, b, :], mx[:, b, :], -1.0, None, ALU.mult).then_inc(sem("s_masked"), 1)

        def p_norm(h):
            b = h % 2
            dve.wait_ge(sem("p_exp"), 2 * (h + 1))
            link(nc.vector.reciprocal(rden[:, b, :], den[:, b, :]))
            nc.vector.tensor_scalar(Sm[:, b, 0:P], Sm[:, b, 0:P], rden[:, b, 0:1], None, ALU.mult)
            nc.vector.tensor_scalar(Sm[:, b, P:384], Sm[:, b, P:384], rden[:, b, 1:2], None,
                                    ALU.mult).then_inc(sem("p_ready"), 1)

        def o_copy(h):
            dve.wait_ge(sem("o_done"), h + 1)
            nc.vector.tensor_copy(ya[:, h, 0:TP], ps[:, 4 + h % 2, 0:TP]).then_inc(sem("ya_ready"), 1)

        for h in range(H + 2):
            if h < H:
                s_mask(h)
            if 1 <= h <= H:
                p_norm(h - 1)
            if h >= 2:
                o_copy(h - 2)

        for p in range(NB * NPG):
            dve.wait_ge(sem("kpT_done"), 2 * p + 2)
            if p >= 2:
                dve.wait_ge(sem("sT_done"), p - 1)
            nc.vector.tensor_copy(kpT[:, p % 2, 512:1024], ps[:, 2 * (p % 2) + 1, :]).then_inc(sem("kpT_hi"), 1)
        dve.wait_ge(sem("lf_past_loaded"), 16 * NB * NPG)
        for c in range(NPG):
            for b in range(NB):
                nc.vector.tensor_scalar(nl_past[:, c, b * SM:(b + 1) * SM].rearrange("p (h q) -> p h q", h=H),
                                        lf_past[:, b * NPG + c, :].unsqueeze(2).to_broadcast([P, H, TS]),
                                        -1.0, None, ALU.mult)
        for b in range(NB):
            last = nc.vector.tensor_scalar(nl_new[:, b * SM:(b + 1) * SM].rearrange("p (h q) -> p h q", h=H),
                                           LF[0:SM, 2, 0:H].unsqueeze(2).to_broadcast([SM, H, TS]),
                                           -1.0, None, ALU.mult)
        last.then_inc(sem("nl_ready"), 1)
        dve.wait_ge(sem("sT_done"), NB * NPG + 1)
        nc.vector.tensor_copy(STs[:, :], ps[:, 6, :])
        nc.vector.tensor_copy(STn[:, :], ps[0:SM, 7, 0:256]).then_inc(sem("sT_ready"), 1)
        for g2 in range(2):
            dve.wait_ge(sem("sample_logits"), g2 + 1)
            link(nc.vector.tensor_reduce(mx[:, 0, g2:g2 + 1], ps[:, 4 + g2, 0:T], AX.X, ALU.max))
            nc.vector.tensor_scalar(nmx[:, 0, g2:g2 + 1], mx[:, 0, g2:g2 + 1], -1.0, None,
                                    ALU.mult).then_inc(sem("sample_max"), 1)
        for g2 in range(2):
            dve.wait_ge(sem("sample_exp"), g2 + 1)
            link(nc.vector.reciprocal(rden[:, 0, g2:g2 + 1], den[:, 0, g2:g2 + 1]))
            nc.vector.tensor_scalar(Ps[:, g2, :], Ps[:, g2, :], rden[:, 0, g2:g2 + 1], None,
                                    ALU.mult).then_inc(sem("sample_p"), 1)
        dve.wait_ge(sem("sample_pv"), NB * NPG)
        nc.vector.tensor_copy(ya[:, :, TP:T], ps[:, 2, 0:256].rearrange("p (h s) -> p h s", h=H)).then_inc(
            sem("ya_ready"), 1)

        dve.wait_ge(out_stored, 6 * 16)
        dve.wait_ge(sem("rows_done"), 2)
        nc.vector.memset(ext[:, :, 0:CW - 1], 0.0).then_inc(sem("ext_edges"), 1)
        nc.vector.tensor_copy(b_row[:, :], ps[0:H, 4, 0:T])
        link(nc.vector.tensor_copy(r_row[:, :], ps[0:H, 3, 0:T]))
        nc.vector.tensor_tensor_scan(R_row[:, 0:TP], r_row[:, 0:TP], r_row[:, 0:TP], 0.0, ALU.max, ALU.max)
        r_s, R_s = (x[:, TP:T].rearrange("h (b t) -> h b t", t=TS) for x in (r_row, R_row))
        dve.wait_ge(sem("state_loaded"), 3 * 16)
        for t in range(TS):
            link(nc.vector.tensor_tensor(R_s[:, :, t], r_s[:, :, t], m0[:, :] if t == 0 else R_s[:, :, t - 1], ALU.max))
        nc.vector.tensor_tensor(m_row[:, :], b_row[:, :], R_row[:, :], ALU.add).then_inc(sem("rows_sum"), 1)
        nc.vector.tensor_scalar(nR_row[:, :], R_row[:, :], -1.0, None, ALU.mult).then_inc(sem("rows_sum"), 1)
        nc.vector.tensor_tensor(ws_row[:, TP:T].rearrange("h (b t) -> h b t", t=TS), r_s,
                                R_s[:, :, TS - 1].unsqueeze(2).to_broadcast([H, NB, TS]),
                                ALU.subtract).then_inc(sem("rows_sum"), 1)
        nc.vector.tensor_tensor(s_rows[:, 0, :].rearrange("h (b t) -> h b t", t=TS),
                                m0[:, :].unsqueeze(2).to_broadcast([H, NB, TS]), R_s,
                                ALU.subtract).then_inc(sem("rows_sum"), 1)
        dve.wait_ge(sem("rows_exp"), 4)
        nc.vector.tensor_copy(s_rows[:, 1, :], nR_row[:, TP:T])
        nc.vector.tensor_copy(s_rows[:, 2, :], em_row[:, TP:T]).then_inc(sem("s_rows_ready"), 1)
        dve.wait_ge(sem("edges_done"), 2)
        nc.vector.tensor_copy(n0T[:, :], ps[:, 0, 0:NB * H])
        nc.vector.tensor_copy(
            ext[:, :, EXT:EXTW].rearrange("p j (b r) -> p j b r", r=EXTS)[:, :, :, 0:CW - 1],
            ps[:, 5, 0:384].rearrange("p (j b r) -> p j b r", j=2 * H, b=NB)).then_inc(sem("ext_edges"), 1)

        def conv(j):
            if j >= 2:
                dve.wait_ge(sem("conv_used"), 2 * (j - 1))
            n = EXTW - CW + 1
            for c in range(CW):
                w, src, acc = vecs[:, V_CW + c * 16 + j:V_CW + c * 16 + j + 1], ext[:, j, c:c + n], conv_acc[:, j % 2, 0:n]
                if c == 0:
                    link(nc.vector.tensor_scalar(acc, src, w, None, ALU.mult))
                elif c < CW - 1:
                    link(nc.vector.scalar_tensor_tensor(acc, src, w, acc, ALU.mult, ALU.add))
                else:
                    nc.vector.scalar_tensor_tensor(acc, src, w, acc, ALU.mult, ALU.add).then_inc(sem("conv_done"), 1)

        g = groups["in_m"]
        for i in range(4):
            if i < 2:
                split_turns(g.turn + i * g.turns, g.turns)
            else:
                for t in range(g.turns):
                    split_turns(g.turn + i * g.turns + t, 1)
                    conv((i - 2) * H + 2 * t)
                    conv((i - 2) * H + 2 * t + 1)
            for b in range(NBANK):
                wait_bank(dve, g, g.turn + i * g.turns, g.index + i, b)
                if i < 2:
                    j = i * H + b
                    nc.vector.tensor_copy(ext[:, j, CW - 1:EXT], ps[:, b, 0:TP])
                    nc.vector.tensor_copy(
                        ext[:, j, EXT:EXTW].rearrange("p (b r) -> p b r", r=EXTS)[:, :, CW - 1:EXTS],
                        ps[:, b, TP:T].rearrange("p (b t) -> p b t", t=TS)).then_inc(banks_free, 1)
                else:
                    nc.vector.tensor_copy((vm if i == 2 else om)[:, b, :], ps[:, b, 0:T]).then_inc(banks_free, 1)
            if i < 2:
                dve.wait_ge(banks_free, NBANK + (g.index + i + 1) * NBANK)
                x = ext[:, i * H:(i + 1) * H, :]
                nc.vector.tensor_copy(conv_last[:, i * H:(i + 1) * H, 0:3], x[:, :, EXT - 3:EXT]).then_inc(sem("conv_last"), 1)
                nc.vector.tensor_copy(conv_last[:, i * H:(i + 1) * H, 3:27].rearrange("p j (b r) -> p j b r", r=3),
                                      x[:, :, EXT:EXTW].rearrange("p j (b r) -> p j b r", r=EXTS)[:, :, :, TS:EXTS]
                                      ).then_inc(sem("conv_last"), 1)
        dve.wait_ge(sem("conv_used"), 4 * H)
        nc.vector.tensor_scalar(ext[:, H:2 * H, 0:T], ext[:, H:2 * H, 0:T], SCALE, None, ALU.mult).then_inc(sem("km_ready"), 1)
        for b in range(4):
            dve.wait_ge(sem("conv_rows_done"), b + 1)
            nc.vector.tensor_copy(conv_rows[:, b * 512:(b + 1) * 512], ps[0:27, 2 + b, :]).then_inc(sem("conv_rows_ready"), 1)
        dve.wait_ge(sem("nat_done"), 1)
        nc.vector.tensor_copy(nat[:, :, :], ps[:, 1, 0:48].rearrange("p (a h) -> p a h", h=H)).then_inc(sem("nat_ready"), 1)
        dve.wait_ge(sem("s_all_ready"), 2)
        link(nc.vector.tensor_tensor(Ws[:, :, :], s_all[0:SM, :, 1, :], mask4_t[:, :].unsqueeze(1).to_broadcast([SM, H, SM]), ALU.add))
        nc.vector.tensor_tensor(Ws[:, :, :], Ws[:, :, :], nat[0:SM, 2, :].unsqueeze(2).to_broadcast([SM, H, SM]),
                                ALU.add).then_inc(sem("ws_logits"), 1)
        link(nc.vector.tensor_tensor(qw[:, :, :], ext[:, 0:H, TP:T], s_all[:, :, 0, :], ALU.mult))
        nc.vector.tensor_tensor(qn[:, :, :].rearrange("p h (b t) -> p h b t", t=TS),
                                qw[:, :, :].rearrange("p h (b t) -> p h b t", t=TS),
                                n0T[:, :].rearrange("p (b h) -> p h b", h=H).unsqueeze(3).to_broadcast([P, H, NB, TS]),
                                ALU.mult).then_inc(sem("qn_ready"), 1)
        dve.wait_ge(sem("ws_exp"), 1)
        dve.wait_ge(sem("ws_scores"), 1)
        nc.vector.tensor_tensor(Ws[:, :, :], Ws[:, :, :], ps[0:SM, 0, 0:256].rearrange("p (h s) -> p h s", h=H),
                                ALU.mult).then_inc(sem("ws_ready"), 1)
        for h in range(H):
            b = h % 2
            dve.wait_ge(sem("sm_done"), h + 1)
            nc.vector.tensor_tensor(Wt[:, b, :], ps[:, 1, 0:384], mask_t[:, :], ALU.add).then_inc(sem("e_logits"), 1)
            dve.wait_ge(sem("e_exp"), 2 * (h + 1))
            nc.vector.tensor_tensor(Wt[:, b, :], Wt[:, b, :], ps[:, 0, 0:384], ALU.mult).then_inc(sem("w_ready"), 1)
            dve.wait_ge(sem("num_done"), h + 1)
            dve.wait_ge(sem("em_ready"), h + 1)
            link(nc.vector.scalar_tensor_tensor(dn[:, b, :], ps[:, 2, TP:512], -1.0, em_all[:, b, :], ALU.mult, ALU.max))
            link(nc.vector.tensor_tensor(dn[:, b, :], ps[:, 2, TP:512], dn[:, b, :], ALU.max))
            link(nc.vector.reciprocal(dn[:, b, :], dn[:, b, :]))
            nc.vector.tensor_tensor(vm[:, h, 0:TP], ps[:, 2, 0:TP], dn[:, b, :], ALU.mult).then_inc(sem("h_ready"), 1)
            dve.wait_ge(sem("C_decayed"), h + 1)
            dve.wait_ge(sem("dC_done"), 2 * (h + 1))
            for c in range(2):
                x = C[:, b, 4 * c:4 * c + 4, :]
                nc.vector.tensor_tensor(x, x, ps[:, 3 + c, :].rearrange("p (b e) -> p b e", b=4), ALU.add).then_inc(sem("C_new"), 1)
            dve.wait_ge(sem("Cp_ready"), h + 1)
            nc.vector.tensor_copy(n_new[:, 0, h:h + 1], ps[:, 7, HD:HD + 1])
            w_last = s_all[:, h, 0, :].rearrange("p (b t) -> p b t", t=TS)[:, :, TS - 1]
            link(nc.vector.tensor_tensor(n_new[:, 1:1 + NB, h], w_last, n0T[:, h:NB * H:H], ALU.mult))
            nc.vector.tensor_tensor(n_new[:, 1:1 + NB, h], n_new[:, 1:1 + NB, h], ps[:, 7, 256:256 + NB],
                                    ALU.add).then_inc(sem("n_new_ready"), 1)
        dve.wait_ge(sem("qC_done"), H)
        dn_s, den_s = dn[:, 0, :].rearrange("p (h s) -> p h s", h=H), ps[:, 5, 256:512].rearrange("p (h s) -> p h s", h=H)
        link(nc.vector.scalar_tensor_tensor(dn_s, den_s, -1.0, s_all[:, :, 2, :], ALU.mult, ALU.max))
        link(nc.vector.tensor_tensor(dn_s, den_s, dn_s, ALU.max))
        link(nc.vector.reciprocal(dn[:, 0, :], dn[:, 0, :]))
        nc.vector.tensor_tensor(vm[:, :, TP:T], ps[:, 5, 0:256].rearrange("p (h s) -> p h s", h=H),
                                dn[:, 0, :].rearrange("p (h s) -> p h s", h=H), ALU.mult).then_inc(sem("h_ready"), 1)
        dve.wait_ge(sem("nT_done"), 1)
        nc.vector.tensor_copy(n_rows[:, 0, :], ps[0:NB * H, 0, 0:HD]).then_inc(sem("n_rows_ready"), 1)
        nc.vector.tensor_copy(n_rows[0:H, 1, :], ps[0:H, 0, HD:2 * HD]).then_inc(sem("n_rows_ready"), 1)
        for kind in ("C_stored", "Cp_stored"):
            for b in range(2):
                dve.wait_ge(sem(f"{kind}{b}"), 16 * (H // 2))
        dve.wait_ge(sem("o_sigmoid"), 1)
        dve.wait_ge(sem("sum_done"), SUM_Y + 2 * H)
        rsqrt_mean(3, root[:, :, :], rs[0:H, :, :], xt[0:H, :, :], ps[0:H, 1:3, 0:T], HD).then_inc(sem("root_ready"), 1)
        for j in range(KD + 1):
            if j < KD:
                if j >= 2:
                    dve.wait_ge(sem("xn_ready"), 32 + j - 1)
                src = (ya if j < H else vm)[:, j % H, :]
                gain = vecs[:, (V_GA if j < H else V_GM) + j % H:(V_GA if j < H else V_GM) + j % H + 1]
                ins = head_norm(2 * H + j, src, gain)(xt[:, j % 2, :])
                if j >= H:
                    link(ins)
                    ins = nc.vector.tensor_tensor(xt[:, j % 2, :], xt[:, j % 2, :], om[:, j % H, :], ALU.mult)
                ins.then_inc(sem("xn_tmp"), 1)
            if j >= 1:
                operand_lo(2, j - 1, y_hi, y_lo)
        g = groups["out"]
        for half in range(2):
            split_turns(g.turn + half * g.turns, g.turns)
            residual(g, half, 1.0)
        norm(3, V_FFN[1], *mem[1]["x"])
        swiglu(1)
        for i in range(12):
            if i % 2 == 1:
                dve.wait_ge(sem("y_rows_done"), i + 1)
                t, n = TT[i // 4]
                nc.vector.tensor_copy(y_rows[0:n, t, (i % 4) * 512:(i % 4 + 1) * 512], ps[0:n, i % 4, :]).then_inc(sem("y_rows_ready_v"), 1)

    @block.tensor
    def _(pe):
        mm, tr = nc.tensor.matmul, nc.tensor.transpose

        def turn_products(g, turn0, gi, kt, x_hi, x_lo, first, last, x_ready):
            for pair in range(2):
                slots = [s for s in (2 * pair, 2 * pair + 1) if not (last and 0 < g.real % SLOTS <= s)]
                pe.wait_ge(w_lo_ready, (turn0 + kt) * SLOTS + (2 * pair + 2))
                pe.wait_ge(x_ready[0], kt * SLOTS + (x_ready[1] + slots[-1] + 1))
                for b, c in enumerate(g.tiles):
                    if first and pair == 0:
                        pe.wait_ge(banks_free, gi * NBANK + (b + 1))
                    out = ps[:, b, 0:T]
                    for s in slots:
                        hi, lo, k = w_hi[:, s, c:c + P], w_lo[:, s, c:c + P], kt * SLOTS + s
                        mm(out, hi, x_hi[:, k, :], start=first and pair == 0 and s == slots[0], stop=False)
                        mm(out, hi, x_lo[:, k, :], start=False, stop=False)
                        ins = mm(out, lo, x_hi[:, k, :], start=False, stop=last and pair == 1 and s == slots[-1])
                    if b == len(g.tiles) - 1:
                        ins.then_inc(w_used, 1)
                    elif last and pair == 1:
                        ins.then_inc(bank_done, 1 if b < len(g.tiles) - 2 else NBANK + 1 - len(g.tiles))

        def group_products(g, i, x_hi, x_lo, x_ready):
            turn0, gi = i * g.turns + g.turn, i + g.index
            turn_products(g, turn0, gi, 0, x_hi, x_lo, True, False, x_ready)
            with pe.Fori(1, g.turns - 1) as kt:
                turn_products(g, turn0, gi, kt, x_hi, x_lo, False, False, x_ready)
            turn_products(g, turn0, gi, g.turns - 1, x_hi, x_lo, False, True, x_ready)

        def groups_products(g, count, x_hi, x_lo, x_ready):
            if count == 1:
                group_products(g, 0, x_hi, x_lo, x_ready)
            else:
                with pe.Fori(0, count) as i:
                    group_products(g, i, x_hi, x_lo, x_ready)

        def sums(i, bank, stop_start):
            pe.wait_ge(sem("sq_ready"), i + 1)
            mm(ps[:, bank, 0:T], ones[:, :], sq[:, i % 2, :], start=stop_start[0],
               stop=stop_start[1]).then_inc(sem("sum_done"), 1)

        def norm_sums(n):
            for t in range(KD):
                sums(SUM_X[n] + t, 0, (t == 0, t == KD - 1))

        def head_sums(i0, bank, used, used0, n):
            for j in range(2 * H):
                pe.wait_ge(sem("sq_ready"), i0 + j + 1)
                mm(ps[0:H, bank + j // H, 0:T], one_hot[:, j % H, :], sq[:, j % 2, :], start=j % H == 0,
                   stop=j % H == H - 1).then_inc(sem("sum_done"), 1)
            pe.wait_ge(sem("root_ready"), n + 1)
            for j in range(2 * H):
                if j >= 2:
                    pe.wait_ge(sem(used), used0 + j - 1)
                mm(ps[:, bank + j % 2, 0:T], sel[:, j % H, :], root[:, j // H, :], start=True,
                   stop=True).then_inc(sem("spread_done"), 1)

        def swiglu(n):
            x, hid = mem[n]["x"], mem[n]["hid"]
            xr, hr = (sem("xn_ready"), 48 * n), sem("hid_ready")
            groups_products(groups[f"gu{n}a"], 6, *x, xr)
            groups_products(groups[f"down{n}a"], 2, *hid, (hr, 43 * n))
            groups_products(groups[f"gu{n}b"], 4, *x, xr)
            groups_products(groups[f"gu{n}c"], 1, *x, xr)
            groups_products(groups[f"down{n}b"], 2, *hid, (hr, 43 * n + CHUNK))

        pe.wait_ge(pool_const, 4)
        pe.wait_ge(sem("x_loaded"), 48)
        for t in range(KD):
            if t >= 4:
                pe.wait_ge(sem("xT_copied"), t - 3)
            for r, n in TT:
                ins = tr(ps[:, t % 4, r * P:r * P + n], x_rows[0:n, r, t * P:(t + 1) * P], ident[0:n, 0:n])
            ins.then_inc(sem("xT_done"), 1)
        pe.wait_ge(small_loaded, 16 * 16)
        tr(ps[:, 7, 0:P], vec_rows[:, 0, :], ident[:, :]).then_inc(w_used, 2)
        tr(ps[:, 7, P:P + 18], vec_rows[0:18, 1, :], ident[0:18, 0:18]).then_inc(sem("vecT_done"), 1)
        pe.wait_ge(sem("xT_copied"), KD)
        norm_sums(0)
        pe.wait_ge(sem("vecs_ready"), 1)
        swiglu(0)
        pe.wait_ge(banks_free, NBANK + (G_A - 1) * NBANK + 1)
        norm_sums(1)
        groups_products(groups["in_a"], 3, xm_hi, xm_lo, (sem("xn_ready"), 16))

        pe.wait_ge(banks_free, NBANK + G_M * NBANK)
        for t, n in TT:
            for k in range(KD):
                for x in (xm_hi, xm_lo):
                    ins = mm(ps[0:n, 0, t * 24:(t + 1) * 24], x[:, k, t * P:t * P + n].bitcast(F32), w_gates[:, k, :],
                             start=k == 0 and x is xm_hi, stop=k == KD - 1 and x is xm_lo)
        ins.then_inc(sem("gates_done"), 1)

        def natural(src, bank0, made, read=None):
            for i in range(6):
                (t, n), half = TT[i // 2], i % 2
                if read:
                    pe.wait_ge(sem(read), i + 1)
                for j in range(4):
                    ins = tr(ps[0:n, bank0 + i, j * P:(j + 1) * P], src(4 * half + j, t * P, n), ident[:, :])
                ins.then_inc(sem(made), 1)

        natural(lambda h, c, n: ya[:, h, c:c + n], 2, "vT_done")
        pe.wait_ge(sem("abs_ready"), 1)
        head_sums(SUM_QK, 0, "qk_normed", 0, 0)
        pe.wait_ge(sem("qk_normed"), 2 * H)
        natural(lambda h, c, n: ka[:, h, c:c + n], 2, "kT_done", "vn_ready")
        pe.wait_ge(sem("lf_ready"), 1)
        lf = lambda t, kind, n=P: LF[0:n, t, kind * H:(kind + 1) * H]
        mm(ps[0:H, 1, 0:P], lf(0, 0), neg_upper[:, :], start=True, stop=True)
        mm(ps[0:H, 1, P:TP], lf(0, 0), neg_ones[:, :], start=True, stop=False)
        mm(ps[0:H, 1, P:TP], lf(1, 0), neg_upper[:, :], start=False, stop=True).then_inc(sem("c_done"), 1)
        pe.wait_ge(sem("neg_c_ready"), 1)
        pe.wait_ge(sem("kn_ready"), 6)

        def scores(h):
            if h >= 2:
                pe.wait_ge(sem("s_masked"), h - 1)
            for q, c0, c1 in ((0, 0, P), (1, P, 384)):
                out, n = ps[:, h % 2, c0:c1], c1 - c0
                mm(out, qa[:, h, q * P:(q + 1) * P], ka[:, h, 0:n], start=True, stop=False)
                ins = mm(out, sel[:, h, :], neg_c[:, 0:n], start=False, stop=True)
            ins.then_inc(sem("s_done"), 1)

        def probs_t(h):
            pe.wait_ge(sem("p_ready"), h + 1)
            if h >= 2:
                pe.wait_ge(sem("pt_ready"), h - 1)
            for c in range(3):
                ins = tr(ps[:, 2 + h % 2, c * P:(c + 1) * P], Sm[:, h % 2, c * P:(c + 1) * P], ident[:, :])
            ins.then_inc(sem("pt_done"), 1)

        def values(h):
            pe.wait_ge(sem("pt_ready"), h + 1)
            if h >= 2:
                pe.wait_ge(sem("ya_ready"), h - 1)
            mm(ps[:, 4 + h % 2, 0:TP], vn[:, 0, h * HD:(h + 1) * HD], PT[:, h % 2, 0:TP], start=True, stop=True)
            mm(ps[:, 4 + h % 2, P:TP], vn[:, 1, h * HD:(h + 1) * HD], PT[:, h % 2, TP:384], start=False, stop=True,
               skip_group_check=True).then_inc(sem("o_done"), 1)

        scores(0)
        for h in range(H):
            if h + 1 < H:
                scores(h + 1)
            probs_t(h)
            if h >= 1:
                values(h - 1)
        values(H - 1)

        pe.wait_ge(sem("s_masked"), H)
        pe.wait_ge(sem("pt_ready"), H)
        pe.wait_ge(sem("ya_ready"), H)
        bhq = lambda x: x.rearrange("p (b h q) -> p b h q", b=NB, h=H)
        for p in range(NB * NPG + 1):
            if p < NB * NPG:
                pe.wait_ge(sem(f"page_loaded{p % 3}"), 16 * (p // 3 + 1))
                if p >= 2:
                    pe.wait_ge(sem("kpT_lo"), p - 1)
                    pe.wait_ge(sem("kpT_hi"), p - 1)
                for half in range(2):
                    for i in range(4):
                        c = (4 * half + i) * HD
                        ins = tr(ps[:, 2 * (p % 2) + half, i * P:(i + 1) * P], page[:, p % 3, c:c + HD], ident[:, :])
                    ins.then_inc(sem("kpT_done"), 1)
            if p >= 1:
                b, c = (p - 1) // NPG, (p - 1) % NPG
                pe.wait_ge(sem("kpT_lo"), p)
                pe.wait_ge(sem("kpT_hi"), p)
                for h in range(H):
                    col = c * 256 + b * SM + h * TS
                    ins = mm(ps[:, 6, col:col + TS], kpT[:, (p - 1) % 2, h * HD:(h + 1) * HD],
                             qa[:, h, TP + b * TS:TP + (b + 1) * TS], start=True, stop=True)
                ins.then_inc(sem("sT_done"), 1)
        for h in range(H):
            ins = mm(bhq(ps[0:SM, 7, 0:256])[:, :, h, :], ka[:, h, TP:T], qa[:, h, TP:T], start=True, stop=True)
        ins.then_inc(sem("sT_done"), 1)
        pe.wait_ge(sem("sT_ready"), 1)
        pe.wait_ge(sem("nl_ready"), 1)
        for g2 in range(2):
            r = slice(g2 * P, (g2 + 1) * P)
            o0, o1, o2 = ps[:, 4 + g2, 0:P], ps[:, 4 + g2, P:2 * P], ps[:, 4 + g2, 2 * P:T]
            add = dict(start=False, skip_group_check=True)
            mm(o0, STs[:, r], ident[:, :], start=True, stop=True)
            mm(o0, nl_past[:, 0, r], upper[:, :], stop=True, **add)
            mm(o1, STs[:, 256 + g2 * P:256 + (g2 + 1) * P], ident[:, :], stop=True, **add)
            mm(o1, nl_past[:, 0, r], ones[:, :], stop=True, **add)
            mm(o1, nl_past[:, 1, r], upper[:, :], stop=True, **add)
            mm(o2, STn[:, r], ident[0:SM, 0:SM], stop=True, **add)
            mm(o2, nl_past[:, 0, r], ones[:, 0:SM], stop=True, **add)
            mm(o2, nl_past[:, 1, r], ones[:, 0:SM], stop=True, **add)
            mm(o2, nl_new[:, r], upper4[:, :], stop=True, **add)
            mm(o2, spread[:, r], mask4_q[:, :], stop=True, **add).then_inc(sem("sample_logits"), 1)
        for g2 in range(2):
            pe.wait_ge(sem("sample_p"), g2 + 1)
            tr(ps[:, 0, g2 * P:(g2 + 1) * P], Ps[:, g2, 0:P], ident[:, :])
            tr(ps[:, 0, 256 + g2 * P:256 + (g2 + 1) * P], Ps[:, g2, P:2 * P], ident[:, :])
            ins = tr(ps[0:SM, 1, g2 * P:(g2 + 1) * P], Ps[:, g2, 2 * P:T], ident[:, :])
        ins.then_inc(sem("sample_pT"), 1)
        pe.wait_ge(sem("sample_pT_ready"), 2)
        for h in range(H):
            mm(ps[:, 2, h * SM:(h + 1) * SM], vn[0:SM, 2, h * HD:(h + 1) * HD], bhq(PTn[:, :])[:, :, h, :],
               start=h == 0, stop=True, skip_group_check=True)
        for p in range(NB * NPG):
            n, b, c = NB * NPG + p, p // NPG, p % NPG
            pe.wait_ge(sem(f"page_loaded{n % 3}"), 16 * (n // 3 + 1))
            for h in range(H):
                col = c * 256 + b * SM + h * TS
                ins = mm(ps[:, 2, h * SM + b * TS:h * SM + (b + 1) * TS], page[:, n % 3, h * HD:(h + 1) * HD],
                         PTs[:, col:col + TS], start=False, stop=True, skip_group_check=True)
            ins.then_inc(sem("sample_pv"), 1)

        gi_ = lambda t, n=P: G[0:n, t, 2 * H:3 * H]
        for bank, up, one, up4 in ((3, neg_upper, neg_ones, neg_upper4), (4, upper, ones, upper4)):
            for t in range(2):
                o = ps[0:H, bank, t * P:(t + 1) * P]
                if bank == 3:
                    mm(o, gi_(t), ident[:, :], start=True, stop=False)
                if t == 1:
                    mm(o, lf(0, 1), one[:, :], start=bank == 4, stop=False)
                mm(o, lf(t, 1), up[:, :], start=bank == 4 and t == 0, stop=True)
            o = ps[0:H, bank, TP:T]
            if bank == 3:
                mm(o, gi_(2, SM), ident[0:SM, 0:SM], start=True, stop=False)
            mm(o, lf(2, 1, SM), up4[:, :], start=bank == 4, stop=True).then_inc(sem("rows_done"), 1)
        pe.wait_ge(sem("state_loaded"), 3 * 16)
        tr(ps[:, 0, 0:NB * H], n_rows[:, 0, :], ident[0:NB * H, 0:NB * H]).then_inc(sem("edges_done"), 1)
        for j in range(2 * H):
            ins = tr(ps[:, 5, j * 24:(j + 1) * 24], conv_rows[0:24, j * P:(j + 1) * P], ident[0:24, 0:24])
        ins.then_inc(sem("edges_done"), 1)
        pe.wait_ge(sem("ext_edges"), 2)
        pe.wait_ge(sem("ya_ready"), H + 1)
        groups_products(groups["in_m"], 4, xm_hi, xm_lo, (sem("xn_ready"), 16))

        pe.wait_ge(banks_free, NBANK + G_O * NBANK)
        pe.wait_ge(sem("s_rows_ready"), 1)
        for b in range(2):
            for j in range(4):
                ins = mm(ps[:, 6 + b, j * 96:(j + 1) * 96], sel[:, 4 * b + j, :], s_rows[:, :, :], start=True, stop=True)
            ins.then_inc(sem("s_all_done"), 1)
        natural(lambda h, c, n: vm[:, h, c:c + n], 0, "vmT_done")
        pe.wait_ge(sem("km_ready"), 1)
        natural(lambda h, c, n: ext[:, H + h, c:c + n], 0, "kmT_done", "vmn_ready")
        pe.wait_ge(sem("kmn_ready"), 6)
        for j in range(2 * H):
            ins = tr(ps[0:27, 2 + j // 4, (j % 4) * P:(j % 4 + 1) * P], conv_last[:, j, :], ident[:, :])
            if j % 4 == 3:
                ins.then_inc(sem("conv_rows_done"), 1)
        pe.wait_ge(sem("rows_exp"), 3)
        for a, row in enumerate((r_row, ws_row)):
            for t, n in TT:
                ins = tr(ps[0:n, 1, (3 * a + t) * H:(3 * a + t + 1) * H], row[:, t * P:t * P + n], ident[0:H, 0:H])
        ins.then_inc(sem("nat_done"), 1)
        for h in range(H):
            ins = mm(ps[0:SM, 0, h * SM:(h + 1) * SM], ext[:, H + h, TP:T], ext[:, h, TP:T], start=True, stop=True)
        ins.then_inc(sem("ws_scores"), 1)
        pe.wait_ge(sem("conv_rows_ready"), 4)
        pe.wait_ge(sem("qn_ready"), 1)
        pe.wait_ge(sem("ws_ready"), 1)
        add = dict(start=False, skip_group_check=True)
        mm(ps[:, 5, 256:512], ones[:, :], qn[:, :, :], start=True, stop=True)
        mm(ps[:, 5, 256:512], ones[0:SM, :], Ws[:, :, :], stop=True, **add)
        for h in range(H):
            mm(ps[:, 5, h * SM:(h + 1) * SM], vmn[0:SM, 2, h * HD:(h + 1) * HD], Ws[:, h, :], stop=True, **add)
        pe.wait_ge(sem("nat_ready"), 1)
        pe.wait_ge(sem("s_all_ready"), 2)
        pe.wait_ge(sem("kw_ready"), 3)
        for h in range(H):
            hd = slice(h * HD, (h + 1) * HD)
            k_, q_ = ext[:, H + h, :], ext[:, h, :]
            if h >= 1:
                pe.wait_ge(sem("w_ready"), h)
            mm(ps[:, 0, 0:TP], k_[:, 0:P], q_[:, 0:TP], start=True, stop=True)
            mm(ps[:, 0, TP:384], k_[:, P:TP], q_[:, P:TP], start=True, stop=True)
            mm(ps[:, 1, 0:TP], sel[:, h, :], nR_row[:, 0:TP], start=True, stop=True)
            mm(ps[:, 1, TP:384], sel[:, h, :], nR_row[:, P:TP], start=True, stop=True).then_inc(sem("sm_done"), 1)
            if h >= 1:
                pe.wait_ge(sem("em_ready"), h)
            mm(ps[:, 6, 0:TP], sel[:, h, :], em_row[:, 0:TP], start=True, stop=True).then_inc(sem("em_done"), 1)
            pe.wait_ge(sem(f"C_loaded{h % 2}"), 16 * (h // 2 + 1))
            for b in range(NB):
                ins = mm(ps[:, 5, h * SM + b * TS:h * SM + (b + 1) * TS], C[:, h % 2, b, :],
                         qw[:, h, b * TS:(b + 1) * TS], stop=True, **add)
            ins.then_inc(sem("qC_done"), 1)
            pe.wait_ge(sem("v_seq_ready"), h + 1)
            if h >= 1:
                pe.wait_ge(sem("C_new"), 2 * h)
            for c in range(2):
                mm(ps[:, 3 + c, :], kmn[0:SM, 2, hd], v_seq[:, 4 * c:4 * c + 4, :], start=True,
                   stop=True).then_inc(sem("dC_done"), 1)
            if h >= 1:
                pe.wait_ge(sem("Cp_ready"), h)
                pe.wait_ge(sem("n_new_ready"), h)
            mm(ps[:, 7, 0:HD], kmn[:, 0, hd], vmn[:, 0, hd], start=True, stop=False)
            mm(ps[:, 7, 0:HD], kmn[:, 1, hd], vmn[:, 1, hd], start=False, stop=True)
            mm(ps[:, 7, HD:HD + 1], kmn[:, 0, hd], ones[:, 0:1], start=True, stop=False)
            mm(ps[:, 7, HD:HD + 1], kmn[:, 1, hd], ones[:, 0:1], start=False, stop=True)
            mm(ps[:, 7, 256:256 + NB], kmn[0:SM, 2, hd], block4[:, 0:SM:TS], start=True, stop=True).then_inc(
                sem("Cp_done"), 1)
            pe.wait_ge(sem("w_ready"), h + 1)
            if h >= 1:
                pe.wait_ge(sem("h_ready"), h)
            W = Wt[:, h % 2, :]
            mm(ps[:, 2, 0:TP], vmn[:, 0, hd], W[:, 0:TP], start=True, stop=True)
            mm(ps[:, 2, P:TP], vmn[:, 1, hd], W[:, TP:384], stop=True, **add)
            mm(ps[:, 2, TP:512], ones[:, :], W[:, 0:TP], stop=True, **add)
            mm(ps[:, 2, TP + P:512], ones[:, :], W[:, TP:384], stop=True, **add).then_inc(sem("num_done"), 1)
        pe.wait_ge(sem("n_new_ready"), H)
        tr(ps[0:NB * H, 0, 0:HD], n_new[:, 1:1 + NB, :].rearrange("p b h -> p (b h)"), ident[:, :])
        tr(ps[0:H, 0, HD:2 * HD], n_new[:, 0, :], ident[:, :]).then_inc(sem("nT_done"), 1)
        pe.wait_ge(sem("h_ready"), H + 1)
        head_sums(SUM_Y, 1, "xn_tmp", 32, 1)
        pe.wait_ge(sem("xn_tmp"), 48)
        pe.wait_ge(sem("n_rows_ready"), 2)
        groups_products(groups["out"], 2, y_hi, y_lo, (sem("xn_ready"), 32))
        pe.wait_ge(banks_free, NBANK + (G_O + 1) * NBANK + 1)
        norm_sums(3)
        swiglu(1)
        pe.wait_ge(banks_free, NBANK + n_groups * NBANK)
        for i in range(12):
            t, n = TT[i // 4]
            if i >= 4:
                pe.wait_ge(sem("y_rows_ready" if i % 2 == 0 else "y_rows_ready_v"), (i - 4) // 2 + 1)
            for j in range(4):
                ins = tr(ps[0:n, i % 4, j * P:(j + 1) * P], X[:, (i % 4) * 4 + j, t * P:t * P + n], ident[:, :])
            ins.then_inc(sem("y_rows_done"), 1)

    ctx.close()


_OUTS = [("y_prompt", (1, TP, D)), ("y_sample", (NB, TS, D)), ("k_prompt", (1, 1, TP, H, HD)),
         ("v_prompt", (1, 1, TP, H, HD)), ("logf_prompt", (1, 1, TP, H)), ("conv_prompt", (1, 1, CW - 1, QK)),
         ("C_prompt", (1, 1, H, HD, HD)), ("n_prompt", (1, 1, H, HD)), ("m_prompt", (1, 1, H)),
         ("k_sample", (1, NB, TS, H, HD)), ("v_sample", (1, NB, TS, H, HD)), ("logf_sample", (1, NB, TS, H)),
         ("conv_sample", (1, NB, CW - 1, QK)), ("C_sample", (1, NB, H, HD, HD)), ("n_sample", (1, NB, H, HD)),
         ("m_sample", (1, NB, H))]


def kernel(**inputs):
    import numpy as _np
    import concourse.bacc as _bacc
    from concourse.bass_utils import run_bass_kernel_spmd as _run

    nc = _bacc.Bacc("TRN2", target_bir_lowering=False, num_devices=1)
    arrays, A, O = {}, {}, {}
    for name, value in inputs.items():
        a = _np.ascontiguousarray(value)
        arrays[f"in_{name}"] = a
        A[name] = nc.dram_tensor(f"in_{name}", a.shape, mybir.dt.from_np(a.dtype), kind="ExternalInput").ap()
    for name, shape in _OUTS:
        O[name] = nc.dram_tensor(f"out_{name}", shape, F32, kind="ExternalOutput").ap()
    build(nc, A, O)
    r = _run(nc, [arrays], core_ids=[0])
    return tuple(r.results[0][f"out_{name}"] for name, _ in _OUTS)
```

```python
from contextlib import ExitStack

import concourse.bass as bass
from concourse import mybir
from concourse.alu_op_type import AluOpType as ALU

F32 = mybir.dt.float32
F32R = mybir.dt.float32r
I32 = mybir.dt.int32
ACT = mybir.ActivationFunctionType
AX = mybir.AxisListType

P = 128
D = 2048
KD = D // P
TP = 256
NB = 8
TS = 4
SM = NB * TS
T = TP + SM
H = 8
HD = 128
PAGE = 128
NPG = 2
F = 5504
CHUNK = 24
CW = 4
QK = 2 * H * HD
EPS = 1e-6
SCALE = float(HD) ** -0.5
BIG = 1.0e30
N_IN = 7192
COL_F_A = 3 * H * HD
COL_M = COL_F_A + H
COL_I_M = N_IN - 2 * H
UW = 1024
SLOTS = 4
NBANK = 8
EXT = CW - 1 + TP
EXTS = CW - 1 + TS
EXTW = EXT + NB * EXTS
TT = [(0, P), (1, P), (2, SM)]


class Group:

    def __init__(self, turn, index, nk, real, tiles):
        self.turn, self.index, self.real, self.tiles = turn, index, real, tiles
        self.turns = nk // SLOTS


def plan():
    turn, index, out = 0, 0, {}
    plain = [j * P for j in range(NBANK)]
    gate_up = [c for j in range(4) for c in (j * P, 512 + j * P)]
    swiglu = [("gu{}a", 6, KD, KD, gate_up), ("down{}a", 2, 24, 24, plain), ("gu{}b", 4, KD, KD, gate_up),
              ("gu{}c", 1, KD, KD, gate_up[:6]), ("down{}b", 2, 20, 19, plain)]
    mixer = [("in_a", 3, KD, KD, plain), ("in_m", 4, KD, KD, plain), ("out", 2, KD, KD, plain)]
    for n, part in ((0, swiglu), (0, mixer), (1, swiglu)):
        for name, count, nk, real, tiles in part:
            out[name.format(n)] = Group(turn, index, nk, real, tiles)
            turn += count * nk // SLOTS
            index += count
    return out, turn, index


def build(nc, A, O):
    groups, n_turns, n_groups = plan()
    ctx = ExitStack()
    sems = {}

    def sem(name):
        if name not in sems:
            sems[name] = ctx.enter_context(nc.semaphore(name))
        return sems[name]

    def area(side):
        scope = ExitStack()
        return scope, lambda name, shape, dt=F32: scope.enter_context(nc.sbuf_tensor(name, shape, dt, side=side))

    ctx.enter_context(nc.allow_non_contiguous_dma(reason="a few small transposed state vectors"))
    keep, t_ = area("left")
    ctx.enter_context(keep)
    ident, ones = t_("ident", [P, P]), t_("ones", [P, P])
    upper = t_("upper", [P, P])
    neg_upper, neg_ones = t_("neg_upper", [P, P]), t_("neg_ones", [P, P])
    lower = t_("lower", [P, P])
    block4 = t_("block4", [SM, SM])
    upper4, neg_upper4, lower4 = t_("upper4", [SM, SM]), t_("neg_upper4", [SM, SM]), t_("lower4", [SM, SM])
    mask_q = t_("mask_q", [P, 3 * P])
    mask_t = t_("mask_t", [P, 3 * P])
    mask4_q = t_("mask4_q", [SM, SM])
    mask4_t = t_("mask4_t", [SM, SM])
    spread = t_("spread", [SM, NB * SM])
    sel = t_("sel", [H, H, P])
    one_hot = t_("one_hot", [P, H, H])
    root = t_("root", [H, 2, T])
    vecs = t_("vecs", [P, 146])
    gq_scaled = t_("gq_scaled", [P, 1])
    w_gates = t_("w_gates", [P, KD, 3 * H])
    b_gates = t_("b_gates", [P, 3 * H])
    G = t_("G", [P, 3, 3 * H])
    LF = t_("LF", [P, 3, 2 * H])
    pages_sb = t_("pages_sb", [1, NB * NPG], I32)
    X = t_("X", [P, KD, T])
    w_raw = t_("w_raw", [P, SLOTS, UW])
    w_hi, w_lo = t_("w_hi", [P, SLOTS, UW], F32R), t_("w_lo", [P, SLOTS, UW], F32R)
    sq, xt, rs = t_("sq", [P, 2, T]), t_("xt", [P, 2, T]), t_("rs", [P, 2, T])
    gates_row = rs[0:3 * H, 0, :]
    ps = ctx.enter_context(nc.psum_tensor("ps", [P, NBANK, 512], F32))
    V_FFN, V_MIX, V_CB, V_CW, V_GQ, V_GK, V_GA, V_GM = (0, 32), 16, 48, 64, 128, 129, 130, 138

    scope, l_ = area("left")
    with scope:
        x_rows, vec_rows = l_("x_rows", [P, 3, D]), l_("vec_rows", [P, 2, P])

    def operand_memory(name):
        scope, r_ = area("right")
        with scope:
            return r_(name + "_hi", [P, KD, T], F32R), r_(name + "_lo", [P, KD, T], F32R)

    x_op = [operand_memory("x0"), operand_memory("x1")]
    xm_hi, xm_lo = operand_memory("xm")
    y_hi, y_lo = operand_memory("y")
    right_side, r_ = area("right")
    kmn = r_("kmn", [P, 3, H * HD])
    C = r_("C", [P, 2, NB, HD])
    v_seq = r_("v_seq", [SM, NB, HD])
    Ws, qw, qn = r_("Ws", [SM, H, SM]), r_("qw", [P, H, SM]), r_("qn", [P, H, SM])
    Wt = r_("Wt", [P, 2, 384])
    em_all, dn = r_("em_all", [P, 2, TP]), r_("dn", [P, 2, TP])
    Cp = r_("Cp", [P, 2, HD])
    r_("operand_rest", [P, 2 * KD * T - 8960])

    def swiglu_memory(n):
        scope, l_ = area("left")
        with scope:
            return dict(x=x_op[n], hid=(l_(f"hid_hi{n}", [P, CHUNK, T], F32R), l_(f"hid_lo{n}", [P, CHUNK, T], F32R)),
                        silu=l_(f"silu{n}", [P, 4, T]), prod=l_(f"prod{n}", [P, 4, T]))

    mem = [swiglu_memory(0), swiglu_memory(1)]
    scope_mixer, m_ = area("left")
    with scope_mixer:
        ya = m_("ya", [P, H, T])
        scope, l_ = area("left")
        with scope:
            qa, ka = l_("qa", [P, H, T]), l_("ka", [P, H, T])
            kn, vn = l_("kn", [P, 3, H * HD]), l_("vn", [P, 3, H * HD])
            mx, nmx, den, rden = (l_(n, [P, 2, 2]) for n in ("mx", "nmx", "den", "rden"))
            neg_c = l_("neg_c", [H, TP])
            page = l_("page", [P, 3, H * HD])
            kpT = l_("kpT", [P, 2, H * HD])
            lf_past = l_("lf_past", [P, NB * NPG, H])
            nl_past = l_("nl_past", [P, NPG, NB * SM])
            nl_new = l_("nl_new", [SM, NB * SM])
            scope_p, p_ = area("left")
            with scope_p:
                lt = p_("lt", [P, 3, 3, 2 * H])
                w_gates_hi, w_gates_lo = (p_(n, [P, KD, 3 * H], F32R) for n in ("w_gates_hi", "w_gates_lo"))
            scope_p, p_ = area("left")
            with scope_p:
                Sm, PT = p_("Sm", [P, 2, 384]), p_("PT", [P, 2, 384])
            flat = [x[:, :, :].rearrange("p h t -> p (h t)") for x in (qa, ka)]
            v_page = ([kn[:, i, :] for i in range(3)] + [page[:, (NB * NPG + i) % 3, :] for i in range(3)]
                      + [kpT[:, i, :] for i in range(2)]
                      + [x[:, i * H * HD:(i + 1) * H * HD] for x in flat for i in range(2)])
            VRING = len(v_page)
            STs, STn = l_("STs", [P, 512]), l_("STn", [SM, 256])
            PTs, PTn = STs, STn
            Ps = l_("Ps", [P, 2, T])
        scope, l_ = area("left")
        with scope:
            ext = l_("ext", [P, 2 * H, EXTW])
            vm, om = l_("vm", [P, H, T]), l_("om", [P, H, T])
            vmn = l_("vmn", [P, 3, H * HD])
            conv_rows = l_("conv_rows", [27, QK])
            conv_last = l_("conv_last", [P, 2 * H, 27])
            r_row, b_row, R_row, nR_row, m_row, em_row, ws_row = (
                l_(n, [H, T]) for n in ("r_row", "b_row", "R_row", "nR_row", "m_row", "em_row", "ws_row"))
            m0 = l_("m0", [H, NB])
            s_rows = l_("s_rows", [H, 3, SM])
            scope_c, c_ = area("left")
            with scope_c:
                conv_acc = c_("conv_acc", [P, 2, EXTW])
            s_all = l_("s_all", [P, H, 3, SM])
            nat = l_("nat", [P, 6, H])
            n_rows = l_("n_rows", [NB * H, 2, HD])
            n0T, n_new = l_("n0T", [P, NB * H]), l_("n_new", [P, 1 + NB, H])
    right_side.close()
    scope, l_ = area("left")
    with scope:
        y_rows = l_("y_rows", [P, 3, D])

    block = ctx.enter_context(nc.Block())
    w_loaded = [sem(f"w_loaded{s}") for s in range(SLOTS)]
    w_hi_ready, w_lo_ready, w_used = sem("w_hi_ready"), sem("w_lo_ready"), sem("w_used")
    bank_done, banks_free = sem("bank_done"), sem("banks_free")
    small_loaded, pool_const, const_ready = sem("small_loaded"), sem("pool_const"), sem("const_ready")
    out_stored = sem("out_stored")

    G_A, G_M, G_O = groups["in_a"].index, groups["in_m"].index, groups["out"].index

    def wait_bank(eng, g, turn, gi, b):
        n = len(g.tiles)
        if b < n - 1:
            eng.wait_ge(bank_done, gi * (NBANK - 1) + (b + 1 if b < n - 2 else NBANK - 1))
        else:
            eng.wait_ge(w_used, (turn + g.turns) * 2 + 2)

    def x_final(eng, n, t):
        if n == 0:
            eng.wait_ge(sem("xT_copied"), t + 1)
        else:
            g = groups["down0b" if n == 1 else "out"]
            eng.wait_ge(banks_free, NBANK + g.index * NBANK + t + 1)
    def tiles_of(w):
        return w[0].rearrange("(k p) n -> k p n", p=P)

    wg, wu, wd = ([tiles_of(A[f"w{n}_{kind}"]) for n in (1, 2)] for kind in ("gate", "up", "down"))
    wi, wo = tiles_of(A["w_in"]), tiles_of(A["w_out"])

    @block.sync
    def _(sp):
        def load_turn(turn, slots, parts, fresh=False):
            for s in slots:
                if not fresh:
                    sp.wait_ge(w_hi_ready, turn * SLOTS + (s + 1 - SLOTS))
                    sp.wait_ge(w_lo_ready, turn * SLOTS + (s + 1 - SLOTS))
                for c, src in parts(s):
                    sp.dma_start(w_raw[:, s, c:c + src.shape[-1]], src).then_inc(w_loaded[s], 32 // len(parts(s)))

        def load_group(g, turn, unit_src, start=0):
            whole = g.real // SLOTS
            with sp.Fori(start, whole) as kt:
                load_turn(turn + kt, range(SLOTS), lambda s: unit_src(kt * SLOTS + s))
            if whole < g.turns:
                load_turn(turn + whole, range(SLOTS), lambda s: unit_src(min(whole * SLOTS + s, g.real - 1)))

        def load_swiglu(n):
            def gate_up(col, w):
                return lambda k: [(0, wg[n][k, :, bass.ds(col, w)]), (512, wu[n][k, :, bass.ds(col, w)])]

            def down(k0, col):
                return lambda k: [(0, wd[n][k + k0, :, bass.ds(col, UW)])]

            g = groups[f"gu{n}a"]
            if n == 0:
                load_turn(0, range(SLOTS), gate_up(0, 512), fresh=True)
                load_group(g, g.turn, gate_up(0, 512), start=1)
            with sp.Fori(1 if n == 0 else 0, 6) as i:
                load_group(g, i * g.turns + g.turn, gate_up(i * 512, 512))
            g = groups[f"down{n}a"]
            with sp.Fori(0, 2) as i:
                load_group(g, i * g.turns + g.turn, down(0, i * UW))
            g = groups[f"gu{n}b"]
            with sp.Fori(0, 4) as i:
                load_group(g, i * g.turns + g.turn, gate_up(i * 512 + CHUNK * P, 512))
            g = groups[f"gu{n}c"]
            load_group(g, g.turn, gate_up(40 * P, 384))
            g = groups[f"down{n}b"]
            with sp.Fori(0, 2) as i:
                load_group(g, i * g.turns + g.turn, down(CHUNK, i * UW))

        load_swiglu(0)

        def columns(w, col):
            return lambda k: [(0, w[k, :, bass.ds(col, UW)])]

        def load_mixer(name, count, w, col, meanwhile=None):
            g = groups[name]
            if meanwhile:
                for kt in range(2):
                    load_turn(g.turn + kt, range(SLOTS), lambda s: columns(w, col)(kt * SLOTS + s))
                meanwhile()
                load_group(g, g.turn, columns(w, col), start=2)
            with sp.Fori(1 if meanwhile else 0, count) as i:
                load_group(g, i * g.turns + g.turn, columns(w, i * UW + col))

        def load_pages():
            sp.wait_ge(small_loaded, 16 * 16)
            sp.wait_ge(banks_free, NBANK + G_A * NBANK)

            def load_page(cache, p, dst, loaded):
                pid = sp.value_load(pages_sb[0:1, p:p + 1], min_val=0, max_val=cache.shape[1] - 1)
                sp.dma_start(dst, cache[0][bass.ds(pid, 1), :, :, :].rearrange("a s h d -> (a s) (h d)")).then_inc(
                    loaded, 16)

            for p in range(NB * NPG):
                if p >= 3:
                    sp.wait_ge(sem("kpT_done"), 2 * (p - 2))
                load_page(A["cache_k"], p, page[:, p % 3, :], sem(f"page_loaded{p % 3}"))
            for p in range(NB * NPG):
                if p == 0:
                    sp.wait_ge(out_stored, 6 * 16)
                if 3 <= p < 6:
                    sp.wait_ge(sem("kpT_done"), 2 * (NB * NPG - 5 + p))
                if 6 <= p < 8:
                    sp.wait_ge(sem("sT_done"), NB * NPG - 7 + p)
                if p == 8:
                    sp.wait_ge(sem("sT_done"), NB * NPG + 1)
                if p >= VRING:
                    sp.wait_ge(sem("sample_pv"), p - VRING + 1)
                load_page(A["cache_v"], p, v_page[p % VRING], sem(f"v_loaded{p % VRING}"))

        def state_traffic():
            sp.wait_ge(banks_free, NBANK + G_O * NBANK)

            def load_state(h):
                sp.dma_start(C[:, h % 2, :, :], A["state_C"][0, :, h, :, :].rearrange("b d e -> d b e")).then_inc(
                    sem(f"C_loaded{h % 2}"), 16)

            load_state(0)
            load_state(1)
            for h in range(H):
                sp.wait_ge(sem("C_new"), 2 * (h + 1))
                sp.dma_start(O["C_sample"][0, :, h, :, :].rearrange("b d e -> d b e"), C[:, h % 2, :, :]).then_inc(
                    sem(f"C_stored{h % 2}"), 16)
                if h + 2 < H:
                    sp.wait_ge(sem(f"C_stored{h % 2}"), 16 * (h // 2 + 1))
                    load_state(h + 2)
                sp.wait_ge(sem("Cp_ready"), h + 1)
                sp.dma_start(O["C_prompt"][0, 0, h, :, :], Cp[:, h % 2, :]).then_inc(sem(f"Cp_stored{h % 2}"), 16)

        load_mixer("in_a", 3, wi, 0)
        load_mixer("in_m", 4, wi, COL_M, load_pages)
        load_mixer("out", 2, wo, 0, state_traffic)
        load_swiglu(1)
        load_turn(n_turns, range(2), lambda s: [(0, wd[1][s, :, 0:UW])])
        for s in range(2):
            sp.wait_ge(w_loaded[s], 32 * (n_turns + 1))

    @block.gpsimd
    def _(pool):
        def small(dst, src):
            pool.dma_start(dst, src).then_inc(small_loaded, 16)

        rows = lambda name: A[name].rearrange("l (r p) -> (l r) p", p=P)
        for name, r0, n in (("g_ffn1", 0, 16), ("g_mix", 16, 16), ("g_ffn2", 32, 16), ("conv_b", 48, 16)):
            small(vec_rows[r0:r0 + n, 0, :], rows(name))
        small(vec_rows[64:128, 0, :], A["conv_w"].rearrange("l c (r p) -> (l c r) p", p=P))
        small(vec_rows[0:1, 1, :], A["g_q"])
        small(vec_rows[1:2, 1, :], A["g_k"])
        small(vec_rows[2:10, 1, :], A["g_out_a"][0])
        small(vec_rows[10:18, 1, :], A["g_out_m"][0])
        wi_p = A["w_in"][0].rearrange("(k p) n -> p k n", p=P)
        small(w_gates[:, :, 0:H], wi_p[:, :, COL_F_A:COL_F_A + H])
        small(w_gates[:, :, H:2 * H], wi_p[:, :, COL_I_M + H:N_IN])
        small(w_gates[:, :, 2 * H:3 * H], wi_p[:, :, COL_I_M:COL_I_M + H])
        for c, name in enumerate(("b_fox_f", "b_m_f", "b_m_i")):
            small(b_gates[:, c * H:(c + 1) * H], A[name].to_broadcast([P, H]))
        small(pages_sb[:, :], A["page_table"].rearrange("b n -> (b n)").unsqueeze(0))

        nc.gpsimd.memset(ones[:, :], 1.0).then_inc(pool_const, 1)
        nc.gpsimd.memset(ident[:, :], 0.0).then_inc(pool_const, 1)
        pool.wait_ge(pool_const, 2)
        nc.gpsimd.affine_select(out=upper[:, :], in_=ones[:, :], compare_op=ALU.is_ge, fill=0.0, base=0,
                                pattern=[[1, P]], channel_multiplier=-1)
        nc.gpsimd.affine_select(out=lower[:, :], in_=ones[:, :], compare_op=ALU.is_ge, fill=0.0, base=0,
                                pattern=[[-1, P]], channel_multiplier=1)
        nc.gpsimd.affine_select(out=block4[:, :].rearrange("p (b t) -> p b t", t=TS),
                                in_=ones[0:SM, 0:SM].rearrange("p (b t) -> p b t", t=TS), compare_op=ALU.is_ge,
                                fill=0.0, base=0, pattern=[[-TS, NB], [0, TS]], channel_multiplier=1)
        nc.gpsimd.affine_select(out=ident[:, :], in_=ident[:, :], compare_op=ALU.not_equal, fill=1.0, base=0,
                                pattern=[[-1, P]], channel_multiplier=1).then_inc(pool_const, 1)
        pool.wait_ge(pool_const, 3)
        nc.gpsimd.affine_select(out=block4[:, :].rearrange("p (b t) -> p b t", t=TS),
                                in_=block4[:, :].rearrange("p (b t) -> p b t", t=TS), compare_op=ALU.is_ge,
                                fill=0.0, base=TS - 1, pattern=[[TS, NB], [0, TS]],
                                channel_multiplier=-1).then_inc(pool_const, 1)

        def store(dst, src):
            pool.dma_start(dst, src).then_inc(out_stored, 16)

        pool.wait_ge(small_loaded, 16 * 16)
        pool.wait_ge(banks_free, NBANK + G_A * NBANK)
        for p in range(NB * NPG):
            pid = pool.value_load(pages_sb[0:1, p:p + 1], min_val=0, max_val=A["cache_logf"].shape[1] - 1)
            pool.dma_start(lf_past[:, p, :], A["cache_logf"][0][bass.ds(pid, 1), :, :]
                           .rearrange("a s h -> (a s) h")).then_inc(sem("lf_past_loaded"), 16)

        pool.wait_ge(sem("lf_ready"), 1)
        store(O["logf_prompt"][0, 0].rearrange("(t p) h -> p t h", p=P), LF[:, 0:2, 0:H])
        store(O["logf_sample"][0].rearrange("b t h -> (b t) h"), LF[0:SM, 2, 0:H])
        pool.wait_ge(sem("vn_ready"), 6)
        store(O["v_prompt"][0, 0].rearrange("(t p) h d -> p t (h d)", p=P), vn[:, 0:2, :])
        store(O["v_sample"][0].rearrange("b t h d -> (b t) (h d)"), vn[0:SM, 2, :])
        pool.wait_ge(sem("kn_ready"), 6)
        store(O["k_prompt"][0, 0].rearrange("(t p) h d -> p t (h d)", p=P), kn[:, 0:2, :])
        store(O["k_sample"][0].rearrange("b t h d -> (b t) (h d)"), kn[0:SM, 2, :])

        pool.wait_ge(sem("ya_ready"), H + 1)
        pool.wait_ge(out_stored, 6 * 16)
        pool.dma_start(conv_rows[0:24, :], A["state_conv"][0].rearrange("b r c -> (b r) c")).then_inc(sem("state_loaded"), 16)
        pool.dma_start(n_rows[:, 0, :], A["state_n"][0].rearrange("b h d -> (b h) d")).then_inc(sem("state_loaded"), 16)
        pool.dma_start(m0[:, :], A["state_m"][0].rearrange("b h -> h b")).then_inc(sem("state_loaded"), 16)
        pool.wait_ge(sem("conv_rows_ready"), 4)
        store(O["conv_prompt"][0, 0], conv_rows[0:3, :])
        store(O["conv_sample"][0].rearrange("b r c -> (b r) c"), conv_rows[3:27, :])
        store(O["m_prompt"][0].rearrange("b h -> h b"), m_row[:, TP - 1:TP])
        store(O["m_sample"][0].rearrange("b h -> h b"),
              m_row[:, TP:T].rearrange("h (b t) -> h b t", t=TS)[:, :, TS - 1])
        pool.wait_ge(sem("kmn_ready"), 6)
        pool.wait_ge(sem("nat_ready"), 1)
        for t, n in TT:
            k3 = kmn[0:n, t, :].rearrange("p (h d) -> p h d", h=H)
            nc.gpsimd.tensor_tensor(k3, k3, nat[0:n, 3 + t, :].unsqueeze(2).to_broadcast([n, H, HD]),
                                    ALU.mult).then_inc(sem("kw_ready"), 1)
        for h in range(H):
            if h >= 1:
                pool.wait_ge(sem("dC_done"), 2 * h)
            nc.gpsimd.tensor_tensor(v_seq[:, :, :],
                                    vmn[0:SM, 2, h * HD:(h + 1) * HD].unsqueeze(1).to_broadcast([SM, NB, HD]),
                                    block4[:, 0:SM:TS].unsqueeze(2).to_broadcast([SM, NB, HD]),
                                    ALU.mult).then_inc(sem("v_seq_ready"), 1)
            pool.wait_ge(sem(f"C_loaded{h % 2}"), 16 * (h // 2 + 1))
            pool.wait_ge(sem("qC_done"), h + 1)
            w_last = s_all[:, h, 0, :].rearrange("p (b t) -> p b t", t=TS)[:, :, TS - 1]
            nc.gpsimd.tensor_tensor(C[:, h % 2, :, :], C[:, h % 2, :, :],
                                    w_last.unsqueeze(2).to_broadcast([P, NB, HD]),
                                    ALU.mult).then_inc(sem("C_decayed"), 1)
        pool.wait_ge(sem("n_rows_ready"), 2)
        store(O["n_sample"][0].rearrange("b h d -> (b h) d"), n_rows[:, 0, :])
        store(O["n_prompt"][0, 0], n_rows[0:H, 1, :])
        for t, n in TT:
            pool.wait_ge(sem("y_rows_ready"), 2 * (t + 1))
            pool.wait_ge(sem("y_rows_ready_v"), 2 * (t + 1))
            if t < 2:
                store(O["y_prompt"][0, t * P:(t + 1) * P, :], y_rows[:, t, :])
            else:
                store(O["y_sample"].rearrange("b t d -> (b t) d"), y_rows[0:SM, 2, :])
        pool.wait_ge(out_stored, 16 * (6 + 4 + 2 + 3))
        for kind in ("C_stored", "Cp_stored"):
            for b in range(2):
                pool.wait_ge(sem(f"{kind}{b}"), 16 * (H // 2))

    N_FFN = (0, 3)
    SUM_X = {0: 0, 1: 16, 3: 64}
    SUM_QK, SUM_Y = 32, 48
    SILU0 = {"gu0a": 0, "gu0b": 24, "gu0c": 40, "gu1a": 43, "gu1b": 67, "gu1c": 83}
    NGRP = {"a": 6, "b": 4, "c": 1}

    @block.scalar
    def _(act):
        def split_hi(turn, slot):
            act.wait_ge(w_loaded[slot], turn * 32 + 32)
            if not (isinstance(turn, int) and turn == 0):
                act.wait_ge(w_used, turn * 2 + (slot // 2 + 1))
            nc.scalar.copy(w_hi[:, slot, :], w_raw[:, slot, :]).then_inc(w_hi_ready, 1)

        def split_turns(turn, n):
            with act.Fori(1, n) as kt:
                for s in range(SLOTS):
                    split_hi(turn + kt, s)
            split_pair(turn + n, 0)

        def split_pair(turn, s):
            split_hi(turn, s)
            split_hi(turn, s + 1)

        def split_groups(g, n, last=False):
            split_turns(g.turn, n * g.turns)
            if not last:
                split_pair(g.turn + n * g.turns, 2)

        def square(i, src):
            if i >= 2:
                act.wait_ge(sem("sum_done"), i - 1)
            nc.scalar.activation(sq[:, i % 2, :], src, ACT.Square).then_inc(sem("sq_ready"), 1)

        def operand_hi(m, t, dst):
            act.wait_ge(sem("xn_tmp"), 16 * m + t + 1)
            nc.scalar.copy(dst[:, t, :], xt[:, t % 2, :]).then_inc(sem("xn_hi"), 1)

        def sqrt(i, out, src):
            act.wait_ge(sem("mean_ready"), i + 1)
            nc.scalar.activation(out, src, ACT.Sqrt).then_inc(sem("sqrt_ready"), 1)

        def norm(n, dst_hi):
            for t in range(KD):
                x_final(act, min(n, 2), t)
                square(SUM_X[n] + t, X[:, t, :])
            sqrt((0, 1, None, 4)[n], rs[:, 1, :], rs[:, 0, :])
            for t in range(KD):
                operand_hi(n, t, dst_hi)

        def swiglu(n):
            for part in "abc":
                g = groups[f"gu{n}{part}"]

                def group(i):
                    turn0 = i * g.turns + g.turn
                    split_turns(turn0, g.turns)
                    act.wait_ge(banks_free, (i + g.index) * NBANK + NBANK)
                    for j in range(len(g.tiles) // 2):
                        wait_bank(act, g, turn0, i + g.index, 2 * j)
                        nc.scalar.activation(mem[n]["silu"][:, j, :], ps[:, 2 * j, 0:T],
                                             ACT.Silu).then_inc(sem("silu_ready"), 1)
                    split_pair(turn0 + g.turns, 2)

                if part != "c":
                    with act.Fori(0, NGRP[part]) as i:
                        group(i)
                    if part == "a":
                        split_groups(groups[f"down{n}a"], 2)
                else:
                    group(0)
            split_groups(groups[f"down{n}b"], 2, last=n == 1)

        for t in range(2):
            act.dma_start(x_rows[:, t, :], A["x_prompt"][0, t * P:(t + 1) * P, :]).then_inc(sem("x_loaded"), 16)
        act.dma_start(x_rows[0:SM, 2, :], A["x_sample"].rearrange("b t d -> (b t) d")).then_inc(sem("x_loaded"), 16)
        split_pair(0, 0)
        split_pair(0, 2)
        norm(0, mem[0]["x"][0])
        swiglu(0)
        norm(1, xm_hi)
        split_groups(groups["in_a"], 3)

        def natural(dst, made, name):
            for i in range(6):
                t, half, n = i // 2, i % 2, TT[i // 2][1]
                act.wait_ge(sem(made), i + 1)
                nc.scalar.copy(dst[0:n, t, half * 512:half * 512 + 512], ps[0:n, 2 + i, :]).then_inc(sem(name), 1)

        act.wait_ge(sem("abs_ready"), 1)
        nc.scalar.activation(lt[:, 1, :, :], lt[:, 0, :, :], ACT.Exp, scale=-1.0).then_inc(sem("abs_exp"), 1)
        natural(vn, "vT_done", "vn_ready")
        for j in range(2 * H):
            act.wait_ge(banks_free, NBANK + G_M * NBANK)
            square(SUM_QK + j, (qa if j < H else ka)[:, j % H, :])
        sqrt(2, root[:, :, :], rs[0:H, :, :])
        natural(kn, "kT_done", "kn_ready")

        def p_exp(h):
            act.wait_ge(sem("s_masked"), h + 1)
            b = h % 2
            for q, c0, c1 in ((0, 0, P), (1, P, 384)):
                nc.scalar.activation(Sm[:, b, c0:c1], Sm[:, b, c0:c1], ACT.Exp, bias=nmx[:, b, q:q + 1],
                                     accum_out=den[:, b, q:q + 1]).then_inc(sem("p_exp"), 1)

        def pt_copy(h):
            act.wait_ge(sem("pt_done"), h + 1)
            if h >= 2:
                act.wait_ge(sem("o_done"), h - 1)
            nc.scalar.copy(PT[:, h % 2, :], ps[:, 2 + h % 2, 0:384]).then_inc(sem("pt_ready"), 1)

        def keys_copy(p):
            act.wait_ge(sem("kpT_done"), 2 * p + 1)
            if p >= 2:
                act.wait_ge(sem("sT_done"), p - 1)
            nc.scalar.copy(kpT[:, p % 2, 0:512], ps[:, 5, :]).then_inc(sem("kpT_lo"), 1)

        for h in range(H):
            p_exp(h)
            keys_copy(2 * h)
            pt_copy(h)
            keys_copy(2 * h + 1)
        for g2 in range(2):
            act.wait_ge(sem("sample_max"), g2 + 1)
            nc.scalar.activation(Ps[:, g2, :], ps[:, 4 + g2, 0:T], ACT.Exp, bias=nmx[:, 0, g2:g2 + 1],
                                 accum_out=den[:, 0, g2:g2 + 1]).then_inc(sem("sample_exp"), 1)
        act.wait_ge(sem("sample_pT"), 1)
        nc.scalar.copy(PTs[:, :], ps[:, 0, :]).then_inc(sem("sample_pT_ready"), 1)
        nc.scalar.copy(PTn[:, :], ps[0:SM, 1, 0:256]).then_inc(sem("sample_pT_ready"), 1)

        act.wait_ge(sem("rows_sum"), 4)
        nc.scalar.activation(em_row[:, :], m_row[:, :], ACT.Exp, scale=-1.0).then_inc(sem("rows_exp"), 1)
        nc.scalar.activation(ws_row[:, 0:TP], r_row[:, 0:TP], ACT.Exp, bias=nR_row[:, TP - 1:TP]).then_inc(sem("rows_exp"), 1)
        nc.scalar.activation(ws_row[:, TP:T], ws_row[:, TP:T], ACT.Exp).then_inc(sem("rows_exp"), 1)
        nc.scalar.activation(s_rows[:, 0, :], s_rows[:, 0, :], ACT.Exp).then_inc(sem("rows_exp"), 1)

        def conv_silu(j):
            act.wait_ge(sem("conv_done"), j + 1)
            act.wait_ge(sem("conv_last"), 2 * (1 + j // H))
            cb = vecs[:, V_CB + j:V_CB + j + 1]
            nc.scalar.activation(ext[:, j, 0:TP], conv_acc[:, j % 2, 0:TP], ACT.Silu, bias=cb).then_inc(sem("conv_used"), 1)
            nc.scalar.activation(ext[:, j, TP:T].rearrange("p (b t) -> p b t", t=TS),
                                 conv_acc[:, j % 2, EXT:EXTW].rearrange("p (b t) -> p b t", t=EXTS)[:, :, 0:TS],
                                 ACT.Silu, bias=cb).then_inc(sem("conv_used"), 1)

        g = groups["in_m"]
        split_groups(g, 2)
        for t in range(2 * g.turns):
            split_pair(g.turn + 2 * g.turns + (t + 1), 0)
            split_pair(g.turn + 2 * g.turns + (t + 1), 2)
            conv_silu(2 * t)
            conv_silu(2 * t + 1)
        act.wait_ge(banks_free, NBANK + G_O * NBANK)
        nc.scalar.activation(om[:, :, :], om[:, :, :], ACT.Sigmoid).then_inc(sem("o_sigmoid"), 1)
        for i in range(6):
            t, half, n = i // 2, i % 2, TT[i // 2][1]
            act.wait_ge(sem("vmT_done"), i + 1)
            nc.scalar.copy(vmn[0:n, t, half * 512:half * 512 + 512], ps[0:n, i, :]).then_inc(sem("vmn_ready"), 1)
        for i in range(6):
            t, half, n = i // 2, i % 2, TT[i // 2][1]
            act.wait_ge(sem("kmT_done"), i + 1)
            nc.scalar.copy(kmn[0:n, t, half * 512:half * 512 + 512], ps[0:n, i, :]).then_inc(sem("kmn_ready"), 1)
        for b in range(2):
            act.wait_ge(sem("s_all_done"), b + 1)
            nc.scalar.copy(s_all[:, 4 * b:4 * b + 4, :, :], ps[:, 6 + b, 0:384].rearrange(
                "p (h r s) -> p h r s", h=4, r=3)).then_inc(sem("s_all_ready"), 1)
        act.wait_ge(sem("ws_logits"), 1)
        nc.scalar.activation(Ws[:, :, :], Ws[:, :, :], ACT.Exp).then_inc(sem("ws_exp"), 1)
        for h in range(H):
            act.wait_ge(sem("e_logits"), h + 1)
            for t, c0, c1 in ((0, 0, TP), (1, TP, 384)):
                nc.scalar.activation(Wt[:, h % 2, c0:c1], Wt[:, h % 2, c0:c1], ACT.Exp,
                                     bias=nat[:, t, h:h + 1]).then_inc(sem("e_exp"), 1)
            act.wait_ge(sem("em_done"), h + 1)
            if h >= 2:
                act.wait_ge(sem("h_ready"), h - 1)
            nc.scalar.copy(em_all[:, h % 2, :], ps[:, 6, 0:TP]).then_inc(sem("em_ready"), 1)
            act.wait_ge(sem("Cp_done"), h + 1)
            if h >= 2:
                act.wait_ge(sem(f"Cp_stored{h % 2}"), 16 * (h // 2))
            nc.scalar.copy(Cp[:, h % 2, :], ps[:, 7, 0:HD]).then_inc(sem("Cp_ready"), 1)
        for j in range(KD):
            act.wait_ge(sem("h_ready"), H + 1)
            square(SUM_Y + j, (ya if j < H else vm)[:, j % H, :])
        sqrt(3, root[:, :, :], rs[0:H, :, :])
        for t in range(KD):
            operand_hi(2, t, y_hi)
        split_groups(groups["out"], 2)
        norm(3, mem[1]["x"][0])
        act.wait_ge(out_stored, 12 * 16)
        swiglu(1)
        for i in range(12):
            if i % 2 == 0:
                act.wait_ge(sem("y_rows_done"), i + 1)
                t, n = TT[i // 4]
                nc.scalar.copy(y_rows[0:n, t, (i % 4) * 512:(i % 4 + 1) * 512], ps[0:n, i % 4, :]).then_inc(sem("y_rows_ready"), 1)

    @block.vector
    def _(dve):
        chain = [0]

        def link(ins):
            chain[0] += 1
            ins.then_inc(sem("dve_chain"), 1)
            dve.wait_ge(sem("dve_chain"), chain[0])

        def split_lo(turn, slot):
            dve.wait_ge(w_hi_ready, turn * SLOTS + (slot + 1))
            nc.vector.tensor_tensor(w_lo[:, slot, :], w_raw[:, slot, :], w_hi[:, slot, :].bitcast(F32),
                                    ALU.subtract).then_inc(w_lo_ready, 1)

        def split_turns(turn, n):
            with dve.Fori(1, n) as kt:
                for s in range(SLOTS):
                    split_lo(turn + kt, s)
            split_pair(turn + n, 0)

        def split_pair(turn, s):
            split_lo(turn, s)
            split_lo(turn, s + 1)

        def rsqrt_mean(i, y, v, tmp, src, width):
            nc.vector.tensor_scalar(v, src, 1.0 / width, EPS, ALU.mult, ALU.add).then_inc(sem("mean_ready"), 1)
            dve.wait_ge(sem("sqrt_ready"), i + 1)
            link(nc.vector.reciprocal(y, y))
            link(nc.vector.tensor_tensor(tmp, y, y, ALU.mult))
            link(nc.vector.scalar_tensor_tensor(tmp, v, -0.5, tmp, ALU.mult, ALU.mult))
            return nc.vector.scalar_tensor_tensor(y, tmp, 1.5, y, ALU.add, ALU.mult)

        def head_norm(j, x, gain):
            dve.wait_ge(sem("spread_done"), j + 1)
            bank = j % 2 + (0 if j < 2 * H else 1)
            return lambda out: nc.vector.scalar_tensor_tensor(out, x, gain, ps[:, bank, 0:T], ALU.mult, ALU.mult)

        def operand_lo(m, t, dst_hi, dst_lo):
            dve.wait_ge(sem("xn_hi"), 16 * m + t + 1)
            nc.vector.tensor_tensor(dst_lo[:, t, :], xt[:, t % 2, :], dst_hi[:, t, :].bitcast(F32),
                                    ALU.subtract).then_inc(sem("xn_ready"), 1)

        def norm(n, gain, dst_hi, dst_lo):
            dve.wait_ge(sem("sum_done"), SUM_X[n] + KD)
            link(rsqrt_mean((0, 1, None, 4)[n], rs[:, 1, :], rs[:, 0, :], xt[:, 0, :], ps[:, 0, 0:T], D))
            for t in range(KD + 1):
                if t < KD:
                    if t >= 2:
                        dve.wait_ge(sem("xn_ready"), 16 * n + t - 1)
                    nc.vector.scalar_tensor_tensor(xt[:, t % 2, :], X[:, t, :], vecs[:, gain + t:gain + t + 1],
                                                   rs[:, 1, :], ALU.mult, ALU.mult).then_inc(sem("xn_tmp"), 1)
                if t >= 1:
                    operand_lo(n, t - 1, dst_hi, dst_lo)

        def swiglu(n):
            hid_hi, hid_lo = mem[n]["hid"]
            silu, prod = mem[n]["silu"], mem[n]["prod"]

            def down(name, last=False):
                g = groups[name]
                for half in range(2):
                    split_turns(half * g.turns + g.turn, g.turns)
                    residual(g, half, 0.5)
                    if not (last and half == 1):
                        split_pair(half * g.turns + (g.turn + g.turns), 2)

            for part in "abc":
                g = groups[f"gu{n}{part}"]
                s0, f0 = SILU0[f"gu{n}{part}"], 16 if part == "c" else 0

                def group(i):
                    turn0, nj = i * g.turns + g.turn, len(g.tiles) // 2
                    split_turns(turn0, g.turns)
                    for j in range(nj):
                        dve.wait_ge(sem("silu_ready"), i * 4 + (s0 + j + 1))
                        wait_bank(dve, g, turn0, i + g.index, 2 * j + 1)
                        freed = 2 if j < nj - 1 else NBANK - 2 * (nj - 1)
                        nc.vector.tensor_tensor(prod[:, j, :], silu[:, j, :], ps[:, 2 * j + 1, 0:T],
                                                ALU.mult).then_inc(banks_free, freed)
                    split_pair(turn0 + g.turns, 2)
                    dve.wait_ge(banks_free, (i + g.index) * NBANK + 2 * NBANK)
                    for j in range(nj):
                        nc.vector.tensor_scalar(hid_hi[:, i * 4 + (f0 + j), :], prod[:, j, :], 1.0, None,
                                                ALU.mult).then_inc(sem("hid_hi_ready"), 1)
                    for j in range(nj):
                        dve.wait_ge(sem("hid_hi_ready"), i * 4 + (s0 + j + 1))
                        nc.vector.tensor_tensor(hid_lo[:, i * 4 + (f0 + j), :], prod[:, j, :],
                                                hid_hi[:, i * 4 + (f0 + j), :].bitcast(F32),
                                                ALU.subtract).then_inc(sem("hid_ready"), 1)
                    dve.wait_ge(sem("hid_ready"), i * 4 + (s0 + nj))

                if part != "c":
                    with dve.Fori(0, NGRP[part]) as i:
                        group(i)
                    if part == "a":
                        down(f"down{n}a")
                else:
                    group(0)
            down(f"down{n}b", last=n == 1)

        def residual(g, half, scale):
            for b in range(NBANK):
                wait_bank(dve, g, half * g.turns + g.turn, half + g.index, b)
                x = X[:, half * NBANK + b, :]
                nc.vector.scalar_tensor_tensor(x, ps[:, b, 0:T], scale, x, ALU.mult, ALU.add).then_inc(banks_free, 1)

        nc.vector.memset(neg_ones[:, :], -1.0)
        nc.vector.memset(mask_q[:, P:2 * P], 0.0)
        nc.vector.memset(mask_t[:, P:2 * P], 0.0)
        nc.vector.memset(G[:, :, :], 0.0)
        dve.wait_ge(pool_const, 4)
        nc.vector.tensor_scalar(neg_upper[:, :], upper[:, :], -1.0, None, ALU.mult)
        for c in (0, 2 * P):
            nc.vector.tensor_scalar(mask_q[:, c:c + P], lower[:, :], -1.0, BIG, ALU.add, ALU.mult)
            nc.vector.tensor_scalar(mask_t[:, c:c + P], upper[:, :], -1.0, BIG, ALU.add, ALU.mult)
        nc.vector.tensor_tensor(upper4[:, :], upper[0:SM, 0:SM], block4[:, :], ALU.mult)
        link(nc.vector.tensor_tensor(lower4[:, :], lower[0:SM, 0:SM], block4[:, :], ALU.mult))
        nc.vector.tensor_scalar(neg_upper4[:, :], upper4[:, :], -1.0, None, ALU.mult)
        nc.vector.tensor_scalar(mask4_q[:, :], lower4[:, :], -1.0, BIG, ALU.add, ALU.mult)
        nc.vector.tensor_scalar(mask4_t[:, :], upper4[:, :], -1.0, BIG, ALU.add, ALU.mult)
        nc.vector.tensor_copy(spread[:, :].rearrange("p (b h q) -> p b h q", b=NB, h=H),
                              ident[0:SM, 0:SM].rearrange("p (b q) -> p b q", q=TS).unsqueeze(2)
                              .to_broadcast([SM, NB, H, TS]))
        nc.vector.memset(one_hot[:, :, :], 0.0).then_inc(sem("one_hot_zero"), 1)
        dve.wait_ge(sem("one_hot_zero"), 1)
        for h in range(H):
            nc.vector.memset(one_hot[:, h, h:h + 1], 1.0)
        nc.vector.tensor_copy(sel[:, :, :], ident[0:H, 0:H].unsqueeze(2).to_broadcast([H, H, P])).then_inc(const_ready, 1)
        split_pair(0, 0)
        for t in range(KD):
            dve.wait_ge(sem("xT_done"), t + 1)
            nc.vector.tensor_copy(X[:, t, :], ps[:, t % 4, 0:T]).then_inc(sem("xT_copied"), 1)
        dve.wait_ge(sem("vecT_done"), 1)
        nc.vector.tensor_copy(vecs[:, :], ps[:, 7, 0:146]).then_inc(banks_free, NBANK)
        dve.wait_ge(banks_free, NBANK)
        nc.vector.tensor_scalar(gq_scaled[:, :], vecs[:, V_GQ:V_GQ + 1], SCALE, None, ALU.mult).then_inc(sem("vecs_ready"), 1)
        split_pair(0, 2)

        norm(0, V_FFN[0], *mem[0]["x"])
        swiglu(0)
        norm(1, V_MIX, xm_hi, xm_lo)

        link(nc.vector.tensor_copy(w_gates_hi[:, :, :], w_gates[:, :, :]))
        nc.vector.tensor_tensor(w_gates_lo[:, :, :], w_gates[:, :, :], w_gates_hi[:, :, :].bitcast(F32),
                                ALU.subtract).then_inc(sem("w_gates_split"), 1)

        g = groups["in_a"]
        for i, dst in enumerate((qa, ka, ya)):
            split_turns(g.turn + i * g.turns, g.turns)
            for b in range(NBANK):
                wait_bank(dve, g, g.turn + i * g.turns, g.index + i, b)
                nc.vector.tensor_copy(dst[:, b, :], ps[:, b, 0:T]).then_inc(banks_free, 1)
            split_pair(g.turn + (i + 1) * g.turns, 2)
        dve.wait_ge(sem("gates_done"), 1)
        nc.vector.tensor_copy(gates_row[:, :], ps[0:3 * H, 0, 0:T]).then_inc(sem("gates_row_ready"), 1)
        dve.wait_ge(sem("gates_t_done"), 1)
        nc.vector.tensor_tensor(G[:, 0:2, :], ps[:, 1, 0:48].rearrange("p (t g) -> p t g", t=2),
                                b_gates[:, :].unsqueeze(1).to_broadcast([P, 2, 3 * H]), ALU.add)
        link(nc.vector.tensor_tensor(G[0:SM, 2, :], ps[0:SM, 1, 48:72], b_gates[0:SM, :], ALU.add))
        gf = G[:, :, 0:2 * H]
        nc.vector.scalar_tensor_tensor(lt[:, 0, :, :], gf, -1.0, gf, ALU.mult, ALU.max).then_inc(sem("abs_ready"), 1)
        dve.wait_ge(sem("abs_exp"), 1)
        e, a, z = lt[:, 1, :, :], lt[:, 0, :, :], lt[:, 2, :, :]
        link(nc.vector.tensor_scalar(a, e, 2.0, None, ALU.add))
        link(nc.vector.reciprocal(a, a))
        link(nc.vector.tensor_tensor(e, e, a, ALU.mult))
        link(nc.vector.tensor_tensor(z, e, e, ALU.mult))
        link(nc.vector.tensor_scalar(a, z, 1.0 / 17, None, ALU.mult))
        for c in range(15, 1, -2):
            link(nc.vector.scalar_tensor_tensor(a, a, 1.0 / c, z, ALU.add, ALU.mult))
        link(nc.vector.scalar_tensor_tensor(e, a, 1.0, e, ALU.add, ALU.mult))
        link(nc.vector.tensor_scalar(z, gf, 0.0, None, ALU.min))
        nc.vector.scalar_tensor_tensor(LF[:, :, :], e, -2.0, z, ALU.mult, ALU.add).then_inc(sem("lf_ready"), 1)
        dve.wait_ge(sem("sum_done"), SUM_QK + 2 * H)
        rsqrt_mean(2, root[:, :, :], rs[0:H, :, :], xt[0:H, :, :], ps[0:H, 0:2, 0:T], HD).then_inc(sem("root_ready"), 1)
        for j in range(2 * H):
            x = (qa if j < H else ka)[:, j % H, :]
            gain = gq_scaled[:, :] if j < H else vecs[:, V_GK:V_GK + 1]
            head_norm(j, x, gain)(x).then_inc(sem("qk_normed"), 1)
        dve.wait_ge(sem("c_done"), 1)
        nc.vector.tensor_copy(neg_c[:, :], ps[0:H, 1, 0:TP]).then_inc(sem("neg_c_ready"), 1)

        def s_mask(h):
            dve.wait_ge(sem("s_done"), h + 1)
            b = h % 2
            if h >= 2:
                dve.wait_ge(sem("pt_done"), h - 1)
            for q, c0, c1 in ((0, 0, P), (1, P, 384)):
                link(nc.vector.tensor_tensor(Sm[:, b, c0:c1], ps[:, b, c0:c1], mask_q[:, c0:c1], ALU.add))
                link(nc.vector.tensor_reduce(mx[:, b, q:q + 1], Sm[:, b, c0:c1], AX.X, ALU.max))
            nc.vector.tensor_scalar(nmx[:, b, :], mx[:, b, :], -1.0, None, ALU.mult).then_inc(sem("s_masked"), 1)

        def p_norm(h):
            b = h % 2
            dve.wait_ge(sem("p_exp"), 2 * (h + 1))
            link(nc.vector.reciprocal(rden[:, b, :], den[:, b, :]))
            nc.vector.tensor_scalar(Sm[:, b, 0:P], Sm[:, b, 0:P], rden[:, b, 0:1], None, ALU.mult)
            nc.vector.tensor_scalar(Sm[:, b, P:384], Sm[:, b, P:384], rden[:, b, 1:2], None,
                                    ALU.mult).then_inc(sem("p_ready"), 1)

        def o_copy(h):
            dve.wait_ge(sem("o_done"), h + 1)
            nc.vector.tensor_copy(ya[:, h, 0:TP], ps[:, 4, 0:TP]).then_inc(sem("ya_ready"), 1)

        def keys_copy(p):
            dve.wait_ge(sem("kpT_done"), 2 * p + 2)
            if p >= 2:
                dve.wait_ge(sem("sT_done"), p - 1)
            nc.vector.tensor_copy(kpT[:, p % 2, 512:1024], ps[:, 7, :]).then_inc(sem("kpT_hi"), 1)

        s_mask(0)
        for h in range(H):
            p_norm(h)
            keys_copy(2 * h)
            if h + 1 < H:
                s_mask(h + 1)
            keys_copy(2 * h + 1)
            if h >= 1:
                o_copy(h - 1)
        o_copy(H - 1)
        dve.wait_ge(sem("lf_past_loaded"), 16 * NB * NPG)
        for c in range(NPG):
            for b in range(NB):
                nc.vector.tensor_scalar(nl_past[:, c, b * SM:(b + 1) * SM].rearrange("p (h q) -> p h q", h=H),
                                        lf_past[:, b * NPG + c, :].unsqueeze(2).to_broadcast([P, H, TS]),
                                        -1.0, None, ALU.mult)
        for b in range(NB):
            last = nc.vector.tensor_scalar(nl_new[:, b * SM:(b + 1) * SM].rearrange("p (h q) -> p h q", h=H),
                                           LF[0:SM, 2, 0:H].unsqueeze(2).to_broadcast([SM, H, TS]),
                                           -1.0, None, ALU.mult)
        last.then_inc(sem("nl_ready"), 1)
        dve.wait_ge(sem("sT_done"), NB * NPG + 1)
        nc.vector.tensor_copy(STs[:, :], ps[:, 6, :])
        nc.vector.tensor_copy(STn[:, :], ps[0:SM, 7, 0:256]).then_inc(sem("sT_ready"), 1)
        for g2 in range(2):
            dve.wait_ge(sem("sample_logits"), g2 + 1)
            link(nc.vector.tensor_reduce(mx[:, 0, g2:g2 + 1], ps[:, 4 + g2, 0:T], AX.X, ALU.max))
            nc.vector.tensor_scalar(nmx[:, 0, g2:g2 + 1], mx[:, 0, g2:g2 + 1], -1.0, None,
                                    ALU.mult).then_inc(sem("sample_max"), 1)
        for g2 in range(2):
            dve.wait_ge(sem("sample_exp"), g2 + 1)
            link(nc.vector.reciprocal(rden[:, 0, g2:g2 + 1], den[:, 0, g2:g2 + 1]))
            nc.vector.tensor_scalar(Ps[:, g2, :], Ps[:, g2, :], rden[:, 0, g2:g2 + 1], None,
                                    ALU.mult).then_inc(sem("sample_p"), 1)
        dve.wait_ge(sem("sample_pv"), NB * NPG)
        nc.vector.tensor_copy(ya[:, :, TP:T], ps[:, 2, 0:256].rearrange("p (h s) -> p h s", h=H)).then_inc(
            sem("ya_ready"), 1)

        dve.wait_ge(out_stored, 6 * 16)
        dve.wait_ge(sem("rows_done"), 2)
        nc.vector.memset(ext[:, :, 0:CW - 1], 0.0).then_inc(sem("ext_edges"), 1)
        nc.vector.tensor_copy(b_row[:, :], ps[0:H, 4, 0:T])
        link(nc.vector.tensor_copy(r_row[:, :], ps[0:H, 3, 0:T]))
        nc.vector.tensor_tensor_scan(R_row[:, 0:TP], r_row[:, 0:TP], r_row[:, 0:TP], 0.0, ALU.max, ALU.max)
        r_s, R_s = (x[:, TP:T].rearrange("h (b t) -> h b t", t=TS) for x in (r_row, R_row))
        dve.wait_ge(sem("state_loaded"), 3 * 16)
        for t in range(TS):
            link(nc.vector.tensor_tensor(R_s[:, :, t], r_s[:, :, t], m0[:, :] if t == 0 else R_s[:, :, t - 1], ALU.max))
        nc.vector.tensor_tensor(m_row[:, :], b_row[:, :], R_row[:, :], ALU.add).then_inc(sem("rows_sum"), 1)
        nc.vector.tensor_scalar(nR_row[:, :], R_row[:, :], -1.0, None, ALU.mult).then_inc(sem("rows_sum"), 1)
        nc.vector.tensor_tensor(ws_row[:, TP:T].rearrange("h (b t) -> h b t", t=TS), r_s,
                                R_s[:, :, TS - 1].unsqueeze(2).to_broadcast([H, NB, TS]),
                                ALU.subtract).then_inc(sem("rows_sum"), 1)
        nc.vector.tensor_tensor(s_rows[:, 0, :].rearrange("h (b t) -> h b t", t=TS),
                                m0[:, :].unsqueeze(2).to_broadcast([H, NB, TS]), R_s,
                                ALU.subtract).then_inc(sem("rows_sum"), 1)
        dve.wait_ge(sem("rows_exp"), 4)
        nc.vector.tensor_copy(s_rows[:, 1, :], nR_row[:, TP:T])
        nc.vector.tensor_copy(s_rows[:, 2, :], em_row[:, TP:T]).then_inc(sem("s_rows_ready"), 1)
        dve.wait_ge(sem("edges_done"), 2)
        nc.vector.tensor_copy(n0T[:, :], ps[:, 0, 0:NB * H])
        nc.vector.tensor_copy(
            ext[:, :, EXT:EXTW].rearrange("p j (b r) -> p j b r", r=EXTS)[:, :, :, 0:CW - 1],
            ps[:, 5, 0:384].rearrange("p (j b r) -> p j b r", j=2 * H, b=NB)).then_inc(sem("ext_edges"), 1)

        def conv(j):
            if j >= 2:
                dve.wait_ge(sem("conv_used"), 2 * (j - 1))
            n = EXTW - CW + 1
            for c in range(CW):
                w, src, acc = vecs[:, V_CW + c * 16 + j:V_CW + c * 16 + j + 1], ext[:, j, c:c + n], conv_acc[:, j % 2, 0:n]
                if c == 0:
                    link(nc.vector.tensor_scalar(acc, src, w, None, ALU.mult))
                elif c < CW - 1:
                    link(nc.vector.scalar_tensor_tensor(acc, src, w, acc, ALU.mult, ALU.add))
                else:
                    nc.vector.scalar_tensor_tensor(acc, src, w, acc, ALU.mult, ALU.add).then_inc(sem("conv_done"), 1)

        g = groups["in_m"]
        for i in range(4):
            if i < 2:
                split_turns(g.turn + i * g.turns, g.turns)
            else:
                for t in range(g.turns):
                    split_pair(g.turn + i * g.turns + (t + 1), 0)
                    if t < g.turns - 1:
                        split_pair(g.turn + i * g.turns + (t + 1), 2)
                    conv((i - 2) * H + 2 * t)
                    conv((i - 2) * H + 2 * t + 1)
            for b in range(NBANK):
                wait_bank(dve, g, g.turn + i * g.turns, g.index + i, b)
                if i < 2:
                    j = i * H + b
                    nc.vector.tensor_copy(ext[:, j, CW - 1:EXT], ps[:, b, 0:TP])
                    nc.vector.tensor_copy(
                        ext[:, j, EXT:EXTW].rearrange("p (b r) -> p b r", r=EXTS)[:, :, CW - 1:EXTS],
                        ps[:, b, TP:T].rearrange("p (b t) -> p b t", t=TS)).then_inc(banks_free, 1)
                else:
                    nc.vector.tensor_copy((vm if i == 2 else om)[:, b, :], ps[:, b, 0:T]).then_inc(banks_free, 1)
            split_pair(g.turn + (i + 1) * g.turns, 2)
            if i < 2:
                dve.wait_ge(banks_free, NBANK + (g.index + i + 1) * NBANK)
                x = ext[:, i * H:(i + 1) * H, :]
                nc.vector.tensor_copy(conv_last[:, i * H:(i + 1) * H, 0:3], x[:, :, EXT - 3:EXT]).then_inc(sem("conv_last"), 1)
                nc.vector.tensor_copy(conv_last[:, i * H:(i + 1) * H, 3:27].rearrange("p j (b r) -> p j b r", r=3),
                                      x[:, :, EXT:EXTW].rearrange("p j (b r) -> p j b r", r=EXTS)[:, :, :, TS:EXTS]
                                      ).then_inc(sem("conv_last"), 1)
        dve.wait_ge(sem("conv_used"), 4 * H)
        nc.vector.tensor_scalar(ext[:, H:2 * H, 0:T], ext[:, H:2 * H, 0:T], SCALE, None, ALU.mult).then_inc(sem("km_ready"), 1)
        for b in range(4):
            dve.wait_ge(sem("conv_rows_done"), b + 1)
            nc.vector.tensor_copy(conv_rows[:, b * 512:(b + 1) * 512], ps[0:27, 2 + b, :]).then_inc(sem("conv_rows_ready"), 1)
        dve.wait_ge(sem("nat_done"), 1)
        nc.vector.tensor_copy(nat[:, :, :], ps[:, 1, 0:48].rearrange("p (a h) -> p a h", h=H)).then_inc(sem("nat_ready"), 1)
        dve.wait_ge(sem("s_all_ready"), 2)
        link(nc.vector.tensor_tensor(Ws[:, :, :], s_all[0:SM, :, 1, :], mask4_t[:, :].unsqueeze(1).to_broadcast([SM, H, SM]), ALU.add))
        nc.vector.tensor_tensor(Ws[:, :, :], Ws[:, :, :], nat[0:SM, 2, :].unsqueeze(2).to_broadcast([SM, H, SM]),
                                ALU.add).then_inc(sem("ws_logits"), 1)
        link(nc.vector.tensor_tensor(qw[:, :, :], ext[:, 0:H, TP:T], s_all[:, :, 0, :], ALU.mult))
        nc.vector.tensor_tensor(qn[:, :, :].rearrange("p h (b t) -> p h b t", t=TS),
                                qw[:, :, :].rearrange("p h (b t) -> p h b t", t=TS),
                                n0T[:, :].rearrange("p (b h) -> p h b", h=H).unsqueeze(3).to_broadcast([P, H, NB, TS]),
                                ALU.mult).then_inc(sem("qn_ready"), 1)
        dve.wait_ge(sem("ws_exp"), 1)
        dve.wait_ge(sem("ws_scores"), 1)
        nc.vector.tensor_tensor(Ws[:, :, :], Ws[:, :, :], ps[0:SM, 0, 0:256].rearrange("p (h s) -> p h s", h=H),
                                ALU.mult).then_inc(sem("ws_ready"), 1)
        for h in range(H):
            b = h % 2
            dve.wait_ge(sem("sm_done"), h + 1)
            nc.vector.tensor_tensor(Wt[:, b, :], ps[:, 1, 0:384], mask_t[:, :], ALU.add).then_inc(sem("e_logits"), 1)
            dve.wait_ge(sem("e_exp"), 2 * (h + 1))
            nc.vector.tensor_tensor(Wt[:, b, :], Wt[:, b, :], ps[:, 0, 0:384], ALU.mult).then_inc(sem("w_ready"), 1)
            dve.wait_ge(sem("num_done"), h + 1)
            dve.wait_ge(sem("em_ready"), h + 1)
            link(nc.vector.scalar_tensor_tensor(dn[:, b, :], ps[:, 2, TP:512], -1.0, em_all[:, b, :], ALU.mult, ALU.max))
            link(nc.vector.tensor_tensor(dn[:, b, :], ps[:, 2, TP:512], dn[:, b, :], ALU.max))
            link(nc.vector.reciprocal(dn[:, b, :], dn[:, b, :]))
            nc.vector.tensor_tensor(vm[:, h, 0:TP], ps[:, 2, 0:TP], dn[:, b, :], ALU.mult).then_inc(sem("h_ready"), 1)
            dve.wait_ge(sem("C_decayed"), h + 1)
            dve.wait_ge(sem("dC_done"), 2 * (h + 1))
            for c in range(2):
                x = C[:, b, 4 * c:4 * c + 4, :]
                nc.vector.tensor_tensor(x, x, ps[:, 3 + c, :].rearrange("p (b e) -> p b e", b=4), ALU.add).then_inc(sem("C_new"), 1)
            dve.wait_ge(sem("Cp_ready"), h + 1)
            nc.vector.tensor_copy(n_new[:, 0, h:h + 1], ps[:, 7, HD:HD + 1])
            w_last = s_all[:, h, 0, :].rearrange("p (b t) -> p b t", t=TS)[:, :, TS - 1]
            link(nc.vector.tensor_tensor(n_new[:, 1:1 + NB, h], w_last, n0T[:, h:NB * H:H], ALU.mult))
            nc.vector.tensor_tensor(n_new[:, 1:1 + NB, h], n_new[:, 1:1 + NB, h], ps[:, 7, 256:256 + NB],
                                    ALU.add).then_inc(sem("n_new_ready"), 1)
        dve.wait_ge(sem("qC_done"), H)
        dn_s, den_s = dn[:, 0, :].rearrange("p (h s) -> p h s", h=H), ps[:, 5, 256:512].rearrange("p (h s) -> p h s", h=H)
        link(nc.vector.scalar_tensor_tensor(dn_s, den_s, -1.0, s_all[:, :, 2, :], ALU.mult, ALU.max))
        link(nc.vector.tensor_tensor(dn_s, den_s, dn_s, ALU.max))
        link(nc.vector.reciprocal(dn[:, 0, :], dn[:, 0, :]))
        nc.vector.tensor_tensor(vm[:, :, TP:T], ps[:, 5, 0:256].rearrange("p (h s) -> p h s", h=H),
                                dn[:, 0, :].rearrange("p (h s) -> p h s", h=H), ALU.mult).then_inc(sem("h_ready"), 1)
        dve.wait_ge(sem("nT_done"), 1)
        nc.vector.tensor_copy(n_rows[:, 0, :], ps[0:NB * H, 0, 0:HD]).then_inc(sem("n_rows_ready"), 1)
        nc.vector.tensor_copy(n_rows[0:H, 1, :], ps[0:H, 0, HD:2 * HD]).then_inc(sem("n_rows_ready"), 1)
        for kind in ("C_stored", "Cp_stored"):
            for b in range(2):
                dve.wait_ge(sem(f"{kind}{b}"), 16 * (H // 2))
        dve.wait_ge(sem("o_sigmoid"), 1)
        dve.wait_ge(sem("sum_done"), SUM_Y + 2 * H)
        rsqrt_mean(3, root[:, :, :], rs[0:H, :, :], xt[0:H, :, :], ps[0:H, 1:3, 0:T], HD).then_inc(sem("root_ready"), 1)
        for j in range(KD + 1):
            if j < KD:
                if j >= 2:
                    dve.wait_ge(sem("xn_ready"), 32 + j - 1)
                src = (ya if j < H else vm)[:, j % H, :]
                gain = vecs[:, (V_GA if j < H else V_GM) + j % H:(V_GA if j < H else V_GM) + j % H + 1]
                ins = head_norm(2 * H + j, src, gain)(xt[:, j % 2, :])
                if j >= H:
                    link(ins)
                    ins = nc.vector.tensor_tensor(xt[:, j % 2, :], xt[:, j % 2, :], om[:, j % H, :], ALU.mult)
                ins.then_inc(sem("xn_tmp"), 1)
            if j >= 1:
                operand_lo(2, j - 1, y_hi, y_lo)
        g = groups["out"]
        for half in range(2):
            split_turns(g.turn + half * g.turns, g.turns)
            residual(g, half, 1.0)
            split_pair(g.turn + (half + 1) * g.turns, 2)
        norm(3, V_FFN[1], *mem[1]["x"])
        dve.wait_ge(out_stored, 12 * 16)
        swiglu(1)
        for i in range(12):
            if i % 2 == 1:
                dve.wait_ge(sem("y_rows_done"), i + 1)
                t, n = TT[i // 4]
                nc.vector.tensor_copy(y_rows[0:n, t, (i % 4) * 512:(i % 4 + 1) * 512], ps[0:n, i % 4, :]).then_inc(sem("y_rows_ready_v"), 1)

    @block.tensor
    def _(pe):
        mm, tr = nc.tensor.matmul, nc.tensor.transpose

        def turn_products(g, turn0, gi, kt, x_hi, x_lo, first, last, x_ready):
            for pair in range(2):
                slots = [s for s in (2 * pair, 2 * pair + 1) if not (last and 0 < g.real % SLOTS <= s)]
                pe.wait_ge(w_lo_ready, (turn0 + kt) * SLOTS + (2 * pair + 2))
                pe.wait_ge(x_ready[0], kt * SLOTS + (x_ready[1] + slots[-1] + 1))
                for b, c in enumerate(g.tiles):
                    if first and pair == 0:
                        pe.wait_ge(banks_free, gi * NBANK + (b + 1))
                    out = ps[:, b, 0:T]
                    for s in slots:
                        hi, lo, k = w_hi[:, s, c:c + P], w_lo[:, s, c:c + P], kt * SLOTS + s
                        mm(out, hi, x_hi[:, k, :], start=first and pair == 0 and s == slots[0], stop=False)
                        mm(out, hi, x_lo[:, k, :], start=False, stop=False)
                        ins = mm(out, lo, x_hi[:, k, :], start=False, stop=last and pair == 1 and s == slots[-1])
                    if b == len(g.tiles) - 1:
                        ins.then_inc(w_used, 1)
                    elif last and pair == 1:
                        ins.then_inc(bank_done, 1 if b < len(g.tiles) - 2 else NBANK + 1 - len(g.tiles))

        def group_products(g, i, x_hi, x_lo, x_ready):
            turn0, gi = i * g.turns + g.turn, i + g.index
            turn_products(g, turn0, gi, 0, x_hi, x_lo, True, False, x_ready)
            with pe.Fori(1, g.turns - 1) as kt:
                turn_products(g, turn0, gi, kt, x_hi, x_lo, False, False, x_ready)
            turn_products(g, turn0, gi, g.turns - 1, x_hi, x_lo, False, True, x_ready)

        def groups_products(g, count, x_hi, x_lo, x_ready):
            if count == 1:
                group_products(g, 0, x_hi, x_lo, x_ready)
            else:
                with pe.Fori(0, count) as i:
                    group_products(g, i, x_hi, x_lo, x_ready)

        def sums(i, bank, stop_start):
            pe.wait_ge(sem("sq_ready"), i + 1)
            mm(ps[:, bank, 0:T], ones[:, :], sq[:, i % 2, :], start=stop_start[0],
               stop=stop_start[1]).then_inc(sem("sum_done"), 1)

        def norm_sums(n):
            for t in range(KD):
                sums(SUM_X[n] + t, 0, (t == 0, t == KD - 1))

        def head_sums(i0, bank, used, used0, n):
            for j in range(2 * H):
                pe.wait_ge(sem("sq_ready"), i0 + j + 1)
                mm(ps[0:H, bank + j // H, 0:T], one_hot[:, j % H, :], sq[:, j % 2, :], start=j % H == 0,
                   stop=j % H == H - 1).then_inc(sem("sum_done"), 1)
            pe.wait_ge(sem("root_ready"), n + 1)
            for j in range(2 * H):
                if j >= 2:
                    pe.wait_ge(sem(used), used0 + j - 1)
                mm(ps[:, bank + j % 2, 0:T], sel[:, j % H, :], root[:, j // H, :], start=True,
                   stop=True).then_inc(sem("spread_done"), 1)

        def swiglu(n):
            x, hid = mem[n]["x"], mem[n]["hid"]
            xr, hr = (sem("xn_ready"), 48 * n), sem("hid_ready")
            groups_products(groups[f"gu{n}a"], 6, *x, xr)
            groups_products(groups[f"down{n}a"], 2, *hid, (hr, 43 * n))
            groups_products(groups[f"gu{n}b"], 4, *x, xr)
            groups_products(groups[f"gu{n}c"], 1, *x, xr)
            groups_products(groups[f"down{n}b"], 2, *hid, (hr, 43 * n + CHUNK))

        pe.wait_ge(pool_const, 4)
        pe.wait_ge(sem("x_loaded"), 48)
        for t in range(KD):
            if t >= 4:
                pe.wait_ge(sem("xT_copied"), t - 3)
            for r, n in TT:
                ins = tr(ps[:, t % 4, r * P:r * P + n], x_rows[0:n, r, t * P:(t + 1) * P], ident[0:n, 0:n])
            ins.then_inc(sem("xT_done"), 1)
        pe.wait_ge(small_loaded, 16 * 16)
        tr(ps[:, 7, 0:P], vec_rows[:, 0, :], ident[:, :]).then_inc(w_used, 2)
        tr(ps[:, 7, P:P + 18], vec_rows[0:18, 1, :], ident[0:18, 0:18]).then_inc(sem("vecT_done"), 1)
        pe.wait_ge(sem("xT_copied"), KD)
        norm_sums(0)
        pe.wait_ge(sem("vecs_ready"), 1)
        swiglu(0)
        pe.wait_ge(banks_free, NBANK + (G_A - 1) * NBANK + 1)
        norm_sums(1)
        groups_products(groups["in_a"], 3, xm_hi, xm_lo, (sem("xn_ready"), 16))

        pe.wait_ge(banks_free, NBANK + G_M * NBANK)
        pe.wait_ge(sem("w_gates_split"), 1)
        for k in range(KD):
            gates = ps[0:3 * H, 0, 0:T]
            mm(gates, w_gates_hi[:, k, :], xm_hi[:, k, :], start=k == 0, stop=False)
            mm(gates, w_gates_hi[:, k, :], xm_lo[:, k, :], start=False, stop=False)
            ins = mm(gates, w_gates_lo[:, k, :], xm_hi[:, k, :], start=False, stop=k == KD - 1)
        ins.then_inc(sem("gates_done"), 1)

        def natural(src, bank0, made, read=None):
            for i in range(6):
                (t, n), half = TT[i // 2], i % 2
                if read:
                    pe.wait_ge(sem(read), i + 1)
                for j in range(4):
                    ins = tr(ps[0:n, bank0 + i, j * P:(j + 1) * P], src(4 * half + j, t * P, n), ident[:, :])
                ins.then_inc(sem(made), 1)

        natural(lambda h, c, n: ya[:, h, c:c + n], 2, "vT_done")
        pe.wait_ge(sem("gates_row_ready"), 1)
        for t, n in TT:
            ins = tr(ps[0:n, 1, t * 3 * H:(t + 1) * 3 * H], gates_row[:, t * P:t * P + n], ident[0:3 * H, 0:3 * H])
        ins.then_inc(sem("gates_t_done"), 1)
        pe.wait_ge(sem("abs_ready"), 1)
        head_sums(SUM_QK, 0, "qk_normed", 0, 0)
        pe.wait_ge(sem("qk_normed"), 2 * H)
        natural(lambda h, c, n: ka[:, h, c:c + n], 2, "kT_done", "vn_ready")
        pe.wait_ge(sem("lf_ready"), 1)
        lf = lambda t, kind, n=P: LF[0:n, t, kind * H:(kind + 1) * H]
        mm(ps[0:H, 1, 0:P], lf(0, 0), neg_upper[:, :], start=True, stop=True)
        mm(ps[0:H, 1, P:TP], lf(0, 0), neg_ones[:, :], start=True, stop=False)
        mm(ps[0:H, 1, P:TP], lf(1, 0), neg_upper[:, :], start=False, stop=True).then_inc(sem("c_done"), 1)
        pe.wait_ge(sem("neg_c_ready"), 1)
        pe.wait_ge(sem("kn_ready"), 6)

        def scores(h):
            if h >= 2:
                pe.wait_ge(sem("s_masked"), h - 1)
            for q, c0, c1 in ((0, 0, P), (1, P, 384)):
                out, n = ps[:, h % 2, c0:c1], c1 - c0
                mm(out, qa[:, h, q * P:(q + 1) * P], ka[:, h, 0:n], start=True, stop=False)
                ins = mm(out, sel[:, h, :], neg_c[:, 0:n], start=False, stop=True)
            ins.then_inc(sem("s_done"), 1)

        def probs_t(h):
            pe.wait_ge(sem("p_ready"), h + 1)
            if h >= 2:
                pe.wait_ge(sem("pt_ready"), h - 1)
            for c in range(3):
                ins = tr(ps[:, 2 + h % 2, c * P:(c + 1) * P], Sm[:, h % 2, c * P:(c + 1) * P], ident[:, :])
            ins.then_inc(sem("pt_done"), 1)

        def values(h):
            pe.wait_ge(sem("pt_ready"), h + 1)
            if h >= 1:
                pe.wait_ge(sem("ya_ready"), h)
            mm(ps[:, 4, 0:TP], vn[:, 0, h * HD:(h + 1) * HD], PT[:, h % 2, 0:TP], start=True, stop=True)
            mm(ps[:, 4, P:TP], vn[:, 1, h * HD:(h + 1) * HD], PT[:, h % 2, TP:384], start=False, stop=True,
               skip_group_check=True).then_inc(sem("o_done"), 1)

        def keys_t(p):
            pe.wait_ge(sem(f"page_loaded{p % 3}"), 16 * (p // 3 + 1))
            if p >= 1:
                pe.wait_ge(sem("kpT_lo"), p)
                pe.wait_ge(sem("kpT_hi"), p)
            for half in range(2):
                for i in range(4):
                    c = (4 * half + i) * HD
                    ins = tr(ps[:, 5 + 2 * half, i * P:(i + 1) * P], page[:, p % 3, c:c + HD], ident[:, :])
                ins.then_inc(sem("kpT_done"), 1)

        def page_scores(p):
            b, c = p // NPG, p % NPG
            pe.wait_ge(sem("kpT_lo"), p + 1)
            pe.wait_ge(sem("kpT_hi"), p + 1)
            for h in range(H):
                col = c * 256 + b * SM + h * TS
                ins = mm(ps[:, 6, col:col + TS], kpT[:, p % 2, h * HD:(h + 1) * HD],
                         qa[:, h, TP + b * TS:TP + (b + 1) * TS], start=True, stop=True)
            ins.then_inc(sem("sT_done"), 1)

        scores(0)
        for h in range(H):
            keys_t(2 * h)
            if h + 1 < H:
                scores(h + 1)
            page_scores(2 * h)
            probs_t(h)
            keys_t(2 * h + 1)
            if h >= 1:
                values(h - 1)
            page_scores(2 * h + 1)
        values(H - 1)
        bhq = lambda x: x.rearrange("p (b h q) -> p b h q", b=NB, h=H)
        for h in range(H):
            ins = mm(bhq(ps[0:SM, 7, 0:256])[:, :, h, :], ka[:, h, TP:T], qa[:, h, TP:T], start=True, stop=True)
        ins.then_inc(sem("sT_done"), 1)
        pe.wait_ge(sem("ya_ready"), H)
        pe.wait_ge(sem("sT_ready"), 1)
        pe.wait_ge(sem("nl_ready"), 1)
        for g2 in range(2):
            r = slice(g2 * P, (g2 + 1) * P)
            o0, o1, o2 = ps[:, 4 + g2, 0:P], ps[:, 4 + g2, P:2 * P], ps[:, 4 + g2, 2 * P:T]
            add = dict(start=False, skip_group_check=True)
            mm(o0, STs[:, r], ident[:, :], start=True, stop=True)
            mm(o0, nl_past[:, 0, r], upper[:, :], stop=True, **add)
            mm(o1, STs[:, 256 + g2 * P:256 + (g2 + 1) * P], ident[:, :], stop=True, **add)
            mm(o1, nl_past[:, 0, r], ones[:, :], stop=True, **add)
            mm(o1, nl_past[:, 1, r], upper[:, :], stop=True, **add)
            mm(o2, STn[:, r], ident[0:SM, 0:SM], stop=True, **add)
            mm(o2, nl_past[:, 0, r], ones[:, 0:SM], stop=True, **add)
            mm(o2, nl_past[:, 1, r], ones[:, 0:SM], stop=True, **add)
            mm(o2, nl_new[:, r], upper4[:, :], stop=True, **add)
            mm(o2, spread[:, r], mask4_q[:, :], stop=True, **add).then_inc(sem("sample_logits"), 1)
        for g2 in range(2):
            pe.wait_ge(sem("sample_p"), g2 + 1)
            tr(ps[:, 0, g2 * P:(g2 + 1) * P], Ps[:, g2, 0:P], ident[:, :])
            tr(ps[:, 0, 256 + g2 * P:256 + (g2 + 1) * P], Ps[:, g2, P:2 * P], ident[:, :])
            ins = tr(ps[0:SM, 1, g2 * P:(g2 + 1) * P], Ps[:, g2, 2 * P:T], ident[:, :])
        ins.then_inc(sem("sample_pT"), 1)
        pe.wait_ge(sem("sample_pT_ready"), 2)
        for h in range(H):
            mm(ps[:, 2, h * SM:(h + 1) * SM], vn[0:SM, 2, h * HD:(h + 1) * HD], bhq(PTn[:, :])[:, :, h, :],
               start=h == 0, stop=True, skip_group_check=True)
        for p in range(NB * NPG):
            b, c = p // NPG, p % NPG
            pe.wait_ge(sem(f"v_loaded{p % VRING}"), 16 * (p // VRING + 1))
            for h in range(H):
                col = c * 256 + b * SM + h * TS
                ins = mm(ps[:, 2, h * SM + b * TS:h * SM + (b + 1) * TS], v_page[p % VRING][:, h * HD:(h + 1) * HD],
                         PTs[:, col:col + TS], start=False, stop=True, skip_group_check=True)
            ins.then_inc(sem("sample_pv"), 1)

        gi_ = lambda t, n=P: G[0:n, t, 2 * H:3 * H]
        for bank, up, one, up4 in ((3, neg_upper, neg_ones, neg_upper4), (4, upper, ones, upper4)):
            for t in range(2):
                o = ps[0:H, bank, t * P:(t + 1) * P]
                if bank == 3:
                    mm(o, gi_(t), ident[:, :], start=True, stop=False)
                if t == 1:
                    mm(o, lf(0, 1), one[:, :], start=bank == 4, stop=False)
                mm(o, lf(t, 1), up[:, :], start=bank == 4 and t == 0, stop=True)
            o = ps[0:H, bank, TP:T]
            if bank == 3:
                mm(o, gi_(2, SM), ident[0:SM, 0:SM], start=True, stop=False)
            mm(o, lf(2, 1, SM), up4[:, :], start=bank == 4, stop=True).then_inc(sem("rows_done"), 1)
        pe.wait_ge(sem("state_loaded"), 3 * 16)
        tr(ps[:, 0, 0:NB * H], n_rows[:, 0, :], ident[0:NB * H, 0:NB * H]).then_inc(sem("edges_done"), 1)
        for j in range(2 * H):
            ins = tr(ps[:, 5, j * 24:(j + 1) * 24], conv_rows[0:24, j * P:(j + 1) * P], ident[0:24, 0:24])
        ins.then_inc(sem("edges_done"), 1)
        pe.wait_ge(sem("ext_edges"), 2)
        pe.wait_ge(sem("ya_ready"), H + 1)
        groups_products(groups["in_m"], 4, xm_hi, xm_lo, (sem("xn_ready"), 16))

        pe.wait_ge(banks_free, NBANK + G_O * NBANK)
        pe.wait_ge(sem("s_rows_ready"), 1)
        for b in range(2):
            for j in range(4):
                ins = mm(ps[:, 6 + b, j * 96:(j + 1) * 96], sel[:, 4 * b + j, :], s_rows[:, :, :], start=True, stop=True)
            ins.then_inc(sem("s_all_done"), 1)
        natural(lambda h, c, n: vm[:, h, c:c + n], 0, "vmT_done")
        pe.wait_ge(sem("km_ready"), 1)
        natural(lambda h, c, n: ext[:, H + h, c:c + n], 0, "kmT_done", "vmn_ready")
        pe.wait_ge(sem("kmn_ready"), 6)
        for j in range(2 * H):
            ins = tr(ps[0:27, 2 + j // 4, (j % 4) * P:(j % 4 + 1) * P], conv_last[:, j, :], ident[:, :])
            if j % 4 == 3:
                ins.then_inc(sem("conv_rows_done"), 1)
        pe.wait_ge(sem("rows_exp"), 3)
        for a, row in enumerate((r_row, ws_row)):
            for t, n in TT:
                ins = tr(ps[0:n, 1, (3 * a + t) * H:(3 * a + t + 1) * H], row[:, t * P:t * P + n], ident[0:H, 0:H])
        ins.then_inc(sem("nat_done"), 1)
        for h in range(H):
            ins = mm(ps[0:SM, 0, h * SM:(h + 1) * SM], ext[:, H + h, TP:T], ext[:, h, TP:T], start=True, stop=True)
        ins.then_inc(sem("ws_scores"), 1)
        pe.wait_ge(sem("conv_rows_ready"), 4)
        pe.wait_ge(sem("qn_ready"), 1)
        pe.wait_ge(sem("ws_ready"), 1)
        add = dict(start=False, skip_group_check=True)
        mm(ps[:, 5, 256:512], ones[:, :], qn[:, :, :], start=True, stop=True)
        mm(ps[:, 5, 256:512], ones[0:SM, :], Ws[:, :, :], stop=True, **add)
        for h in range(H):
            mm(ps[:, 5, h * SM:(h + 1) * SM], vmn[0:SM, 2, h * HD:(h + 1) * HD], Ws[:, h, :], stop=True, **add)
        pe.wait_ge(sem("nat_ready"), 1)
        pe.wait_ge(sem("s_all_ready"), 2)
        pe.wait_ge(sem("kw_ready"), 3)
        for h in range(H):
            hd = slice(h * HD, (h + 1) * HD)
            k_, q_ = ext[:, H + h, :], ext[:, h, :]
            if h >= 1:
                pe.wait_ge(sem("w_ready"), h)
            mm(ps[:, 0, 0:TP], k_[:, 0:P], q_[:, 0:TP], start=True, stop=True)
            mm(ps[:, 0, TP:384], k_[:, P:TP], q_[:, P:TP], start=True, stop=True)
            mm(ps[:, 1, 0:TP], sel[:, h, :], nR_row[:, 0:TP], start=True, stop=True)
            mm(ps[:, 1, TP:384], sel[:, h, :], nR_row[:, P:TP], start=True, stop=True).then_inc(sem("sm_done"), 1)
            if h >= 1:
                pe.wait_ge(sem("em_ready"), h)
            mm(ps[:, 6, 0:TP], sel[:, h, :], em_row[:, 0:TP], start=True, stop=True).then_inc(sem("em_done"), 1)
            pe.wait_ge(sem(f"C_loaded{h % 2}"), 16 * (h // 2 + 1))
            for b in range(NB):
                ins = mm(ps[:, 5, h * SM + b * TS:h * SM + (b + 1) * TS], C[:, h % 2, b, :],
                         qw[:, h, b * TS:(b + 1) * TS], stop=True, **add)
            ins.then_inc(sem("qC_done"), 1)
            pe.wait_ge(sem("v_seq_ready"), h + 1)
            if h >= 1:
                pe.wait_ge(sem("C_new"), 2 * h)
            for c in range(2):
                mm(ps[:, 3 + c, :], kmn[0:SM, 2, hd], v_seq[:, 4 * c:4 * c + 4, :], start=True,
                   stop=True).then_inc(sem("dC_done"), 1)
            if h >= 1:
                pe.wait_ge(sem("Cp_ready"), h)
                pe.wait_ge(sem("n_new_ready"), h)
            mm(ps[:, 7, 0:HD], kmn[:, 0, hd], vmn[:, 0, hd], start=True, stop=False)
            mm(ps[:, 7, 0:HD], kmn[:, 1, hd], vmn[:, 1, hd], start=False, stop=True)
            mm(ps[:, 7, HD:HD + 1], kmn[:, 0, hd], ones[:, 0:1], start=True, stop=False)
            mm(ps[:, 7, HD:HD + 1], kmn[:, 1, hd], ones[:, 0:1], start=False, stop=True)
            mm(ps[:, 7, 256:256 + NB], kmn[0:SM, 2, hd], block4[:, 0:SM:TS], start=True, stop=True).then_inc(
                sem("Cp_done"), 1)
            pe.wait_ge(sem("w_ready"), h + 1)
            if h >= 1:
                pe.wait_ge(sem("h_ready"), h)
            W = Wt[:, h % 2, :]
            mm(ps[:, 2, 0:TP], vmn[:, 0, hd], W[:, 0:TP], start=True, stop=True)
            mm(ps[:, 2, P:TP], vmn[:, 1, hd], W[:, TP:384], stop=True, **add)
            mm(ps[:, 2, TP:512], ones[:, :], W[:, 0:TP], stop=True, **add)
            mm(ps[:, 2, TP + P:512], ones[:, :], W[:, TP:384], stop=True, **add).then_inc(sem("num_done"), 1)
        pe.wait_ge(sem("n_new_ready"), H)
        tr(ps[0:NB * H, 0, 0:HD], n_new[:, 1:1 + NB, :].rearrange("p b h -> p (b h)"), ident[:, :])
        tr(ps[0:H, 0, HD:2 * HD], n_new[:, 0, :], ident[:, :]).then_inc(sem("nT_done"), 1)
        pe.wait_ge(sem("h_ready"), H + 1)
        head_sums(SUM_Y, 1, "xn_tmp", 32, 1)
        pe.wait_ge(sem("xn_tmp"), 48)
        pe.wait_ge(sem("n_rows_ready"), 2)
        groups_products(groups["out"], 2, y_hi, y_lo, (sem("xn_ready"), 32))
        pe.wait_ge(banks_free, NBANK + (G_O + 1) * NBANK + 1)
        norm_sums(3)
        swiglu(1)
        pe.wait_ge(banks_free, NBANK + n_groups * NBANK)
        for i in range(12):
            t, n = TT[i // 4]
            if i >= 4:
                pe.wait_ge(sem("y_rows_ready" if i % 2 == 0 else "y_rows_ready_v"), (i - 4) // 2 + 1)
            for j in range(4):
                ins = tr(ps[0:n, i % 4, j * P:(j + 1) * P], X[:, (i % 4) * 4 + j, t * P:t * P + n], ident[:, :])
            ins.then_inc(sem("y_rows_done"), 1)

    ctx.close()


_OUTS = [("y_prompt", (1, TP, D)), ("y_sample", (NB, TS, D)), ("k_prompt", (1, 1, TP, H, HD)),
         ("v_prompt", (1, 1, TP, H, HD)), ("logf_prompt", (1, 1, TP, H)), ("conv_prompt", (1, 1, CW - 1, QK)),
         ("C_prompt", (1, 1, H, HD, HD)), ("n_prompt", (1, 1, H, HD)), ("m_prompt", (1, 1, H)),
         ("k_sample", (1, NB, TS, H, HD)), ("v_sample", (1, NB, TS, H, HD)), ("logf_sample", (1, NB, TS, H)),
         ("conv_sample", (1, NB, CW - 1, QK)), ("C_sample", (1, NB, H, HD, HD)), ("n_sample", (1, NB, H, HD)),
         ("m_sample", (1, NB, H))]


def kernel(**inputs):
    import numpy as _np
    import concourse.bacc as _bacc
    from concourse.bass_utils import run_bass_kernel_spmd as _run

    nc = _bacc.Bacc("TRN2", target_bir_lowering=False, num_devices=1)
    arrays, A, O = {}, {}, {}
    for name, value in inputs.items():
        a = _np.ascontiguousarray(value)
        arrays[f"in_{name}"] = a
        A[name] = nc.dram_tensor(f"in_{name}", a.shape, mybir.dt.from_np(a.dtype), kind="ExternalInput").ap()
    for name, shape in _OUTS:
        O[name] = nc.dram_tensor(f"out_{name}", shape, F32, kind="ExternalOutput").ap()
    build(nc, A, O)
    r = _run(nc, [arrays], core_ids=[0])
    return tuple(r.results[0][f"out_{name}"] for name, _ in _OUTS)
```

```python
from contextlib import ExitStack

import concourse.bass as bass
from concourse import mybir
from concourse.alu_op_type import AluOpType as ALU

F32 = mybir.dt.float32
F32R = mybir.dt.float32r
I32 = mybir.dt.int32
ACT = mybir.ActivationFunctionType
AX = mybir.AxisListType

P = 128
D = 2048
KD = D // P
TP = 256
NB = 8
TS = 4
SM = NB * TS
T = TP + SM
H = 8
HD = 128
NPG = 2
CHUNK = 24
CW = 4
QK = 2 * H * HD
EPS = 1e-6
SCALE = float(HD) ** -0.5
BIG = 1.0e30
N_IN = 7192
COL_F_A = 3 * H * HD
COL_M = COL_F_A + H
COL_I_M = N_IN - 2 * H
UW = 1024
SLOTS = 4
NBANK = 8
EXT = CW - 1 + TP
EXTS = CW - 1 + TS
EXTW = EXT + NB * EXTS
TT = [(0, P), (1, P), (2, SM)]


class Group:

    def __init__(self, turn, index, nk, real, tiles):
        self.turn, self.index, self.real, self.tiles = turn, index, real, tiles
        self.turns = nk // SLOTS


def plan():
    turn, index, out = 0, 0, {}
    plain = [j * P for j in range(NBANK)]
    gate_up = [c for j in range(4) for c in (j * P, 512 + j * P)]
    swiglu = [("gu{}a", 6, KD, KD, gate_up), ("down{}a", 2, 24, 24, plain), ("gu{}b", 4, KD, KD, gate_up),
              ("gu{}c", 1, KD, KD, gate_up[:6]), ("down{}b", 2, 20, 19, plain)]
    mixer = [("in_a", 3, KD, KD, plain), ("in_m", 4, KD, KD, plain), ("out", 2, KD, KD, plain)]
    for n, part in ((0, swiglu), (0, mixer), (1, swiglu)):
        for name, count, nk, real, tiles in part:
            out[name.format(n)] = Group(turn, index, nk, real, tiles)
            turn += count * nk // SLOTS
            index += count
    return out, turn, index


def build(nc, A, O):
    groups, n_turns, n_groups = plan()
    ctx = ExitStack()
    sems = {}

    def sem(name):
        if name not in sems:
            sems[name] = ctx.enter_context(nc.semaphore(name))
        return sems[name]

    def area(side):
        scope = ExitStack()
        return scope, lambda name, shape, dt=F32: scope.enter_context(nc.sbuf_tensor(name, shape, dt, side=side))

    def twin(side, alloc, name, shape):
        scope, s_ = area(side)
        with scope:
            rounded = s_(name + "_r", shape, F32R)
        return alloc(name, shape), rounded

    ctx.enter_context(nc.allow_non_contiguous_dma(reason="a few small transposed state vectors"))
    keep, t_ = area("left")
    ctx.enter_context(keep)
    ident, ones = t_("ident", [P, P]), t_("ones", [P, P])
    upper = t_("upper", [P, P])
    neg_upper, neg_ones = t_("neg_upper", [P, P]), t_("neg_ones", [P, P])
    lower = t_("lower", [P, P])
    block4 = t_("block4", [SM, SM])
    upper4, neg_upper4, lower4 = t_("upper4", [SM, SM]), t_("neg_upper4", [SM, SM]), t_("lower4", [SM, SM])
    mask_q = t_("mask_q", [P, 3 * P])
    mask_t = t_("mask_t", [P, 3 * P])
    mask4_q = t_("mask4_q", [SM, SM])
    mask4_t = t_("mask4_t", [SM, SM])
    spread = t_("spread", [SM, NB * SM])
    sel = t_("sel", [H, H, P], F32R)
    one_hot = t_("one_hot", [P, H, H])
    root, root_r = twin("left", t_, "root", [H, 2, T])
    vecs = t_("vecs", [P, 146])
    gq_scaled = t_("gq_scaled", [P, 1])
    w_gates = t_("w_gates", [P, KD, 3 * H])
    b_gates = t_("b_gates", [P, 3 * H])
    G = t_("G", [P, 3, 3 * H])
    LF = t_("LF", [P, 3, 2 * H])
    pages_sb = t_("pages_sb", [1, NB * NPG], I32)
    X = t_("X", [P, KD, T])
    w_raw = t_("w_raw", [P, SLOTS, UW])
    w_hi, w_lo = t_("w_hi", [P, SLOTS, UW], F32R), t_("w_lo", [P, SLOTS, UW], F32R)
    sq, xt = t_("sq", [P, 2, T]), t_("xt", [P, 2, T])
    rs, rs_r = twin("left", t_, "rs", [P, 2, T])
    sq_ring = [sq[:, 0, :], sq[:, 1, :], xt[:, 0, :], xt[:, 1, :]]
    root_parts = rs_r[0:H, :, :], root_r[:, :, :]
    gates_row = rs[0:3 * H, 0, :]
    ps = ctx.enter_context(nc.psum_tensor("ps", [P, NBANK, 512], F32))
    V_FFN, V_MIX, V_CB, V_CW, V_GQ, V_GK, V_GA, V_GM = (0, 32), 16, 48, 64, 128, 129, 130, 138

    scope, l_ = area("left")
    with scope:
        x_rows, vec_rows = l_("x_rows", [P, 3, D]), l_("vec_rows", [P, 2, P])

    def operand_memory(name):
        scope, r_ = area("right")
        with scope:
            return r_(name + "_hi", [P, KD, T], F32R), r_(name + "_lo", [P, KD, T], F32R)

    x_op = [operand_memory("x0"), operand_memory("x1")]
    xm_hi, xm_lo = operand_memory("xm")
    y_hi, y_lo = operand_memory("y")
    right_side, r_ = area("right")
    kmn = r_("kmn", [P, 3, H * HD])
    C = r_("C", [P, 2, NB, HD])
    v_seq = r_("v_seq", [SM, NB, HD])
    Ws, qw, qn = r_("Ws", [SM, H, SM]), r_("qw", [P, H, SM]), r_("qn", [P, H, SM])
    Wt = r_("Wt", [P, 2, 384])
    em_all, dn = r_("em_all", [P, 2, TP]), r_("dn", [P, 2, TP])
    Cp = r_("Cp", [P, 2, HD])
    qw_apart = [r_("qw_apart", [P, NB, SM]), qn]

    def swiglu_memory(n):
        scope, l_ = area("left")
        with scope:
            return dict(x=x_op[n], hid=(l_(f"hid_hi{n}", [P, CHUNK, T], F32R), l_(f"hid_lo{n}", [P, CHUNK, T], F32R)),
                        silu=l_(f"silu{n}", [P, 4, T]), prod=l_(f"prod{n}", [P, 4, T]))

    mem = [swiglu_memory(0), swiglu_memory(1)]
    scope_mixer, m_ = area("left")
    with scope_mixer:
        ya = m_("ya", [P, H, T])
        scope, l_ = area("left")
        with scope:
            qa, ka = l_("qa", [P, H, T]), l_("ka", [P, H, T])
            kn, vn = l_("kn", [P, 3, H * HD]), l_("vn", [P, 3, H * HD])
            mx, nmx, den, rden = (l_(n, [P, 2, 2]) for n in ("mx", "nmx", "den", "rden"))
            neg_c, neg_c_r = twin("left", l_, "neg_c", [H, TP])
            neg_c_parts = rs_r[0:H, 1, 0:TP], neg_c_r[:, :]
            page = l_("page", [P, 3, H * HD])
            kpT = l_("kpT", [P, 2, H * HD])
            lf_past = l_("lf_past", [P, NB * NPG, H])
            nl_past = l_("nl_past", [P, NPG, NB * SM])
            nl_new = l_("nl_new", [SM, NB * SM])
            scope_p, p_ = area("left")
            with scope_p:
                lt = p_("lt", [P, 3, 3, 2 * H])
                w_gates_hi, w_gates_lo = (p_(n, [P, KD, 3 * H], F32R) for n in ("w_gates_hi", "w_gates_lo"))
            scope_p, p_ = area("left")
            with scope_p:
                Sm, PT = p_("Sm", [P, 2, 384]), p_("PT", [P, 2, 384])
            qz = nl_past
            pz, out_rows = kpT[:, 0, :].rearrange("p (r n) -> p r n", r=4), kpT[0:SM, 1, :]
            flat = [x[:, :, :].rearrange("p h t -> p (h t)") for x in (qa, ka)]
            v_page = ([kn[:, i, :] for i in range(3)] + [page[:, (NB * NPG + i) % 3, :] for i in range(3)]
                      + [x[:, i * H * HD:(i + 1) * H * HD] for x in flat for i in range(2)])
            VRING = len(v_page)
            PTs, STn = l_("PTs", [P, 512]), l_("STn", [SM, 256])
            PTn = STn
            Ps = l_("Ps", [P, 2, T])
        scope, l_ = area("left")
        with scope:
            ext = l_("ext", [P, 2 * H, EXTW])
            vm, om = l_("vm", [P, H, T]), l_("om", [P, H, T])
            vmn = l_("vmn", [P, 3, H, HD + 1])
            conv_rows = l_("conv_rows", [27, QK])
            conv_last = l_("conv_last", [P, 2 * H, 27])
            r_row, nR_row, m_row, ws_row = (l_(n, [H, T]) for n in ("r_row", "nR_row", "m_row", "ws_row"))
            (b_row, b_row_r), (R_row, R_row_r), (em_row, em_row_r) = (
                twin("left", l_, n, [H, T]) for n in ("b_row", "R_row", "em_row"))
            nR_parts, em_parts = (R_row_r[:, :], b_row_r[:, :]), (rs_r[0:H, 1, :], em_row_r[:, :])
            m0 = l_("m0", [H, NB])
            s_rows = l_("s_rows", [H, 3, SM])
            scope_c, c_ = area("left")
            with scope_c:
                conv_acc = c_("conv_acc", [P, 2, EXTW])
            s_all = l_("s_all", [P, H, 3, SM])
            nat = l_("nat", [P, 6, H])
            n_rows = l_("n_rows", [NB * H, 2, HD])
            n0T, n_new = l_("n0T", [P, NB * H]), l_("n_new", [P, 1 + NB, H])
    right_side.close()
    scope, l_ = area("left")
    with scope:
        y_rows = l_("y_rows", [P, 3, D])

    block = ctx.enter_context(nc.Block())
    w_loaded = [sem(f"w_loaded{s}") for s in range(SLOTS)]
    w_hi_ready, w_lo_ready, w_used = sem("w_hi_ready"), sem("w_lo_ready"), sem("w_used")
    bank_done, banks_free = sem("bank_done"), sem("banks_free")
    small_loaded, pool_const = sem("small_loaded"), sem("pool_const")
    out_stored = sem("out_stored")

    G_A, G_M, G_O = groups["in_a"].index, groups["in_m"].index, groups["out"].index

    def wait_bank(eng, g, turn, gi, b):
        n = len(g.tiles)
        if b < n - 1:
            eng.wait_ge(bank_done, gi * (NBANK - 1) + (b + 1 if b < n - 2 else NBANK - 1))
        else:
            eng.wait_ge(w_used, (turn + g.turns) * 2 + 2)

    def x_final(eng, n, t):
        if n == 0:
            eng.wait_ge(sem("xT_copied"), t + 1)
        else:
            g = groups["down0b" if n == 1 else "out"]
            eng.wait_ge(banks_free, NBANK + g.index * NBANK + t + 1)
    def tiles_of(w):
        return w[0].rearrange("(k p) n -> k p n", p=P)

    wg, wu, wd = ([tiles_of(A[f"w{n}_{kind}"]) for n in (1, 2)] for kind in ("gate", "up", "down"))
    wi, wo = tiles_of(A["w_in"]), tiles_of(A["w_out"])

    @block.sync
    def _(sp):
        def load_turn(turn, slots, parts, fresh=False):
            for s in slots:
                if not fresh:
                    sp.wait_ge(w_hi_ready, turn * SLOTS + (s + 1 - SLOTS))
                    sp.wait_ge(w_lo_ready, turn * SLOTS + (s + 1 - SLOTS))
                for c, src in parts(s):
                    sp.dma_start(w_raw[:, s, c:c + src.shape[-1]], src).then_inc(w_loaded[s], 32 // len(parts(s)))

        def load_group(g, turn, unit_src, start=0):
            whole = g.real // SLOTS
            with sp.Fori(start, whole) as kt:
                load_turn(turn + kt, range(SLOTS), lambda s: unit_src(kt * SLOTS + s))
            if whole < g.turns:
                load_turn(turn + whole, range(SLOTS), lambda s: unit_src(min(whole * SLOTS + s, g.real - 1)))

        def load_swiglu(n):
            def gate_up(col, w):
                return lambda k: [(0, wg[n][k, :, bass.ds(col, w)]), (512, wu[n][k, :, bass.ds(col, w)])]

            def down(k0, col):
                return lambda k: [(0, wd[n][k + k0, :, bass.ds(col, UW)])]

            g = groups[f"gu{n}a"]
            if n == 0:
                load_turn(0, range(SLOTS), gate_up(0, 512), fresh=True)
                load_group(g, g.turn, gate_up(0, 512), start=1)
            with sp.Fori(1 if n == 0 else 0, 6) as i:
                load_group(g, i * g.turns + g.turn, gate_up(i * 512, 512))
            g = groups[f"down{n}a"]
            with sp.Fori(0, 2) as i:
                load_group(g, i * g.turns + g.turn, down(0, i * UW))
            g = groups[f"gu{n}b"]
            with sp.Fori(0, 4) as i:
                load_group(g, i * g.turns + g.turn, gate_up(i * 512 + CHUNK * P, 512))
            g = groups[f"gu{n}c"]
            load_group(g, g.turn, gate_up(40 * P, 384))
            g = groups[f"down{n}b"]
            with sp.Fori(0, 2) as i:
                load_group(g, i * g.turns + g.turn, down(CHUNK, i * UW))

        load_swiglu(0)

        def columns(w, col):
            return lambda k: [(0, w[k, :, bass.ds(col, UW)])]

        def load_mixer(name, count, w, col, meanwhile=None):
            g = groups[name]
            if meanwhile:
                for kt in range(2):
                    load_turn(g.turn + kt, range(SLOTS), lambda s: columns(w, col)(kt * SLOTS + s))
                meanwhile()
                load_group(g, g.turn, columns(w, col), start=2)
            with sp.Fori(1 if meanwhile else 0, count) as i:
                load_group(g, i * g.turns + g.turn, columns(w, i * UW + col))

        def load_pages():
            sp.wait_ge(small_loaded, 16 * 16)
            sp.wait_ge(banks_free, NBANK + G_A * NBANK)

            def load_page(cache, p, dst, loaded):
                pid = sp.value_load(pages_sb[0:1, p:p + 1], min_val=0, max_val=cache.shape[1] - 1)
                sp.dma_start(dst, cache[0][bass.ds(pid, 1), :, :, :].rearrange("a s h d -> (a s) (h d)")).then_inc(
                    loaded, 16)

            for p in range(NB * NPG):
                if p >= 3:
                    sp.wait_ge(sem("kpT_done"), 2 * (p - 2))
                load_page(A["cache_k"], p, page[:, p % 3, :], sem(f"page_loaded{p % 3}"))
            for p in range(NB * NPG):
                if p == 0:
                    sp.wait_ge(out_stored, 6 * 16)
                if 3 <= p < 6:
                    sp.wait_ge(sem("kpT_done"), 2 * (NB * NPG - 5 + p))
                if p == 6:
                    sp.wait_ge(sem("sT_done"), NB * NPG + 1)
                if p >= VRING:
                    sp.wait_ge(sem("sample_pv"), p - VRING + 1)
                load_page(A["cache_v"], p, v_page[p % VRING], sem(f"v_loaded{p % VRING}"))

        def state_traffic():
            sp.wait_ge(banks_free, NBANK + G_O * NBANK)

            def load_state(h):
                sp.dma_start(C[:, h % 2, :, :], A["state_C"][0, :, h, :, :].rearrange("b d e -> d b e")).then_inc(
                    sem(f"C_loaded{h % 2}"), 16)

            load_state(0)
            load_state(1)
            for h in range(H):
                sp.wait_ge(sem("C_new"), 2 * (h + 1))
                sp.dma_start(O["C_sample"][0, :, h, :, :].rearrange("b d e -> d b e"), C[:, h % 2, :, :]).then_inc(
                    sem(f"C_stored{h % 2}"), 16)
                if h + 2 < H:
                    sp.wait_ge(sem(f"C_stored{h % 2}"), 16 * (h // 2 + 1))
                    load_state(h + 2)
                sp.wait_ge(sem("Cp_ready"), h + 1)
                sp.dma_start(O["C_prompt"][0, 0, h, :, :], Cp[:, h % 2, :]).then_inc(sem(f"Cp_stored{h % 2}"), 16)

        load_mixer("in_a", 3, wi, 0)
        load_mixer("in_m", 4, wi, COL_M, load_pages)
        load_mixer("out", 2, wo, 0, state_traffic)
        load_swiglu(1)
        load_turn(n_turns, range(2), lambda s: [(0, wd[1][s, :, 0:UW])])
        for s in range(2):
            sp.wait_ge(w_loaded[s], 32 * (n_turns + 1))

    SUM_X = {0: 0, 1: 16, 3: 64}
    SUM_QK, SUM_Y = 32, 48

    @block.gpsimd
    def _(pool):
        nc.gpsimd.memset(ones[:, :], 1.0).then_inc(pool_const, 1)
        nc.gpsimd.memset(ident[:, :], 0.0).then_inc(pool_const, 1)
        pool.wait_ge(pool_const, 2)
        nc.gpsimd.affine_select(out=upper[:, :], in_=ones[:, :], compare_op=ALU.is_ge, fill=0.0, base=0,
                                pattern=[[1, P]], channel_multiplier=-1)
        nc.gpsimd.affine_select(out=lower[:, :], in_=ones[:, :], compare_op=ALU.is_ge, fill=0.0, base=0,
                                pattern=[[-1, P]], channel_multiplier=1)
        nc.gpsimd.affine_select(out=block4[:, :].rearrange("p (b t) -> p b t", t=TS),
                                in_=ones[0:SM, 0:SM].rearrange("p (b t) -> p b t", t=TS), compare_op=ALU.is_ge,
                                fill=0.0, base=0, pattern=[[-TS, NB], [0, TS]], channel_multiplier=1)
        nc.gpsimd.affine_select(out=ident[:, :], in_=ident[:, :], compare_op=ALU.not_equal, fill=1.0, base=0,
                                pattern=[[-1, P]], channel_multiplier=1).then_inc(pool_const, 1)
        pool.wait_ge(pool_const, 3)
        nc.gpsimd.affine_select(out=block4[:, :].rearrange("p (b t) -> p b t", t=TS),
                                in_=block4[:, :].rearrange("p (b t) -> p b t", t=TS), compare_op=ALU.is_ge,
                                fill=0.0, base=TS - 1, pattern=[[TS, NB], [0, TS]],
                                channel_multiplier=-1).then_inc(pool_const, 1)

        def small(dst, src):
            pool.dma_start(dst, src).then_inc(small_loaded, 16)

        rows = lambda name: A[name].rearrange("l (r p) -> (l r) p", p=P)
        for name, r0, n in (("g_ffn1", 0, 16), ("g_mix", 16, 16), ("g_ffn2", 32, 16), ("conv_b", 48, 16)):
            small(vec_rows[r0:r0 + n, 0, :], rows(name))
        small(vec_rows[64:128, 0, :], A["conv_w"].rearrange("l c (r p) -> (l c r) p", p=P))
        small(vec_rows[0:1, 1, :], A["g_q"])
        small(vec_rows[1:2, 1, :], A["g_k"])
        small(vec_rows[2:10, 1, :], A["g_out_a"][0])
        small(vec_rows[10:18, 1, :], A["g_out_m"][0])
        wi_p = A["w_in"][0].rearrange("(k p) n -> p k n", p=P)
        small(w_gates[:, :, 0:H], wi_p[:, :, COL_F_A:COL_F_A + H])
        small(w_gates[:, :, H:2 * H], wi_p[:, :, COL_I_M + H:N_IN])
        small(w_gates[:, :, 2 * H:3 * H], wi_p[:, :, COL_I_M:COL_I_M + H])
        for c, name in enumerate(("b_fox_f", "b_m_f", "b_m_i")):
            small(b_gates[:, c * H:(c + 1) * H], A[name].to_broadcast([P, H]))
        small(pages_sb[:, :], A["page_table"].rearrange("b n -> (b n)").unsqueeze(0))

        def store(dst, src):
            pool.dma_start(dst, src).then_inc(out_stored, 16)

        pool.wait_ge(small_loaded, 16 * 16)
        pool.wait_ge(banks_free, NBANK + G_A * NBANK)
        for p in range(NB * NPG):
            pid = pool.value_load(pages_sb[0:1, p:p + 1], min_val=0, max_val=A["cache_logf"].shape[1] - 1)
            pool.dma_start(lf_past[:, p, :], A["cache_logf"][0][bass.ds(pid, 1), :, :]
                           .rearrange("a s h -> (a s) h")).then_inc(sem("lf_past_loaded"), 16)

        pool.wait_ge(sem("lf_ready"), 1)
        store(O["logf_prompt"][0, 0].rearrange("(t p) h -> p t h", p=P), LF[:, 0:2, 0:H])
        store(O["logf_sample"][0].rearrange("b t h -> (b t) h"), LF[0:SM, 2, 0:H])
        pool.wait_ge(sem("vn_ready"), 6)
        store(O["v_prompt"][0, 0].rearrange("(t p) h d -> p t (h d)", p=P), vn[:, 0:2, :])
        store(O["v_sample"][0].rearrange("b t h d -> (b t) (h d)"), vn[0:SM, 2, :])
        pool.wait_ge(sem("kn_ready"), 6)
        store(O["k_prompt"][0, 0].rearrange("(t p) h d -> p t (h d)", p=P), kn[:, 0:2, :])
        store(O["k_sample"][0].rearrange("b t h d -> (b t) (h d)"), kn[0:SM, 2, :])

        pool.wait_ge(sem("ya_ready"), H + 1)
        pool.wait_ge(out_stored, 6 * 16)
        pool.dma_start(conv_rows[0:24, :], A["state_conv"][0].rearrange("b r c -> (b r) c")).then_inc(sem("state_loaded"), 16)
        pool.dma_start(n_rows[:, 0, :], A["state_n"][0].rearrange("b h d -> (b h) d")).then_inc(sem("state_loaded"), 16)
        pool.dma_start(m0[:, :], A["state_m"][0].rearrange("b h -> h b")).then_inc(sem("state_loaded"), 16)
        for j in range(H, 2 * H):
            pool.wait_ge(sem("conv_used"), 2 * (j + 1))
            nc.gpsimd.tensor_scalar(ext[:, j, 0:T], ext[:, j, 0:T], SCALE, None, ALU.mult).then_inc(sem("km_ready"), 1)
        pool.wait_ge(sem("kmn_ready"), 6)
        pool.wait_ge(sem("nat_ready"), 1)
        for t, n in TT:
            k3 = kmn[0:n, t, :].rearrange("p (h d) -> p h d", h=H)
            nc.gpsimd.tensor_tensor(k3, k3, nat[0:n, 3 + t, :].unsqueeze(2).to_broadcast([n, H, HD]),
                                    ALU.mult).then_inc(sem("kw_ready"), 1)
        for h in range(H):
            if h >= 1:
                pool.wait_ge(sem("dC_done"), 2 * h)
            nc.gpsimd.tensor_tensor(v_seq[:, :, :],
                                    vmn[0:SM, 2, h, 0:HD].unsqueeze(1).to_broadcast([SM, NB, HD]),
                                    block4[:, 0:SM:TS].unsqueeze(2).to_broadcast([SM, NB, HD]),
                                    ALU.mult).then_inc(sem("v_seq_ready"), 1)
            pool.wait_ge(sem(f"C_loaded{h % 2}"), 16 * (h // 2 + 1))
            pool.wait_ge(sem("qC_done"), h + 1)
            w_last = s_all[:, h, 0, :].rearrange("p (b t) -> p b t", t=TS)[:, :, TS - 1]
            nc.gpsimd.tensor_tensor(C[:, h % 2, :, :], C[:, h % 2, :, :],
                                    w_last.unsqueeze(2).to_broadcast([P, NB, HD]),
                                    ALU.mult).then_inc(sem("C_decayed"), 1)
        pool.wait_ge(sem("conv_rows_ready"), 4)
        store(O["conv_prompt"][0, 0], conv_rows[0:3, :])
        store(O["conv_sample"][0].rearrange("b r c -> (b r) c"), conv_rows[3:27, :])
        store(O["m_prompt"][0].rearrange("b h -> h b"), m_row[:, TP - 1:TP])
        store(O["m_sample"][0].rearrange("b h -> h b"),
              m_row[:, TP:T].rearrange("h (b t) -> h b t", t=TS)[:, :, TS - 1])
        pool.wait_ge(sem("o_sigmoid"), 1)
        for h in range(H):
            pool.wait_ge(sem("sq_ready"), SUM_Y + H + h + 1)
            nc.gpsimd.tensor_tensor(vm[:, h, :], vm[:, h, :], om[:, h, :], ALU.mult).then_inc(sem("gated"), 1)
        pool.wait_ge(sem("n_rows_ready"), 2)
        store(O["n_sample"][0].rearrange("b h d -> (b h) d"), n_rows[:, 0, :])
        store(O["n_prompt"][0, 0], n_rows[0:H, 1, :])
        for t, n in TT:
            pool.wait_ge(sem("y_rows_ready"), 2 * (t + 1))
            pool.wait_ge(sem("y_rows_ready_v"), 2 * (t + 1))
            if t < 2:
                store(O["y_prompt"][0, t * P:(t + 1) * P, :], y_rows[:, t, :])
            else:
                store(O["y_sample"].rearrange("b t d -> (b t) d"), y_rows[0:SM, 2, :])
        pool.wait_ge(out_stored, 16 * (6 + 4 + 2 + 3))
        for kind in ("C_stored", "Cp_stored"):
            for b in range(2):
                pool.wait_ge(sem(f"{kind}{b}"), 16 * (H // 2))

    SILU0 = {"gu0a": 0, "gu0b": 24, "gu0c": 40, "gu1a": 43, "gu1b": 67, "gu1c": 83}
    NGRP = {"a": 6, "b": 4, "c": 1}

    @block.scalar
    def _(act):
        def split_hi(turn, slot):
            act.wait_ge(w_loaded[slot], turn * 32 + 32)
            if not (isinstance(turn, int) and turn == 0):
                act.wait_ge(w_used, turn * 2 + (slot // 2 + 1))
            nc.scalar.copy(w_hi[:, slot, :], w_raw[:, slot, :]).then_inc(w_hi_ready, 1)

        def split_turns(turn, n):
            with act.Fori(1, n) as kt:
                for s in range(SLOTS):
                    split_hi(turn + kt, s)
            split_pair(turn + n, 0)

        def split_pair(turn, s):
            split_hi(turn, s)
            split_hi(turn, s + 1)

        def split_groups(g, n, last=False):
            split_turns(g.turn, n * g.turns)
            if not last:
                split_pair(g.turn + n * g.turns, 2)

        def square(i, src):
            if i >= 4:
                act.wait_ge(sem("sum_done"), i - 3)
            nc.scalar.activation(sq_ring[i % 4], src, ACT.Square).then_inc(sem("sq_ready"), 1)

        def operand_hi(m, t, dst):
            act.wait_ge(sem("xn_tmp"), 16 * m + t + 1)
            nc.scalar.copy(dst[:, t, :], xt[:, t % 2, :]).then_inc(sem("xn_hi"), 1)

        def sqrt(i, out, src):
            act.wait_ge(sem("mean_ready"), i + 1)
            nc.scalar.activation(out, src, ACT.Sqrt).then_inc(sem("sqrt_ready"), 1)

        def norm(n, dst_hi):
            for t in range(KD):
                x_final(act, min(n, 2), t)
                square(SUM_X[n] + t, X[:, t, :])
            sqrt((0, 1, None, 4)[n], rs[:, 1, :], rs[:, 0, :])
            for t in range(KD):
                operand_hi(n, t, dst_hi)

        def swiglu(n):
            for part in "abc":
                g = groups[f"gu{n}{part}"]

                def group(i):
                    turn0 = i * g.turns + g.turn
                    split_turns(turn0, g.turns)
                    act.wait_ge(banks_free, (i + g.index) * NBANK + NBANK)
                    for j in range(len(g.tiles) // 2):
                        wait_bank(act, g, turn0, i + g.index, 2 * j)
                        nc.scalar.activation(mem[n]["silu"][:, j, :], ps[:, 2 * j, 0:T],
                                             ACT.Silu).then_inc(sem("silu_ready"), 1)
                    split_pair(turn0 + g.turns, 2)

                if part != "c":
                    with act.Fori(0, NGRP[part]) as i:
                        group(i)
                    if part == "a":
                        split_groups(groups[f"down{n}a"], 2)
                else:
                    group(0)
            split_groups(groups[f"down{n}b"], 2, last=n == 1)

        for t in range(2):
            act.dma_start(x_rows[:, t, :], A["x_prompt"][0, t * P:(t + 1) * P, :]).then_inc(sem("x_loaded"), 16)
        act.dma_start(x_rows[0:SM, 2, :], A["x_sample"].rearrange("b t d -> (b t) d")).then_inc(sem("x_loaded"), 16)
        split_pair(0, 0)
        split_pair(0, 2)
        norm(0, mem[0]["x"][0])
        swiglu(0)
        norm(1, xm_hi)
        split_groups(groups["in_a"], 3)

        def natural(dst, made, name):
            for i in range(6):
                t, half, n = i // 2, i % 2, TT[i // 2][1]
                act.wait_ge(sem(made), i + 1)
                nc.scalar.copy(dst[0:n, t, half * 512:half * 512 + 512], ps[0:n, 2 + i, :]).then_inc(sem(name), 1)

        for j in range(2 * H):
            act.wait_ge(banks_free, NBANK + G_M * NBANK)
            square(SUM_QK + j, (qa if j < H else ka)[:, j % H, :])
            if j == H - 1:
                act.wait_ge(sem("abs_ready"), 1)
                nc.scalar.activation(lt[:, 1, :, :], lt[:, 0, :, :], ACT.Exp, scale=-1.0).then_inc(sem("abs_exp"), 1)
        sqrt(2, root[:, :, :], rs[0:H, :, :])
        natural(vn, "vT_done", "vn_ready")
        natural(kn, "kT_done", "kn_ready")

        def p_exp(h):
            act.wait_ge(sem("s_masked"), h + 1)
            b = h % 2
            for q, c0, c1 in ((0, 0, P), (1, P, 384)):
                nc.scalar.activation(Sm[:, b, c0:c1], Sm[:, b, c0:c1], ACT.Exp, bias=nmx[:, b, q:q + 1],
                                     accum_out=den[:, b, q:q + 1]).then_inc(sem("p_exp"), 1)

        def pt_copy(h):
            act.wait_ge(sem("pt_done"), h + 1)
            if h >= 2:
                act.wait_ge(sem("o_done"), h - 1)
            nc.scalar.copy(PT[:, h % 2, :], ps[:, 2 + h % 2, 0:384]).then_inc(sem("pt_ready"), 1)

        def keys_copy(p):
            act.wait_ge(sem("kpT_done"), 2 * p + 1)
            if p >= 2:
                act.wait_ge(sem("sT_done"), p - 1)
            nc.scalar.copy(kpT[:, p % 2, 0:512], ps[:, 5, :]).then_inc(sem("kpT_lo"), 1)

        for h in range(H):
            p_exp(h)
            keys_copy(2 * h)
            pt_copy(h)
            keys_copy(2 * h + 1)
        act.wait_ge(sem("sample_max"), 1)
        for g2 in range(2):
            for k, (c0, src) in enumerate(((0, ps[:, 6, g2 * 256:(g2 + 1) * 256]), (256, ps[:, 5, g2 * SM:(g2 + 1) * SM]))):
                nc.scalar.activation(Ps[:, g2, c0:c0 + src.shape[-1]], src, ACT.Exp, bias=nmx[:, 0, g2:g2 + 1],
                                     accum_out=den[:, k, g2:g2 + 1]).then_inc(sem("sample_exp"), 1)
        act.wait_ge(sem("sample_pT"), 1)
        nc.scalar.copy(PTs[:, :], ps[:, 0, :]).then_inc(sem("sample_pT_ready"), 1)
        nc.scalar.copy(PTn[:, :].rearrange("p (h b q) -> p b h q", h=H, b=NB),
                       ps[0:SM, 1, 0:256].rearrange("p (b h q) -> p b h q", b=NB, h=H)).then_inc(sem("sample_pT_ready"), 1)

        act.wait_ge(sem("rows_sum"), 4)
        nc.scalar.activation(em_row[:, :], m_row[:, :], ACT.Exp, scale=-1.0).then_inc(sem("rows_exp"), 1)
        nc.scalar.activation(ws_row[:, 0:TP], r_row[:, 0:TP], ACT.Exp, bias=nR_row[:, TP - 1:TP]).then_inc(sem("rows_exp"), 1)
        nc.scalar.activation(ws_row[:, TP:T], ws_row[:, TP:T], ACT.Exp).then_inc(sem("rows_exp"), 1)
        nc.scalar.activation(s_rows[:, 0, :], s_rows[:, 0, :], ACT.Exp).then_inc(sem("rows_exp"), 1)

        def conv_silu(j):
            act.wait_ge(sem("conv_done"), j + 1)
            act.wait_ge(sem("conv_last"), 2 * (1 + j // H))
            cb = vecs[:, V_CB + j:V_CB + j + 1]
            nc.scalar.activation(ext[:, j, 0:TP], conv_acc[:, j % 2, 0:TP], ACT.Silu, bias=cb).then_inc(sem("conv_used"), 1)
            nc.scalar.activation(ext[:, j, TP:T].rearrange("p (b t) -> p b t", t=TS),
                                 conv_acc[:, j % 2, EXT:EXTW].rearrange("p (b t) -> p b t", t=EXTS)[:, :, 0:TS],
                                 ACT.Silu, bias=cb).then_inc(sem("conv_used"), 1)

        g = groups["in_m"]
        split_groups(g, 2)
        for t in range(2 * g.turns):
            split_pair(g.turn + 2 * g.turns + (t + 1), 0)
            conv_silu(2 * t)
            conv_silu(2 * t + 1)
            split_pair(g.turn + 2 * g.turns + (t + 1), 2)
        act.wait_ge(banks_free, NBANK + G_O * NBANK)
        for i in range(6):
            t, half, n = i // 2, i % 2, TT[i // 2][1]
            act.wait_ge(sem("kmT_done"), i + 1)
            nc.scalar.copy(kmn[0:n, t, half * 512:half * 512 + 512], ps[0:n, i, :]).then_inc(sem("kmn_ready"), 1)
        for b in range(2):
            act.wait_ge(sem("s_all_done"), b + 1)
            nc.scalar.copy(s_all[:, 4 * b:4 * b + 4, :, :], ps[:, 6 + b, 0:384].rearrange(
                "p (h r s) -> p h r s", h=4, r=3)).then_inc(sem("s_all_ready"), 1)
        act.wait_ge(sem("ws_logits"), 1)
        nc.scalar.activation(Ws[:, :, :], Ws[:, :, :], ACT.Exp).then_inc(sem("ws_exp"), 1)
        for h in range(H):
            if h == H // 2:
                nc.scalar.activation(om[:, :, :], om[:, :, :], ACT.Sigmoid).then_inc(sem("o_sigmoid"), 1)
            act.wait_ge(sem("e_logits"), h + 1)
            for t, c0, c1 in ((0, 0, TP), (1, TP, 384)):
                nc.scalar.activation(Wt[:, h % 2, c0:c1], Wt[:, h % 2, c0:c1], ACT.Exp,
                                     bias=nat[:, t, h:h + 1]).then_inc(sem("e_exp"), 1)
            act.wait_ge(sem("em_done"), h + 1)
            if h >= 2:
                act.wait_ge(sem("h_ready"), h - 1)
            nc.scalar.copy(em_all[:, h % 2, :], ps[:, 6, 0:TP]).then_inc(sem("em_ready"), 1)
            act.wait_ge(sem("Cp_done"), h + 1)
            if h >= 2:
                act.wait_ge(sem(f"Cp_stored{h % 2}"), 16 * (h // 2))
            nc.scalar.copy(Cp[:, h % 2, :], ps[:, 7, 0:HD]).then_inc(sem("Cp_ready"), 1)
            act.wait_ge(sem("qC_done"), h + 1)
            if h >= 2:
                act.wait_ge(sem("qC_added"), h - 1)
            nc.scalar.copy(n_rows[0:SM, h % 2, :], ps[0:SM, 7, TP + NB:TP + NB + HD]).then_inc(sem("qC_rows"), 1)
        for j in range(KD):
            if j >= H:
                act.wait_ge(sem("h_ready"), H + 1)
            square(SUM_Y + j, (ya if j < H else vm)[:, j % H, :])
        sqrt(3, root[:, :, :], rs[0:H, :, :])
        for t in range(KD):
            operand_hi(2, t, y_hi)
        split_groups(groups["out"], 2)
        norm(3, mem[1]["x"][0])
        act.wait_ge(out_stored, 12 * 16)
        swiglu(1)
        for i in range(12):
            if i % 2 == 0:
                act.wait_ge(sem("y_rows_done"), i + 1)
                t, n = TT[i // 4]
                nc.scalar.copy(y_rows[0:n, t, (i % 4) * 512:(i % 4 + 1) * 512], ps[0:n, i % 4, :]).then_inc(sem("y_rows_ready"), 1)

    @block.vector
    def _(dve):
        chain = [0]

        def link(ins):
            chain[0] += 1
            ins.then_inc(sem("dve_chain"), 1)
            dve.wait_ge(sem("dve_chain"), chain[0])

        def split_lo(turn, slot):
            dve.wait_ge(w_hi_ready, turn * SLOTS + (slot + 1))
            nc.vector.tensor_tensor(w_lo[:, slot, :], w_raw[:, slot, :], w_hi[:, slot, :].bitcast(F32),
                                    ALU.subtract).then_inc(w_lo_ready, 1)

        def split_turns(turn, n):
            with dve.Fori(1, n) as kt:
                for s in range(SLOTS):
                    split_lo(turn + kt, s)
            split_pair(turn + n, 0)

        def split_pair(turn, s):
            split_lo(turn, s)
            split_lo(turn, s + 1)

        def rsqrt_mean(i, y, v, tmp, src, width):
            nc.vector.tensor_scalar(v, src, 1.0 / width, EPS, ALU.mult, ALU.add).then_inc(sem("mean_ready"), 1)
            dve.wait_ge(sem("sqrt_ready"), i + 1)
            link(nc.vector.reciprocal(y, y))
            link(nc.vector.tensor_tensor(tmp, y, y, ALU.mult))
            link(nc.vector.scalar_tensor_tensor(tmp, v, -0.5, tmp, ALU.mult, ALU.mult))
            return nc.vector.scalar_tensor_tensor(y, tmp, 1.5, y, ALU.add, ALU.mult)

        def head_norm(j, x, gain):
            dve.wait_ge(sem("spread_done"), j + 1)
            bank = j % 2 + (0 if j < 2 * H else 1)
            return lambda out: nc.vector.scalar_tensor_tensor(out, x, gain, ps[:, bank, 0:T], ALU.mult, ALU.mult)

        def parts(x, hi, lo):
            link(nc.vector.tensor_copy(hi, x))
            return nc.vector.tensor_tensor(lo, x, hi.bitcast(F32), ALU.subtract)

        def operand_lo(m, t, dst_hi, dst_lo):
            dve.wait_ge(sem("xn_hi"), 16 * m + t + 1)
            nc.vector.tensor_tensor(dst_lo[:, t, :], xt[:, t % 2, :], dst_hi[:, t, :].bitcast(F32),
                                    ALU.subtract).then_inc(sem("xn_ready"), 1)

        def norm(n, gain, dst_hi, dst_lo):
            dve.wait_ge(sem("sum_done"), SUM_X[n] + KD)
            link(rsqrt_mean((0, 1, None, 4)[n], rs[:, 1, :], rs[:, 0, :], xt[:, 0, :], ps[:, 0, 0:T], D))
            for t in range(KD + 1):
                if t < KD:
                    if t >= 2:
                        dve.wait_ge(sem("xn_ready"), 16 * n + t - 1)
                    nc.vector.scalar_tensor_tensor(xt[:, t % 2, :], X[:, t, :], vecs[:, gain + t:gain + t + 1],
                                                   rs[:, 1, :], ALU.mult, ALU.mult).then_inc(sem("xn_tmp"), 1)
                if t >= 1:
                    operand_lo(n, t - 1, dst_hi, dst_lo)

        def swiglu(n):
            hid_hi, hid_lo = mem[n]["hid"]
            silu, prod = mem[n]["silu"], mem[n]["prod"]

            def down(name, last=False):
                g = groups[name]
                for half in range(2):
                    split_turns(half * g.turns + g.turn, g.turns)
                    residual(g, half, 0.5)
                    if not (last and half == 1):
                        split_pair(half * g.turns + (g.turn + g.turns), 2)

            for part in "abc":
                g = groups[f"gu{n}{part}"]
                s0, f0 = SILU0[f"gu{n}{part}"], 16 if part == "c" else 0

                def group(i):
                    turn0, nj = i * g.turns + g.turn, len(g.tiles) // 2
                    split_turns(turn0, g.turns)
                    for j in range(nj):
                        dve.wait_ge(sem("silu_ready"), i * 4 + (s0 + j + 1))
                        wait_bank(dve, g, turn0, i + g.index, 2 * j + 1)
                        freed = 2 if j < nj - 1 else NBANK - 2 * (nj - 1)
                        nc.vector.tensor_tensor(prod[:, j, :], silu[:, j, :], ps[:, 2 * j + 1, 0:T],
                                                ALU.mult).then_inc(banks_free, freed)
                    split_pair(turn0 + g.turns, 2)
                    dve.wait_ge(banks_free, (i + g.index) * NBANK + 2 * NBANK)
                    for j in range(nj):
                        nc.vector.tensor_scalar(hid_hi[:, i * 4 + (f0 + j), :], prod[:, j, :], 1.0, None,
                                                ALU.mult).then_inc(sem("hid_hi_ready"), 1)
                    for j in range(nj):
                        dve.wait_ge(sem("hid_hi_ready"), i * 4 + (s0 + j + 1))
                        nc.vector.tensor_tensor(hid_lo[:, i * 4 + (f0 + j), :], prod[:, j, :],
                                                hid_hi[:, i * 4 + (f0 + j), :].bitcast(F32),
                                                ALU.subtract).then_inc(sem("hid_ready"), 1)
                    dve.wait_ge(sem("hid_ready"), i * 4 + (s0 + nj))

                if part != "c":
                    with dve.Fori(0, NGRP[part]) as i:
                        group(i)
                    if part == "a":
                        down(f"down{n}a")
                else:
                    group(0)
            down(f"down{n}b", last=n == 1)

        def residual(g, half, scale):
            for b in range(NBANK):
                wait_bank(dve, g, half * g.turns + g.turn, half + g.index, b)
                x = X[:, half * NBANK + b, :]
                nc.vector.scalar_tensor_tensor(x, ps[:, b, 0:T], scale, x, ALU.mult, ALU.add).then_inc(banks_free, 1)

        nc.vector.memset(neg_ones[:, :], -1.0)
        nc.vector.memset(mask_q[:, P:2 * P], 0.0)
        nc.vector.memset(mask_t[:, P:2 * P], 0.0)
        nc.vector.memset(G[:, :, :], 0.0)
        dve.wait_ge(pool_const, 4)
        nc.vector.tensor_scalar(neg_upper[:, :], upper[:, :], -1.0, None, ALU.mult)
        for c in (0, 2 * P):
            nc.vector.tensor_scalar(mask_q[:, c:c + P], lower[:, :], -1.0, BIG, ALU.add, ALU.mult)
            nc.vector.tensor_scalar(mask_t[:, c:c + P], upper[:, :], -1.0, BIG, ALU.add, ALU.mult)
        nc.vector.tensor_tensor(upper4[:, :], upper[0:SM, 0:SM], block4[:, :], ALU.mult)
        link(nc.vector.tensor_tensor(lower4[:, :], lower[0:SM, 0:SM], block4[:, :], ALU.mult))
        nc.vector.tensor_scalar(neg_upper4[:, :], upper4[:, :], -1.0, None, ALU.mult)
        nc.vector.tensor_scalar(mask4_q[:, :], lower4[:, :], -1.0, BIG, ALU.add, ALU.mult)
        nc.vector.tensor_scalar(mask4_t[:, :], upper4[:, :], -1.0, BIG, ALU.add, ALU.mult)
        nc.vector.tensor_copy(spread[:, :].rearrange("p (b h q) -> p b h q", b=NB, h=H),
                              ident[0:SM, 0:SM].rearrange("p (b q) -> p b q", q=TS).unsqueeze(2)
                              .to_broadcast([SM, NB, H, TS]))
        nc.vector.memset(one_hot[:, :, :], 0.0).then_inc(sem("one_hot_zero"), 1)
        dve.wait_ge(sem("one_hot_zero"), 1)
        for h in range(H):
            nc.vector.memset(one_hot[:, h, h:h + 1], 1.0)
        nc.vector.tensor_copy(sel[:, :, :], ident[0:H, 0:H].unsqueeze(2).to_broadcast([H, H, P]))
        split_pair(0, 0)
        for t in range(KD):
            dve.wait_ge(sem("xT_done"), t + 1)
            nc.vector.tensor_copy(X[:, t, :], ps[:, 1 + t % 4, 0:T]).then_inc(sem("xT_copied"), 1)
            if t in (6, 10):
                split_lo(0, 2 if t == 6 else 3)
        dve.wait_ge(sem("vecT_done"), 1)
        nc.vector.tensor_copy(vecs[:, :], ps[:, 7, 0:146]).then_inc(banks_free, NBANK)
        dve.wait_ge(banks_free, NBANK)
        nc.vector.tensor_scalar(gq_scaled[:, :], vecs[:, V_GQ:V_GQ + 1], SCALE, None, ALU.mult).then_inc(sem("vecs_ready"), 1)

        norm(0, V_FFN[0], *mem[0]["x"])
        swiglu(0)
        norm(1, V_MIX, xm_hi, xm_lo)

        link(nc.vector.tensor_copy(w_gates_hi[:, :, :], w_gates[:, :, :]))
        nc.vector.tensor_tensor(w_gates_lo[:, :, :], w_gates[:, :, :], w_gates_hi[:, :, :].bitcast(F32),
                                ALU.subtract).then_inc(sem("w_gates_split"), 1)

        g = groups["in_a"]
        for i, dst in enumerate((qa, ka, ya)):
            split_turns(g.turn + i * g.turns, g.turns)
            for b in range(NBANK):
                wait_bank(dve, g, g.turn + i * g.turns, g.index + i, b)
                nc.vector.tensor_copy(dst[:, b, :], ps[:, b, 0:T]).then_inc(banks_free, 1)
            split_pair(g.turn + (i + 1) * g.turns, 2)
        dve.wait_ge(sem("gates_done"), 1)
        nc.vector.tensor_copy(gates_row[:, :], ps[0:3 * H, 2, 0:T]).then_inc(sem("gates_row_ready"), 1)
        dve.wait_ge(sem("gates_t_done"), 1)
        nc.vector.tensor_tensor(G[:, 0:2, :], ps[:, 3, 0:48].rearrange("p (t g) -> p t g", t=2),
                                b_gates[:, :].unsqueeze(1).to_broadcast([P, 2, 3 * H]), ALU.add)
        link(nc.vector.tensor_tensor(G[0:SM, 2, :], ps[0:SM, 3, 48:72], b_gates[0:SM, :], ALU.add))
        gf = G[:, :, 0:2 * H]
        nc.vector.scalar_tensor_tensor(lt[:, 0, :, :], gf, -1.0, gf, ALU.mult, ALU.max).then_inc(sem("abs_ready"), 1)
        dve.wait_ge(sem("abs_exp"), 1)
        e, a, z = lt[:, 1, :, :], lt[:, 0, :, :], lt[:, 2, :, :]
        link(nc.vector.tensor_scalar(a, e, 2.0, None, ALU.add))
        link(nc.vector.reciprocal(a, a))
        link(nc.vector.tensor_tensor(e, e, a, ALU.mult))
        link(nc.vector.tensor_tensor(z, e, e, ALU.mult))
        link(nc.vector.tensor_scalar(a, z, 1.0 / 17, None, ALU.mult))
        for c in range(15, 1, -2):
            link(nc.vector.scalar_tensor_tensor(a, a, 1.0 / c, z, ALU.add, ALU.mult))
        link(nc.vector.scalar_tensor_tensor(e, a, 1.0, e, ALU.add, ALU.mult))
        link(nc.vector.tensor_scalar(z, gf, 0.0, None, ALU.min))
        nc.vector.scalar_tensor_tensor(LF[:, :, :], e, -2.0, z, ALU.mult, ALU.add).then_inc(sem("lf_ready"), 1)
        dve.wait_ge(sem("sum_done"), SUM_QK + 2 * H)
        link(rsqrt_mean(2, root[:, :, :], rs[0:H, :, :], xt[0:H, :, :], ps[0:H, 0:2, 0:T], HD))
        parts(root[:, :, :], *root_parts).then_inc(sem("root_ready"), 1)
        for j in range(2 * H):
            x = (qa if j < H else ka)[:, j % H, :]
            gain = gq_scaled[:, :] if j < H else vecs[:, V_GK:V_GK + 1]
            head_norm(j, x, gain)(x).then_inc(sem("qk_normed"), 1)
        dve.wait_ge(sem("c_done"), 1)
        link(nc.vector.tensor_copy(neg_c[:, :], ps[0:H, 1, 0:TP]))
        parts(neg_c[:, :], *neg_c_parts).then_inc(sem("neg_c_ready"), 1)

        def s_mask(h):
            dve.wait_ge(sem("s_done"), h + 1)
            b = h % 2
            if h >= 2:
                dve.wait_ge(sem("pt_done"), h - 1)
            for q, c0, c1 in ((0, 0, P), (1, P, 384)):
                link(nc.vector.tensor_tensor(Sm[:, b, c0:c1], ps[:, b, c0:c1], mask_q[:, c0:c1], ALU.add))
                link(nc.vector.tensor_reduce(mx[:, b, q:q + 1], Sm[:, b, c0:c1], AX.X, ALU.max))
            nc.vector.tensor_scalar(nmx[:, b, :], mx[:, b, :], -1.0, None, ALU.mult).then_inc(sem("s_masked"), 1)

        def p_norm(h):
            b = h % 2
            dve.wait_ge(sem("p_exp"), 2 * (h + 1))
            link(nc.vector.reciprocal(rden[:, b, :], den[:, b, :]))
            nc.vector.tensor_scalar(Sm[:, b, 0:P], Sm[:, b, 0:P], rden[:, b, 0:1], None, ALU.mult)
            nc.vector.tensor_scalar(Sm[:, b, P:384], Sm[:, b, P:384], rden[:, b, 1:2], None,
                                    ALU.mult).then_inc(sem("p_ready"), 1)

        def o_copy(h):
            dve.wait_ge(sem("o_done"), h + 1)
            nc.vector.tensor_copy(ya[:, h, 0:TP], ps[:, 4, 0:TP]).then_inc(sem("ya_ready"), 1)

        def keys_copy(p):
            dve.wait_ge(sem("kpT_done"), 2 * p + 2)
            if p >= 2:
                dve.wait_ge(sem("sT_done"), p - 1)
            nc.vector.tensor_copy(kpT[:, p % 2, 512:1024], ps[:, 7, :]).then_inc(sem("kpT_hi"), 1)

        def queries_apart(b):
            if b >= 2:
                dve.wait_ge(sem("sT_done"), NPG * (b - 1))
            nc.vector.tensor_tensor(
                qz[:, b % 2, :].rearrange("p (h g q) -> p h g q", h=H, g=H),
                qa[:, :, TP + b * TS:TP + (b + 1) * TS].unsqueeze(1).to_broadcast([P, H, H, TS]),
                one_hot[:, :, :].unsqueeze(3).to_broadcast([P, H, H, TS]), ALU.mult).then_inc(sem("qz_ready"), 1)

        dve.wait_ge(sem("qk_normed"), 2 * H)
        queries_apart(0)
        s_mask(0)
        for h in range(H):
            p_norm(h)
            if h + 1 < NB:
                queries_apart(h + 1)
            keys_copy(2 * h)
            if h + 1 < H:
                s_mask(h + 1)
            keys_copy(2 * h + 1)
            if h >= 1:
                o_copy(h - 1)
        o_copy(H - 1)
        nc.vector.tensor_scalar(nl_new[:, :].rearrange("p (b h q) -> p b h q", b=NB, h=H),
                                LF[0:SM, 2, 0:H].unsqueeze(1).unsqueeze(3).to_broadcast([SM, NB, H, TS]), -1.0, None, ALU.mult)
        dve.wait_ge(sem("lf_past_loaded"), 16 * NB * NPG)
        dve.wait_ge(sem("sT_done"), NB * NPG)
        for c in range(NPG):
            last = nc.vector.tensor_scalar(
                nl_past[:, c, :].rearrange("p (b h q) -> p b h q", b=NB, h=H),
                lf_past[:, :, :].rearrange("p (b c) h -> p b c h", c=NPG)[:, :, c, :].unsqueeze(3)
                .to_broadcast([P, NB, H, TS]), -1.0, None, ALU.mult)
        last.then_inc(sem("nl_ready"), 1)
        dve.wait_ge(sem("sT_done"), NB * NPG + 1)
        nc.vector.tensor_copy(STn[:, :], ps[0:SM, 7, 0:256]).then_inc(sem("sT_ready"), 1)
        dve.wait_ge(sem("sample_logits"), 1)
        nc.vector.tensor_reduce(mx[:, 0, :], ps[:, 6, :].rearrange("p (g s) -> p g s", g=2), AX.X, ALU.max)
        link(nc.vector.tensor_reduce(mx[:, 1, :], ps[:, 5, 0:2 * SM].rearrange("p (g s) -> p g s", g=2), AX.X, ALU.max))
        link(nc.vector.tensor_tensor(mx[:, 0, :], mx[:, 0, :], mx[:, 1, :], ALU.max))
        nc.vector.tensor_scalar(nmx[:, 0, :], mx[:, 0, :], -1.0, None, ALU.mult).then_inc(sem("sample_max"), 1)
        dve.wait_ge(sem("sample_exp"), 4)
        link(nc.vector.tensor_tensor(rden[:, 0, :], den[:, 0, :], den[:, 1, :], ALU.add))
        link(nc.vector.reciprocal(rden[:, 0, :], rden[:, 0, :]))
        for g2 in range(2):
            nc.vector.tensor_scalar(Ps[:, g2, :], Ps[:, g2, :], rden[:, 0, g2:g2 + 1], None,
                                    ALU.mult).then_inc(sem("sample_p"), 1)
        dve.wait_ge(sem("sample_pT_ready"), 2)
        for p in range(NB * NPG):
            b, c = p // NPG, p % NPG
            if p >= 4:
                dve.wait_ge(sem("sample_pv"), p - 3)
            nc.vector.tensor_tensor(
                pz[:, p % 4, :].rearrange("p (h b q) -> p h b q", h=H, b=NB),
                PTs[:, c * 256 + b * SM:c * 256 + (b + 1) * SM].rearrange("p (h q) -> p h q", h=H).unsqueeze(2)
                .to_broadcast([P, H, NB, TS]),
                one_hot[:, b, :].unsqueeze(1).unsqueeze(3).to_broadcast([P, H, NB, TS]), ALU.mult).then_inc(sem("pz_ready"), 1)
        dve.wait_ge(sem("sample_pv"), NB * NPG)
        for half in range(2):
            nc.vector.tensor_copy(out_rows[:, half * 512:(half + 1) * 512], ps[0:SM, 2 + half, :]).then_inc(sem("out_rows_ready"), 1)
        dve.wait_ge(sem("sample_oT"), 1)
        nc.vector.tensor_copy(ya[:, :, TP:T], ps[:, 1, 0:256].rearrange("p (h s) -> p h s", h=H)).then_inc(
            sem("ya_ready"), 1)

        dve.wait_ge(out_stored, 6 * 16)
        dve.wait_ge(sem("rows_done"), 2)
        nc.vector.memset(ext[:, :, 0:CW - 1], 0.0).then_inc(sem("ext_edges"), 1)
        nc.vector.tensor_copy(b_row[:, :], ps[0:H, 4, 0:T])
        link(nc.vector.tensor_copy(r_row[:, :], ps[0:H, 3, 0:T]))
        nc.vector.tensor_tensor_scan(R_row[:, 0:TP], r_row[:, 0:TP], r_row[:, 0:TP], 0.0, ALU.max, ALU.max)
        r_s, R_s = (x[:, TP:T].rearrange("h (b t) -> h b t", t=TS) for x in (r_row, R_row))
        dve.wait_ge(sem("state_loaded"), 3 * 16)
        for t in range(TS):
            link(nc.vector.tensor_tensor(R_s[:, :, t], r_s[:, :, t], m0[:, :] if t == 0 else R_s[:, :, t - 1], ALU.max))
        nc.vector.tensor_tensor(m_row[:, :], b_row[:, :], R_row[:, :], ALU.add).then_inc(sem("rows_sum"), 1)
        nc.vector.tensor_scalar(nR_row[:, :], R_row[:, :], -1.0, None, ALU.mult).then_inc(sem("rows_sum"), 1)
        nc.vector.tensor_tensor(ws_row[:, TP:T].rearrange("h (b t) -> h b t", t=TS), r_s,
                                R_s[:, :, TS - 1].unsqueeze(2).to_broadcast([H, NB, TS]),
                                ALU.subtract).then_inc(sem("rows_sum"), 1)
        nc.vector.tensor_tensor(s_rows[:, 0, :].rearrange("h (b t) -> h b t", t=TS),
                                m0[:, :].unsqueeze(2).to_broadcast([H, NB, TS]), R_s,
                                ALU.subtract).then_inc(sem("rows_sum"), 1)
        dve.wait_ge(sem("rows_exp"), 4)
        nc.vector.tensor_copy(s_rows[:, 1, :], nR_row[:, TP:T])
        ins = nc.vector.tensor_copy(s_rows[:, 2, :], em_row[:, TP:T])
        ins.then_inc(sem("s_rows_ready"), 1)
        dve.wait_ge(sem("s_rows_ready"), 1)
        link(parts(nR_row[:, :], *nR_parts))
        parts(em_row[:, :], *em_parts).then_inc(sem("rows_split"), 1)
        dve.wait_ge(sem("edges_done"), 2)
        nc.vector.tensor_copy(n0T[:, :], ps[:, 0, 0:NB * H])
        nc.vector.tensor_copy(
            ext[:, :, EXT:EXTW].rearrange("p j (b r) -> p j b r", r=EXTS)[:, :, :, 0:CW - 1],
            ps[:, 5, 0:384].rearrange("p (j b r) -> p j b r", j=2 * H, b=NB)).then_inc(sem("ext_edges"), 1)

        def conv(j):
            if j >= 2:
                dve.wait_ge(sem("conv_used"), 2 * (j - 1))
            n = EXTW - CW + 1
            for c in range(CW):
                w, src, acc = vecs[:, V_CW + c * 16 + j:V_CW + c * 16 + j + 1], ext[:, j, c:c + n], conv_acc[:, j % 2, 0:n]
                if c == 0:
                    link(nc.vector.tensor_scalar(acc, src, w, None, ALU.mult))
                elif c < CW - 1:
                    link(nc.vector.scalar_tensor_tensor(acc, src, w, acc, ALU.mult, ALU.add))
                else:
                    nc.vector.scalar_tensor_tensor(acc, src, w, acc, ALU.mult, ALU.add).then_inc(sem("conv_done"), 1)

        g = groups["in_m"]
        for i in range(4):
            if i < 2:
                split_turns(g.turn + i * g.turns, g.turns)
            else:
                for t in range(g.turns):
                    conv((i - 2) * H + 2 * t)
                    conv((i - 2) * H + 2 * t + 1)
                    split_pair(g.turn + i * g.turns + (t + 1), 0)
                    if t < g.turns - 1:
                        split_pair(g.turn + i * g.turns + (t + 1), 2)
            for b in range(NBANK):
                wait_bank(dve, g, g.turn + i * g.turns, g.index + i, b)
                if i < 2:
                    j = i * H + b
                    nc.vector.tensor_copy(ext[:, j, CW - 1:EXT], ps[:, b, 0:TP])
                    nc.vector.tensor_copy(
                        ext[:, j, EXT:EXTW].rearrange("p (b r) -> p b r", r=EXTS)[:, :, CW - 1:EXTS],
                        ps[:, b, TP:T].rearrange("p (b t) -> p b t", t=TS)).then_inc(banks_free, 1)
                else:
                    nc.vector.tensor_copy((vm if i == 2 else om)[:, b, :], ps[:, b, 0:T]).then_inc(banks_free, 1)
            split_pair(g.turn + (i + 1) * g.turns, 2)
            if i < 2:
                dve.wait_ge(banks_free, NBANK + (g.index + i + 1) * NBANK)
                x = ext[:, i * H:(i + 1) * H, :]
                nc.vector.tensor_copy(conv_last[:, i * H:(i + 1) * H, 0:3], x[:, :, EXT - 3:EXT]).then_inc(sem("conv_last"), 1)
                nc.vector.tensor_copy(conv_last[:, i * H:(i + 1) * H, 3:27].rearrange("p j (b r) -> p j b r", r=3),
                                      x[:, :, EXT:EXTW].rearrange("p j (b r) -> p j b r", r=EXTS)[:, :, :, TS:EXTS]
                                      ).then_inc(sem("conv_last"), 1)
        nc.vector.memset(vmn[:, 0:2, :, HD:HD + 1], 1.0).then_inc(sem("vmn_ones"), 1)
        for i in range(6):
            t, half, n = i // 2, i % 2, TT[i // 2][1]
            dve.wait_ge(sem("vmT_done"), i + 1)
            nc.vector.tensor_copy(vmn[0:n, t, 4 * half:4 * half + 4, 0:HD],
                                  ps[0:n, i, :].rearrange("p (h d) -> p h d", h=4)).then_inc(sem("vmn_ready"), 1)
        for b in range(4):
            dve.wait_ge(sem("conv_rows_done"), b + 1)
            nc.vector.tensor_copy(conv_rows[:, b * 512:(b + 1) * 512], ps[0:27, 2 + b, :]).then_inc(sem("conv_rows_ready"), 1)
        dve.wait_ge(sem("nat_done"), 1)
        nc.vector.tensor_copy(nat[:, :, :], ps[:, 1, 0:48].rearrange("p (a h) -> p a h", h=H)).then_inc(sem("nat_ready"), 1)
        dve.wait_ge(sem("s_all_ready"), 2)
        link(nc.vector.tensor_tensor(Ws[:, :, :], s_all[0:SM, :, 1, :], mask4_t[:, :].unsqueeze(1).to_broadcast([SM, H, SM]), ALU.add))
        nc.vector.tensor_tensor(Ws[:, :, :], Ws[:, :, :], nat[0:SM, 2, :].unsqueeze(2).to_broadcast([SM, H, SM]),
                                ALU.add).then_inc(sem("ws_logits"), 1)
        link(nc.vector.tensor_tensor(qw[:, :, :], ext[:, 0:H, TP:T], s_all[:, :, 0, :], ALU.mult))
        nc.vector.tensor_tensor(qn[:, :, :].rearrange("p h (b t) -> p h b t", t=TS),
                                qw[:, :, :].rearrange("p h (b t) -> p h b t", t=TS),
                                n0T[:, :].rearrange("p (b h) -> p h b", h=H).unsqueeze(3).to_broadcast([P, H, NB, TS]),
                                ALU.mult).then_inc(sem("qn_ready"), 1)
        dve.wait_ge(sem("ws_exp"), 1)
        dve.wait_ge(sem("ws_scores"), 1)
        nc.vector.tensor_tensor(Ws[:, :, :], Ws[:, :, :], ps[0:SM, 0, 0:256].rearrange("p (h s) -> p h s", h=H),
                                ALU.mult).then_inc(sem("ws_ready"), 1)

        def queries_by_sequence(h):
            if h == 1:
                dve.wait_ge(sem("dn_summed"), 1)
            if h >= 2:
                dve.wait_ge(sem("qC_done"), h - 1)
            nc.vector.tensor_tensor(
                qw_apart[h % 2][:, :, :].rearrange("p b (g t) -> p b g t", g=NB),
                qw[:, h, :].rearrange("p (g t) -> p g t", g=NB).unsqueeze(1).to_broadcast([P, NB, NB, TS]),
                one_hot[:, :, :].unsqueeze(3).to_broadcast([P, NB, NB, TS]), ALU.mult).then_inc(sem("qw_apart"), 1)

        queries_by_sequence(0)
        for h in range(H):
            b = h % 2
            dve.wait_ge(sem("sm_done"), h + 1)
            nc.vector.tensor_tensor(Wt[:, b, :], ps[:, 1, 0:384], mask_t[:, :], ALU.add).then_inc(sem("e_logits"), 1)
            if h + 1 < H:
                queries_by_sequence(h + 1)
            dve.wait_ge(sem("e_exp"), 2 * (h + 1))
            nc.vector.tensor_tensor(Wt[:, b, :], Wt[:, b, :], ps[:, 0, 0:384], ALU.mult).then_inc(sem("w_ready"), 1)
            dve.wait_ge(sem("C_decayed"), h + 1)
            dve.wait_ge(sem("dC_done"), 2 * (h + 1))
            for c in range(2):
                x = C[:, b, 4 * c:4 * c + 4, :]
                nc.vector.tensor_tensor(x, x, ps[:, 3 + c, :].rearrange("p (b e) -> p b e", b=4), ALU.add).then_inc(sem("C_new"), 1)
            dve.wait_ge(sem("qC_rows"), h + 1)
            nc.vector.tensor_copy(n_new[:, 0, h:h + 1], ps[:, 7, HD:HD + 1])
            w_last = s_all[:, h, 0, :].rearrange("p (b t) -> p b t", t=TS)[:, :, TS - 1]
            link(nc.vector.tensor_tensor(n_new[:, 1:1 + NB, h], w_last, n0T[:, h:NB * H:H], ALU.mult))
            nc.vector.tensor_tensor(n_new[:, 1:1 + NB, h], n_new[:, 1:1 + NB, h], ps[:, 7, 256:256 + NB],
                                    ALU.add).then_inc(sem("n_new_ready"), 1)
            dve.wait_ge(sem("num_done"), h + 1)
            dve.wait_ge(sem("em_ready"), h + 1)
            link(nc.vector.scalar_tensor_tensor(dn[:, b, :], ps[:, 2, TP:512], -1.0, em_all[:, b, :], ALU.mult, ALU.max))
            link(nc.vector.tensor_tensor(dn[:, b, :], ps[:, 2, TP:512], dn[:, b, :], ALU.max))
            link(nc.vector.reciprocal(dn[:, b, :], dn[:, b, :]))
            nc.vector.tensor_tensor(vm[:, h, 0:TP], ps[:, 2, 0:TP], dn[:, b, :], ALU.mult).then_inc(sem("h_ready"), 1)
        dve.wait_ge(sem("qC_added"), H)
        dn_s, den_s = dn[:, 0, :].rearrange("p (h s) -> p h s", h=H), ps[:, 5, 256:512].rearrange("p (h s) -> p h s", h=H)
        link(nc.vector.scalar_tensor_tensor(dn_s, den_s, -1.0, s_all[:, :, 2, :], ALU.mult, ALU.max))
        link(nc.vector.tensor_tensor(dn_s, den_s, dn_s, ALU.max))
        link(nc.vector.reciprocal(dn[:, 0, :], dn[:, 0, :]))
        nc.vector.tensor_tensor(vm[:, :, TP:T], ps[:, 5, 0:256].rearrange("p (h s) -> p h s", h=H),
                                dn[:, 0, :].rearrange("p (h s) -> p h s", h=H), ALU.mult).then_inc(sem("h_ready"), 1)
        dve.wait_ge(sem("nT_done"), 1)
        nc.vector.tensor_copy(n_rows[:, 0, :], ps[0:NB * H, 0, 0:HD]).then_inc(sem("n_rows_ready"), 1)
        nc.vector.tensor_copy(n_rows[0:H, 1, :], ps[0:H, 0, HD:2 * HD]).then_inc(sem("n_rows_ready"), 1)
        for kind in ("C_stored", "Cp_stored"):
            for b in range(2):
                dve.wait_ge(sem(f"{kind}{b}"), 16 * (H // 2))
        dve.wait_ge(sem("sum_done"), SUM_Y + 2 * H)
        link(rsqrt_mean(3, root[:, :, :], rs[0:H, :, :], xt[0:H, :, :], ps[0:H, 1:3, 0:T], HD))
        parts(root[:, :, :], *root_parts).then_inc(sem("root_ready"), 1)
        for j in range(KD + 1):
            if j < KD:
                if j >= 2:
                    dve.wait_ge(sem("xn_ready"), 32 + j - 1)
                src = (ya if j < H else vm)[:, j % H, :]
                gain = vecs[:, (V_GA if j < H else V_GM) + j % H:(V_GA if j < H else V_GM) + j % H + 1]
                if j >= H:
                    dve.wait_ge(sem("gated"), j - H + 1)
                ins = head_norm(2 * H + j, src, gain)(xt[:, j % 2, :])
                ins.then_inc(sem("xn_tmp"), 1)
            if j >= 1:
                operand_lo(2, j - 1, y_hi, y_lo)
        g = groups["out"]
        for half in range(2):
            split_turns(g.turn + half * g.turns, g.turns)
            residual(g, half, 1.0)
            split_pair(g.turn + (half + 1) * g.turns, 2)
        norm(3, V_FFN[1], *mem[1]["x"])
        dve.wait_ge(out_stored, 12 * 16)
        swiglu(1)
        for i in range(12):
            if i % 2 == 1:
                dve.wait_ge(sem("y_rows_done"), i + 1)
                t, n = TT[i // 4]
                nc.vector.tensor_copy(y_rows[0:n, t, (i % 4) * 512:(i % 4 + 1) * 512], ps[0:n, i % 4, :]).then_inc(sem("y_rows_ready_v"), 1)

    @block.tensor
    def _(pe):
        mm, tr = nc.tensor.matmul, nc.tensor.transpose

        def turn_products(g, turn0, gi, kt, x_hi, x_lo, first, last, x_ready):
            for pair in range(2):
                slots = [s for s in (2 * pair, 2 * pair + 1) if not (last and 0 < g.real % SLOTS <= s)]
                pe.wait_ge(w_lo_ready, (turn0 + kt) * SLOTS + (2 * pair + 2))
                pe.wait_ge(x_ready[0], kt * SLOTS + (x_ready[1] + slots[-1] + 1))
                for b, c in enumerate(g.tiles):
                    if first and pair == 0:
                        pe.wait_ge(banks_free, gi * NBANK + (b + 1))
                    out = ps[:, b, 0:T]
                    for s in slots:
                        hi, lo, k = w_hi[:, s, c:c + P], w_lo[:, s, c:c + P], kt * SLOTS + s
                        mm(out, hi, x_hi[:, k, :], start=first and pair == 0 and s == slots[0], stop=False)
                        mm(out, hi, x_lo[:, k, :], start=False, stop=False)
                        ins = mm(out, lo, x_hi[:, k, :], start=False, stop=last and pair == 1 and s == slots[-1])
                    if b == len(g.tiles) - 1:
                        ins.then_inc(w_used, 1)
                    elif last and pair == 1:
                        ins.then_inc(bank_done, 1 if b < len(g.tiles) - 2 else NBANK + 1 - len(g.tiles))

        def group_products(g, i, x_hi, x_lo, x_ready):
            turn0, gi = i * g.turns + g.turn, i + g.index
            turn_products(g, turn0, gi, 0, x_hi, x_lo, True, False, x_ready)
            with pe.Fori(1, g.turns - 1) as kt:
                turn_products(g, turn0, gi, kt, x_hi, x_lo, False, False, x_ready)
            turn_products(g, turn0, gi, g.turns - 1, x_hi, x_lo, False, True, x_ready)

        def groups_products(g, count, x_hi, x_lo, x_ready):
            if count == 1:
                group_products(g, 0, x_hi, x_lo, x_ready)
            else:
                with pe.Fori(0, count) as i:
                    group_products(g, i, x_hi, x_lo, x_ready)

        def sums(i, bank, stop_start):
            pe.wait_ge(sem("sq_ready"), i + 1)
            mm(ps[:, bank, 0:T], ones[:, :], sq_ring[i % 4], start=stop_start[0],
               stop=stop_start[1]).then_inc(sem("sum_done"), 1)

        def norm_sums(n):
            for t in range(KD):
                sums(SUM_X[n] + t, 0, (t == 0, t == KD - 1))

        def spread_row(out, h, parts, start=True):
            mm(out, sel[:, h, :], parts[0], start=start, stop=False)
            return mm(out, sel[:, h, :], parts[1], start=False, stop=True)

        def head_sums(i0, bank, heads):
            for j in heads:
                pe.wait_ge(sem("sq_ready"), i0 + j + 1)
                mm(ps[0:H, bank + j // H, 0:T], one_hot[:, j % H, :], sq_ring[(i0 + j) % 4], start=j % H == 0,
                   stop=j % H == H - 1).then_inc(sem("sum_done"), 1)

        def head_spread(bank, used, used0, n):
            pe.wait_ge(sem("root_ready"), n + 1)
            for j in range(2 * H):
                if j >= 2:
                    pe.wait_ge(sem(used), used0 + j - 1)
                spread_row(ps[:, bank + j % 2, 0:T], j % H, [x[:, j // H, :] for x in root_parts]).then_inc(
                    sem("spread_done"), 1)

        def swiglu(n):
            x, hid = mem[n]["x"], mem[n]["hid"]
            xr, hr = (sem("xn_ready"), 48 * n), sem("hid_ready")
            groups_products(groups[f"gu{n}a"], 6, *x, xr)
            groups_products(groups[f"down{n}a"], 2, *hid, (hr, 43 * n))
            groups_products(groups[f"gu{n}b"], 4, *x, xr)
            groups_products(groups[f"gu{n}c"], 1, *x, xr)
            groups_products(groups[f"down{n}b"], 2, *hid, (hr, 43 * n + CHUNK))

        pe.wait_ge(pool_const, 4)
        pe.wait_ge(sem("x_loaded"), 48)
        for t in range(KD):
            if t >= 4:
                pe.wait_ge(sem("xT_copied"), t - 3)
            for r, n in TT:
                ins = tr(ps[:, 1 + t % 4, r * P:r * P + n], x_rows[0:n, r, t * P:(t + 1) * P], ident[0:n, 0:n])
            ins.then_inc(sem("xT_done"), 1)
            if t >= 4:
                sums(t - 4, 0, (t == 4, False))
        for t in range(KD - 4, KD):
            sums(t, 0, (False, t == KD - 1))
        pe.wait_ge(small_loaded, 16 * 16)
        tr(ps[:, 7, 0:P], vec_rows[:, 0, :], ident[:, :]).then_inc(w_used, 2)
        tr(ps[:, 7, P:P + 18], vec_rows[0:18, 1, :], ident[0:18, 0:18]).then_inc(sem("vecT_done"), 1)
        pe.wait_ge(sem("vecs_ready"), 1)
        swiglu(0)
        pe.wait_ge(banks_free, NBANK + (G_A - 1) * NBANK + 1)
        norm_sums(1)
        groups_products(groups["in_a"], 3, xm_hi, xm_lo, (sem("xn_ready"), 16))

        pe.wait_ge(banks_free, NBANK + G_M * NBANK)
        pe.wait_ge(sem("w_gates_split"), 1)
        for k in range(KD):
            gates = ps[0:3 * H, 2, 0:T]
            mm(gates, w_gates_hi[:, k, :], xm_hi[:, k, :], start=k == 0, stop=False)
            mm(gates, w_gates_hi[:, k, :], xm_lo[:, k, :], start=False, stop=False)
            ins = mm(gates, w_gates_lo[:, k, :], xm_hi[:, k, :], start=False, stop=k == KD - 1)
        ins.then_inc(sem("gates_done"), 1)
        head_sums(SUM_QK, 0, range(0, 4))
        pe.wait_ge(sem("gates_row_ready"), 1)
        for t, n in TT:
            ins = tr(ps[0:n, 3, t * 3 * H:(t + 1) * 3 * H], gates_row[:, t * P:t * P + n], ident[0:3 * H, 0:3 * H])
        ins.then_inc(sem("gates_t_done"), 1)
        head_sums(SUM_QK, 0, range(4, 2 * H))

        def natural(src, bank0, made, read=None):
            for i in range(6):
                (t, n), half = TT[i // 2], i % 2
                if read:
                    pe.wait_ge(sem(read), i + 1)
                for j in range(4):
                    ins = tr(ps[0:n, bank0 + i, j * P:(j + 1) * P], src(4 * half + j, t * P, n), ident[:, :])
                ins.then_inc(sem(made), 1)

        pe.wait_ge(sem("abs_ready"), 1)
        natural(lambda h, c, n: ya[:, h, c:c + n], 2, "vT_done")
        head_spread(0, "qk_normed", 0, 0)
        pe.wait_ge(sem("qk_normed"), 2 * H)
        natural(lambda h, c, n: ka[:, h, c:c + n], 2, "kT_done", "vn_ready")
        pe.wait_ge(sem("lf_ready"), 1)
        lf = lambda t, kind, n=P: LF[0:n, t, kind * H:(kind + 1) * H]
        mm(ps[0:H, 1, 0:P], lf(0, 0), neg_upper[:, :], start=True, stop=True)
        mm(ps[0:H, 1, P:TP], lf(0, 0), neg_ones[:, :], start=True, stop=False)
        mm(ps[0:H, 1, P:TP], lf(1, 0), neg_upper[:, :], start=False, stop=True).then_inc(sem("c_done"), 1)
        pe.wait_ge(sem("neg_c_ready"), 1)
        pe.wait_ge(sem("kn_ready"), 6)

        def scores(h):
            if h >= 2:
                pe.wait_ge(sem("s_masked"), h - 1)
            for q, c0, c1 in ((0, 0, P), (1, P, 384)):
                out, n = ps[:, h % 2, c0:c1], c1 - c0
                mm(out, qa[:, h, q * P:(q + 1) * P], ka[:, h, 0:n], start=True, stop=False)
                ins = spread_row(out, h, [x[:, 0:n] for x in neg_c_parts], start=False)
            ins.then_inc(sem("s_done"), 1)

        def probs_t(h):
            pe.wait_ge(sem("p_ready"), h + 1)
            if h >= 2:
                pe.wait_ge(sem("pt_ready"), h - 1)
            for c in range(3):
                ins = tr(ps[:, 2 + h % 2, c * P:(c + 1) * P], Sm[:, h % 2, c * P:(c + 1) * P], ident[:, :])
            ins.then_inc(sem("pt_done"), 1)

        def values(h):
            pe.wait_ge(sem("pt_ready"), h + 1)
            if h >= 1:
                pe.wait_ge(sem("ya_ready"), h)
            mm(ps[:, 4, 0:TP], vn[:, 0, h * HD:(h + 1) * HD], PT[:, h % 2, 0:TP], start=True, stop=True)
            mm(ps[:, 4, P:TP], vn[:, 1, h * HD:(h + 1) * HD], PT[:, h % 2, TP:384], start=False, stop=True,
               skip_group_check=True).then_inc(sem("o_done"), 1)

        def keys_t(p):
            pe.wait_ge(sem(f"page_loaded{p % 3}"), 16 * (p // 3 + 1))
            if p >= 1:
                pe.wait_ge(sem("kpT_lo"), p)
                pe.wait_ge(sem("kpT_hi"), p)
            for half in range(2):
                for i in range(4):
                    c = (4 * half + i) * HD
                    ins = tr(ps[:, 5 + 2 * half, i * P:(i + 1) * P], page[:, p % 3, c:c + HD], ident[:, :])
                ins.then_inc(sem("kpT_done"), 1)

        def page_scores(p):
            b, c = p // NPG, p % NPG
            pe.wait_ge(sem("kpT_lo"), p + 1)
            pe.wait_ge(sem("kpT_hi"), p + 1)
            pe.wait_ge(sem("qz_ready"), b + 1)
            r, col = b % 4 * SM, b // 4 * 256 + c * P
            for h in range(H):
                ins = mm(ps[r:r + SM, 6, col:col + P], qz[:, b % 2, h * SM:(h + 1) * SM],
                         kpT[:, p % 2, h * HD:(h + 1) * HD], start=b < 4 and c == 0 and h == 0,
                         stop=True, skip_group_check=True)
            ins.then_inc(sem("sT_done"), 1)

        scores(0)
        for h in range(H):
            keys_t(2 * h)
            if h + 1 < H:
                scores(h + 1)
            page_scores(2 * h)
            probs_t(h)
            keys_t(2 * h + 1)
            if h >= 1:
                values(h - 1)
            page_scores(2 * h + 1)
        values(H - 1)
        bhq = lambda x: x.rearrange("p (b h q) -> p b h q", b=NB, h=H)
        for h in range(H):
            ins = mm(bhq(ps[0:SM, 7, 0:256])[:, :, h, :], ka[:, h, TP:T], qa[:, h, TP:T], start=True, stop=True)
        ins.then_inc(sem("sT_done"), 1)
        pe.wait_ge(sem("nl_ready"), 1)
        add = dict(start=False, stop=True, skip_group_check=True)
        for g2 in range(2):
            r = slice(g2 * P, (g2 + 1) * P)
            o0, o1 = ps[:, 6, g2 * 256:g2 * 256 + P], ps[:, 6, g2 * 256 + P:(g2 + 1) * 256]
            mm(o0, nl_past[:, 0, r], upper[:, :], **add)
            mm(o1, nl_past[:, 0, r], ones[:, :], **add)
            mm(o1, nl_past[:, 1, r], upper[:, :], **add)
        pe.wait_ge(sem("sT_ready"), 1)
        for g2 in range(2):
            r = slice(g2 * P, (g2 + 1) * P)
            o2 = ps[:, 5, g2 * SM:(g2 + 1) * SM]
            mm(o2, STn[:, r], ident[0:SM, 0:SM], start=True, stop=True)
            mm(o2, nl_past[:, 0, r], ones[:, 0:SM], **add)
            mm(o2, nl_past[:, 1, r], ones[:, 0:SM], **add)
            mm(o2, nl_new[:, r], upper4[:, :], **add)
            ins = mm(o2, spread[:, r], mask4_q[:, :], **add)
        ins.then_inc(sem("sample_logits"), 1)
        for g2 in range(2):
            pe.wait_ge(sem("sample_p"), g2 + 1)
            tr(ps[:, 0, g2 * P:(g2 + 1) * P], Ps[:, g2, 0:P], ident[:, :])
            tr(ps[:, 0, 256 + g2 * P:256 + (g2 + 1) * P], Ps[:, g2, P:2 * P], ident[:, :])
            ins = tr(ps[0:SM, 1, g2 * P:(g2 + 1) * P], Ps[:, g2, 2 * P:T], ident[:, :])
        ins.then_inc(sem("sample_pT"), 1)
        pe.wait_ge(sem("sample_pT_ready"), 2)
        for h in range(H):
            mm(ps[0:SM, 2 + h // 4, h % 4 * HD:(h % 4 + 1) * HD], PTn[:, h * SM:(h + 1) * SM],
               vn[0:SM, 2, h * HD:(h + 1) * HD], start=h % 4 == 0, stop=True, skip_group_check=True)
        for p in range(NB * NPG):
            pe.wait_ge(sem(f"v_loaded{p % VRING}"), 16 * (p // VRING + 1))
            pe.wait_ge(sem("pz_ready"), p + 1)
            for h in range(H):
                ins = mm(ps[0:SM, 2 + h // 4, h % 4 * HD:(h % 4 + 1) * HD], pz[:, p % 4, h * SM:(h + 1) * SM],
                         v_page[p % VRING][:, h * HD:(h + 1) * HD], **add)
            ins.then_inc(sem("sample_pv"), 1)
        for h in range(H):
            pe.wait_ge(sem("out_rows_ready"), 1 + h // 4)
            ins = tr(ps[:, 1, h * SM:(h + 1) * SM], out_rows[:, h * HD:(h + 1) * HD], ident[0:SM, 0:SM])
        ins.then_inc(sem("sample_oT"), 1)

        gi_ = lambda t, n=P: G[0:n, t, 2 * H:3 * H]
        for bank, up, one, up4 in ((3, neg_upper, neg_ones, neg_upper4), (4, upper, ones, upper4)):
            for t in range(2):
                o = ps[0:H, bank, t * P:(t + 1) * P]
                if bank == 3:
                    mm(o, gi_(t), ident[:, :], start=True, stop=False)
                if t == 1:
                    mm(o, lf(0, 1), one[:, :], start=bank == 4, stop=False)
                mm(o, lf(t, 1), up[:, :], start=bank == 4 and t == 0, stop=True)
            o = ps[0:H, bank, TP:T]
            if bank == 3:
                mm(o, gi_(2, SM), ident[0:SM, 0:SM], start=True, stop=False)
            mm(o, lf(2, 1, SM), up4[:, :], start=bank == 4, stop=True).then_inc(sem("rows_done"), 1)
        pe.wait_ge(sem("state_loaded"), 3 * 16)
        tr(ps[:, 0, 0:NB * H], n_rows[:, 0, :], ident[0:NB * H, 0:NB * H]).then_inc(sem("edges_done"), 1)
        for j in range(2 * H):
            ins = tr(ps[:, 5, j * 24:(j + 1) * 24], conv_rows[0:24, j * P:(j + 1) * P], ident[0:24, 0:24])
        ins.then_inc(sem("edges_done"), 1)
        pe.wait_ge(sem("ext_edges"), 2)
        pe.wait_ge(sem("ya_ready"), H + 1)
        groups_products(groups["in_m"], 4, xm_hi, xm_lo, (sem("xn_ready"), 16))

        pe.wait_ge(banks_free, NBANK + G_O * NBANK)
        pe.wait_ge(sem("s_rows_ready"), 1)
        for b in range(2):
            for j in range(4):
                ins = mm(ps[:, 6 + b, j * 96:(j + 1) * 96], sel[:, 4 * b + j, :].bitcast(F32), s_rows[:, :, :], start=True, stop=True)
            ins.then_inc(sem("s_all_done"), 1)
        natural(lambda h, c, n: vm[:, h, c:c + n], 0, "vmT_done")
        pe.wait_ge(sem("km_ready"), H)
        natural(lambda h, c, n: ext[:, H + h, c:c + n], 0, "kmT_done", "vmn_ready")
        pe.wait_ge(sem("kmn_ready"), 6)
        for j in range(2 * H):
            ins = tr(ps[0:27, 2 + j // 4, (j % 4) * P:(j % 4 + 1) * P], conv_last[:, j, :], ident[:, :])
            if j % 4 == 3:
                ins.then_inc(sem("conv_rows_done"), 1)
        pe.wait_ge(sem("rows_exp"), 3)
        for a, row in enumerate((r_row, ws_row)):
            for t, n in TT:
                ins = tr(ps[0:n, 1, (3 * a + t) * H:(3 * a + t + 1) * H], row[:, t * P:t * P + n], ident[0:H, 0:H])
        ins.then_inc(sem("nat_done"), 1)
        for h in range(H):
            ins = mm(ps[0:SM, 0, h * SM:(h + 1) * SM], ext[:, H + h, TP:T], ext[:, h, TP:T], start=True, stop=True)
        ins.then_inc(sem("ws_scores"), 1)
        pe.wait_ge(sem("conv_rows_ready"), 4)
        pe.wait_ge(sem("qn_ready"), 1)
        pe.wait_ge(sem("ws_ready"), 1)
        add = dict(start=False, skip_group_check=True)
        mm(ps[:, 5, 256:512], ones[:, :], qn[:, :, :], start=True, stop=True)
        mm(ps[:, 5, 256:512], ones[0:SM, :], Ws[:, :, :], stop=True, **add).then_inc(sem("dn_summed"), 1)
        for h in range(H):
            mm(ps[:, 5, h * SM:(h + 1) * SM], vmn[0:SM, 2, h, 0:HD], Ws[:, h, :], stop=True, **add)
        pe.wait_ge(sem("nat_ready"), 1)
        pe.wait_ge(sem("s_all_ready"), 2)
        pe.wait_ge(sem("rows_split"), 1)

        def add_qC(h):
            pe.wait_ge(sem("qC_rows"), h + 1)
            mm(ps[:, 5, h * SM:(h + 1) * SM], n_rows[0:SM, h % 2, :], ident[0:SM, 0:SM], stop=True,
               **add).then_inc(sem("qC_added"), 1)

        for h in range(H):
            hd = slice(h * HD, (h + 1) * HD)
            k_, q_ = ext[:, H + h, :], ext[:, h, :]
            if h >= 1:
                pe.wait_ge(sem("w_ready"), h)
            mm(ps[:, 0, 0:TP], k_[:, 0:P], q_[:, 0:TP], start=True, stop=True)
            mm(ps[:, 0, TP:384], k_[:, P:TP], q_[:, P:TP], start=True, stop=True)
            spread_row(ps[:, 1, 0:TP], h, [x[:, 0:TP] for x in nR_parts])
            spread_row(ps[:, 1, TP:384], h, [x[:, P:TP] for x in nR_parts]).then_inc(sem("sm_done"), 1)
            if h >= 1:
                pe.wait_ge(sem("em_ready"), h)
            spread_row(ps[:, 6, 0:TP], h, [x[:, 0:TP] for x in em_parts]).then_inc(sem("em_done"), 1)
            if h >= 1:
                add_qC(h - 1)
            if h == 0:
                pe.wait_ge(sem("kw_ready"), 3)
            pe.wait_ge(sem("v_seq_ready"), h + 1)
            if h == 0:
                pe.wait_ge(sem("vmn_ones"), 1)
            if h >= 1:
                pe.wait_ge(sem("C_new"), 2 * h)
            for c in range(2):
                mm(ps[:, 3 + c, :], kmn[0:SM, 2, hd], v_seq[:, 4 * c:4 * c + 4, :], start=True,
                   stop=True).then_inc(sem("dC_done"), 1)
            pe.wait_ge(sem(f"C_loaded{h % 2}"), 16 * (h // 2 + 1))
            pe.wait_ge(sem("qw_apart"), h + 1)
            if h >= 1:
                pe.wait_ge(sem("Cp_ready"), h)
                pe.wait_ge(sem("n_new_ready"), h)
            for b in range(NB):
                ins = mm(ps[0:SM, 7, TP + NB:TP + NB + HD], qw_apart[h % 2][:, b, :], C[:, h % 2, b, :], start=b == 0, stop=b == NB - 1)
            ins.then_inc(sem("qC_done"), 1)
            mm(ps[:, 7, 0:HD + 1], kmn[:, 0, hd], vmn[:, 0, h, :], start=True, stop=False)
            mm(ps[:, 7, 0:HD + 1], kmn[:, 1, hd], vmn[:, 1, h, :], start=False, stop=True)
            mm(ps[:, 7, 256:256 + NB], kmn[0:SM, 2, hd], block4[:, 0:SM:TS], start=True, stop=True).then_inc(
                sem("Cp_done"), 1)
            pe.wait_ge(sem("w_ready"), h + 1)
            if h >= 1:
                pe.wait_ge(sem("h_ready"), h)
            W = Wt[:, h % 2, :]
            mm(ps[:, 2, 0:TP], vmn[:, 0, h, 0:HD], W[:, 0:TP], start=True, stop=True)
            mm(ps[:, 2, P:TP], vmn[:, 1, h, 0:HD], W[:, TP:384], stop=True, **add)
            mm(ps[:, 2, TP:512], ones[:, :], W[:, 0:TP], stop=True, **add)
            mm(ps[:, 2, TP + P:512], ones[:, :], W[:, TP:384], stop=True, **add).then_inc(sem("num_done"), 1)
        add_qC(H - 1)
        pe.wait_ge(sem("n_new_ready"), H)
        tr(ps[0:NB * H, 0, 0:HD], n_new[:, 1:1 + NB, :].rearrange("p b h -> p (b h)"), ident[:, :])
        tr(ps[0:H, 0, HD:2 * HD], n_new[:, 0, :], ident[:, :]).then_inc(sem("nT_done"), 1)
        head_sums(SUM_Y, 1, range(0, H))
        pe.wait_ge(sem("h_ready"), H + 1)
        head_sums(SUM_Y, 1, range(H, 2 * H))
        head_spread(1, "xn_tmp", 32, 1)
        pe.wait_ge(sem("xn_tmp"), 48)
        pe.wait_ge(sem("n_rows_ready"), 2)
        groups_products(groups["out"], 2, y_hi, y_lo, (sem("xn_ready"), 32))
        pe.wait_ge(banks_free, NBANK + (G_O + 1) * NBANK + 1)
        norm_sums(3)
        swiglu(1)
        pe.wait_ge(banks_free, NBANK + n_groups * NBANK)
        for i in range(12):
            t, n = TT[i // 4]
            if i >= 4:
                pe.wait_ge(sem("y_rows_ready" if i % 2 == 0 else "y_rows_ready_v"), (i - 4) // 2 + 1)
            for j in range(4):
                ins = tr(ps[0:n, i % 4, j * P:(j + 1) * P], X[:, (i % 4) * 4 + j, t * P:t * P + n], ident[:, :])
            ins.then_inc(sem("y_rows_done"), 1)

    ctx.close()


_OUTS = [("y_prompt", (1, TP, D)), ("y_sample", (NB, TS, D)), ("k_prompt", (1, 1, TP, H, HD)),
         ("v_prompt", (1, 1, TP, H, HD)), ("logf_prompt", (1, 1, TP, H)), ("conv_prompt", (1, 1, CW - 1, QK)),
         ("C_prompt", (1, 1, H, HD, HD)), ("n_prompt", (1, 1, H, HD)), ("m_prompt", (1, 1, H)),
         ("k_sample", (1, NB, TS, H, HD)), ("v_sample", (1, NB, TS, H, HD)), ("logf_sample", (1, NB, TS, H)),
         ("conv_sample", (1, NB, CW - 1, QK)), ("C_sample", (1, NB, H, HD, HD)), ("n_sample", (1, NB, H, HD)),
         ("m_sample", (1, NB, H))]


def kernel(**inputs):
    import numpy as _np
    import concourse.bacc as _bacc
    from concourse.bass_utils import run_bass_kernel_spmd as _run

    nc = _bacc.Bacc("TRN2", target_bir_lowering=False, num_devices=1)
    arrays, A, O = {}, {}, {}
    for name, value in inputs.items():
        a = _np.ascontiguousarray(value)
        arrays[f"in_{name}"] = a
        A[name] = nc.dram_tensor(f"in_{name}", a.shape, mybir.dt.from_np(a.dtype), kind="ExternalInput").ap()
    for name, shape in _OUTS:
        O[name] = nc.dram_tensor(f"out_{name}", shape, F32, kind="ExternalOutput").ap()
    build(nc, A, O)
    r = _run(nc, [arrays], core_ids=[0])
    return tuple(r.results[0][f"out_{name}"] for name, _ in _OUTS)
```
